# Optimizing a Trainium2 kernel written in Bass

```python
import jax, jax.numpy as jnp
from jax import lax
import numpy as np
import jax
import jax.numpy as jnp

D_MODEL = 1024
BATCH = 1
SEQ = 1024
DEPTH = 1

GRID_W = 64
N_HEADS = 16
HEAD_DIM = D_MODEL // N_HEADS
ATTN_WIDTH = N_HEADS * HEAD_DIM
WIN_ROWS = 8
WIN_COLS = 16
Q_COLS = 16
K_COLS = 32
N_CBLK = GRID_W // Q_COLS
LRU_WIDTH = D_MODEL
LRU_BLOCKS = 16
LRU_BLOCK = LRU_WIDTH // LRU_BLOCKS
LRU_C = 8.0
CONV_W = 4
CONV_LEFT = 2
D_FF = 2816
FFN_RES = 0.5
EPS = 1e-6
IN_WIDTH = 2 * LRU_WIDTH + 3 * ATTN_WIDTH + 2 * D_MODEL


def _rmsnorm(x, g):
    xf = x.astype(jnp.float32)
    y = xf * lax.rsqrt(jnp.mean(xf * xf, axis=-1, keepdims=True) + EPS)
    return (y * g.astype(jnp.float32)).astype(x.dtype)

def _swiglu(h, w_gu, w_down):
    g, u = jnp.split(h @ w_gu, 2, axis=-1)
    return (jax.nn.silu(g) * u) @ w_down

def _centred_dwconv(x, w, b):
    S = x.shape[1]
    xp = jnp.pad(x, ((0, 0), (CONV_LEFT, CONV_W - 1 - CONV_LEFT), (0, 0)))
    y = b
    for k in range(CONV_W):
        y = y + xp[:, k:k + S] * w[k]
    return y

def _lin_combine(left, right):
    a1, b1 = left
    a2, b2 = right
    return a1 * a2, a2 * b1 + b2

def _rglru_scan(xc, w_gates, b_gates, lam):
    B_, S, W = xc.shape
    xb = xc.reshape(B_, S, LRU_BLOCKS, LRU_BLOCK)
    gates = jnp.einsum('bsni,gnio->gbsno', xb, w_gates.astype(jnp.float32)).reshape(2, B_, S, W)
    gates = gates + b_gates.astype(jnp.float32)[:, None, None, :]
    r = jax.nn.sigmoid(gates[0])
    i = jax.nn.sigmoid(gates[1])
    log_a = -LRU_C * r * jax.nn.softplus(-lam.astype(jnp.float32))
    a = jnp.exp(log_a)
    bx = jnp.sqrt(-jnp.expm1(2.0 * log_a)) * (i * xc)
    _, h = lax.associative_scan(_lin_combine, (a, bx), axis=1)
    return h

def _col_tables():
    qc = np.arange(GRID_W).reshape(N_CBLK, Q_COLS)
    kstart = np.clip(np.arange(N_CBLK) * Q_COLS - WIN_COLS // 2, 0, GRID_W - K_COLS)
    kc = kstart[:, None] + np.arange(K_COLS)[None, :]
    cs = np.clip(qc - WIN_COLS // 2, 0, GRID_W - WIN_COLS)
    valid = (kc[:, None, :] >= cs[:, :, None]) & (kc[:, None, :] < cs[:, :, None] + WIN_COLS)
    dc = np.clip(kc[:, None, :] - qc[:, :, None], -(WIN_COLS - 1), WIN_COLS - 1) + WIN_COLS - 1
    return kc, valid, dc

def _neighbourhood_attention(q, k, v, rpb):
    B_, S, H, Dh = q.shape
    rows = S // GRID_W
    kr = min(WIN_ROWS, rows)
    kc, valid, dc = _col_tables()
    kg = k.reshape(B_, rows, GRID_W, H, Dh)[:, :, kc]
    vg = v.reshape(B_, rows, GRID_W, H, Dh)[:, :, kc]
    qg = jnp.moveaxis(q.reshape(B_, rows, N_CBLK, Q_COLS, H, Dh), 1, 0)
    rpb32 = rpb.astype(jnp.float32)
    mask = valid[None, None, :, :, None, :]

    def row_block(args):
        r, q_r = args
        rs = jnp.clip(r - kr // 2, 0, rows - kr)
        k_r = lax.dynamic_slice_in_dim(kg, rs, kr, axis=1)
        v_r = lax.dynamic_slice_in_dim(vg, rs, kr, axis=1)
        s = jnp.einsum('bnqhd,brnkhd->bhnqrk', q_r, k_r, preferred_element_type=jnp.float32)
        dr = rs + jnp.arange(kr) - r + WIN_ROWS - 1
        bias = rpb32[:, dr][:, :, dc]
        s = s + jnp.transpose(bias, (0, 2, 3, 1, 4))[None]
        s = jnp.where(mask, s, -jnp.inf)
        shp = s.shape
        p = jax.nn.softmax(s.reshape(shp[:4] + (kr * K_COLS,)), axis=-1).reshape(shp)
        return jnp.einsum('bhnqrk,brnkhd->bnqhd', p.astype(v.dtype), v_r)

    o = lax.map(row_block, (jnp.arange(rows), qg))
    return jnp.moveaxis(o, 0, 1).reshape(B_, S, H * Dh)

def first_inputs(seed: int = 0) -> dict:
    key = jax.random.key(seed)
    ks = jax.random.split(key, 20)
    f32 = jnp.float32
    nrm = lambda k, shape, s: jax.random.normal(k, shape, f32) * s
    u = jax.random.uniform(ks[10], (DEPTH, 2, LRU_WIDTH), f32, minval=0.9, maxval=0.999)
    sg = u ** (1.0 / LRU_C)
    lru_lambda = jnp.log(sg) - jnp.log1p(-sg)
    return {
        'x': jax.random.normal(ks[0], (BATCH, SEQ, D_MODEL), f32),
        'norm_ffn1': 1.0 + nrm(ks[1], (DEPTH, D_MODEL), 0.02),
        'w_ffn1_gu': nrm(ks[2], (DEPTH, D_MODEL, 2 * D_FF), D_MODEL ** -0.5),
        'w_ffn1_down': nrm(ks[3], (DEPTH, D_FF, D_MODEL), D_FF ** -0.5),
        'norm_mix': 1.0 + nrm(ks[4], (DEPTH, D_MODEL), 0.02),
        'w_in': nrm(ks[5], (DEPTH, D_MODEL, IN_WIDTH), D_MODEL ** -0.5),
        'conv_w': nrm(ks[6], (DEPTH, CONV_W, LRU_WIDTH), CONV_W ** -0.5),
        'conv_b': nrm(ks[7], (DEPTH, LRU_WIDTH), 0.01),
        'lru_w_gates': nrm(ks[8], (DEPTH, 2, 2, LRU_BLOCKS, LRU_BLOCK, LRU_BLOCK), LRU_BLOCK ** -0.5),
        'lru_b_gates': nrm(ks[9], (DEPTH, 2, 2, LRU_WIDTH), 0.1),
        'lru_lambda': lru_lambda,
        'q_norm': 1.0 + nrm(ks[11], (DEPTH, HEAD_DIM), 0.02),
        'k_norm': 1.0 + nrm(ks[12], (DEPTH, HEAD_DIM), 0.02),
        'rel_pos_bias': nrm(ks[13], (DEPTH, N_HEADS, 2 * WIN_ROWS - 1, 2 * WIN_COLS - 1), 0.1),
        'w_out': nrm(ks[14], (DEPTH, D_MODEL, D_MODEL), D_MODEL ** -0.5),
        'norm_ffn2': 1.0 + nrm(ks[15], (DEPTH, D_MODEL), 0.02),
        'w_ffn2_gu': nrm(ks[16], (DEPTH, D_MODEL, 2 * D_FF), D_MODEL ** -0.5),
        'w_ffn2_down': nrm(ks[17], (DEPTH, D_FF, D_MODEL), D_FF ** -0.5),
    }

def first_block(x, norm_ffn1, w_ffn1_gu, w_ffn1_down, norm_mix, w_in, conv_w, conv_b,
              lru_w_gates, lru_b_gates, lru_lambda, q_norm, k_norm, rel_pos_bias, w_out,
              norm_ffn2, w_ffn2_gu, w_ffn2_down):
    B_, S, _ = x.shape
    splits = list(np.cumsum([LRU_WIDTH, LRU_WIDTH, ATTN_WIDTH, ATTN_WIDTH, ATTN_WIDTH, D_MODEL]))
    for l in range(DEPTH):
        x = x + FFN_RES * _swiglu(_rmsnorm(x, norm_ffn1[l]), w_ffn1_gu[l], w_ffn1_down[l])

        h = _rmsnorm(x, norm_mix[l])
        xr, gr, q, k, v, ga, gb = jnp.split(h @ w_in[l], splits, axis=-1)

        xc = _centred_dwconv(xr, conv_w[l], conv_b[l]).astype(jnp.float32)
        h_fwd = _rglru_scan(xc, lru_w_gates[l, 0], lru_b_gates[l, 0], lru_lambda[l, 0])
        h_bwd = jnp.flip(_rglru_scan(jnp.flip(xc, 1), lru_w_gates[l, 1], lru_b_gates[l, 1],
                                     lru_lambda[l, 1]), 1)
        y_lru = ((h_fwd + h_bwd) * jax.nn.gelu(gr.astype(jnp.float32))).astype(x.dtype)

        q = _rmsnorm(q.reshape(B_, S, N_HEADS, HEAD_DIM), q_norm[l]) * (HEAD_DIM ** -0.5)
        k = _rmsnorm(k.reshape(B_, S, N_HEADS, HEAD_DIM), k_norm[l])
        v = v.reshape(B_, S, N_HEADS, HEAD_DIM)
        y_att = _neighbourhood_attention(q, k, v, rel_pos_bias[l]).astype(x.dtype)

        y = jax.nn.sigmoid(ga) * y_lru + jax.nn.sigmoid(gb) * y_att
        x = x + y @ w_out[l]

        x = x + FFN_RES * _swiglu(_rmsnorm(x, norm_ffn2[l]), w_ffn2_gu[l], w_ffn2_down[l])
    return x


CTX_LEN = 256
MIX_W = D_MODEL
A_W = MIX_W // 2
A_GROUPS = 4
A_GROUP_DIM = A_W // A_GROUPS
A_CHUNK = 128
ROWS_PER_CHUNK = A_CHUNK // GRID_W
B_W = MIX_W - A_W
B_HEADS = 4
B_HEAD_DIM = B_W // B_HEADS
CONV_K = 3
GDN_CHUNK = 64
N_EXPERTS = 16
EC_CAPACITY = 2
EXPERT_FF = 1024
N_MOD = 6
NORM_EPS = 1e-6
COL_QKV = 3 * B_W
N_STATE_COLS = COL_QKV + 4 * B_HEADS
COL_Z_END = N_STATE_COLS + B_W
IN_COLS = COL_Z_END + 2 * A_W


def rms_norm(x, g):
    xf = x.astype(jnp.float32)
    y = xf * lax.rsqrt(jnp.mean(xf * xf, axis=-1, keepdims=True) + NORM_EPS)
    return (y * g.astype(jnp.float32)).astype(x.dtype)

def l2_normalize(x):
    return x * lax.rsqrt(jnp.sum(x * x, axis=-1, keepdims=True) + NORM_EPS)

def short_conv(x, w):
    pad = (CONV_K - 1) // 2
    y = lax.conv_general_dilated(
        x, w[:, None, :].astype(x.dtype), window_strides=(1,), padding=[(pad, pad)],
        dimension_numbers=("NWC", "WIO", "NWC"), feature_group_count=x.shape[-1])
    return jax.nn.silu(y)

def chunk_mlp(uv, n_chunks, norm_g, ws, bs):
    B, T, _ = uv.shape
    u, v = jnp.split(jax.nn.gelu(uv, approximate=False), 2, axis=-1)
    v = rms_norm(v.reshape(B, T, A_GROUPS, A_GROUP_DIM), norm_g.reshape(A_GROUPS, A_GROUP_DIM))
    vc = v.reshape(B, n_chunks, A_CHUNK, A_GROUPS, A_GROUP_DIM)
    s = jnp.einsum("gts,bnsgd->bntgd", ws, vc) + jnp.swapaxes(bs, 0, 1)[None, None, :, :, None]
    return u * s.reshape(B, T, A_W)

def gdn_streams(p, conv_w, a_log, dt_bias):
    B, T, _ = p.shape
    qkv = short_conv(p[..., :COL_QKV], conv_w).astype(jnp.float32)
    qkv = qkv.reshape(B, T, 3, B_HEADS, B_HEAD_DIM)
    q = l2_normalize(qkv[:, :, 0]) * (B_HEAD_DIM ** -0.5)
    k = l2_normalize(qkv[:, :, 1])
    v = qkv[:, :, 2]
    ab = p[..., COL_QKV:N_STATE_COLS].astype(jnp.float32).reshape(B, T, 2, 2, B_HEADS)
    g = -jnp.exp(a_log.astype(jnp.float32)) * jax.nn.softplus(ab[:, :, 0] + dt_bias.astype(jnp.float32))
    beta = jax.nn.sigmoid(ab[:, :, 1])
    return q, k, v, g, beta

def gdn_chunked(q, k, v, g, beta, s0):
    B, T, H, Dk = q.shape
    C = GDN_CHUNK
    N = T // C

    def chunks(t):
        t = t.reshape(B, N, C, H, *t.shape[3:])
        return jnp.moveaxis(t, (1, 3), (0, 2))

    qc, kc, vc = chunks(q), chunks(k), chunks(v)
    gcum = jnp.cumsum(chunks(g), axis=-1)
    bc = chunks(beta)
    tri = jnp.tril(jnp.ones((C, C), dtype=bool))
    strict = jnp.tril(jnp.ones((C, C), dtype=bool), -1)
    diff = gcum[..., :, None] - gcum[..., None, :]
    decay = jnp.where(tri, jnp.exp(jnp.where(tri, diff, 0.0)), 0.0)
    kb = kc * bc[..., None]
    a_mat = jnp.where(strict, jnp.einsum("nbhid,nbhjd->nbhij", kb, kc) * decay, 0.0)
    eye = jnp.eye(C, dtype=jnp.float32)
    t_inv = lax.linalg.triangular_solve(eye + a_mat, jnp.broadcast_to(eye, a_mat.shape),
                                        left_side=True, lower=True, unit_diagonal=True)
    u = t_inv @ (vc * bc[..., None])
    w = t_inv @ (kb * jnp.exp(gcum)[..., None])
    attn = jnp.einsum("nbhid,nbhjd->nbhij", qc, kc) * decay
    q_g = qc * jnp.exp(gcum)[..., None]
    g_last = gcum[..., -1]
    k_g = kc * jnp.exp(g_last[..., None] - gcum)[..., None]

    def step(state, xs):
        q_i, k_i, u_i, w_i, a_i, gl_i = xs
        v_new = u_i - w_i @ state
        o_i = q_i @ state + a_i @ v_new
        state = state * jnp.exp(gl_i)[..., None, None] + jnp.swapaxes(k_i, -1, -2) @ v_new
        return state, o_i

    s_final, o = lax.scan(step, s0, (q_g, k_g, u, w, attn, g_last))
    o = jnp.moveaxis(o, (0, 2), (1, 3)).reshape(B, T, H, v.shape[-1])
    return o, s_final

def gdn_two_dirs(q, k, v, g, beta, s0_f, s0_b):
    o_f, s_f = gdn_chunked(q, k, v, g[:, :, 0], beta[:, :, 0], s0_f)
    flip = lambda t: jnp.flip(t, axis=1)
    o_b, s_b = gdn_chunked(flip(q), flip(k), flip(v), flip(g[:, :, 1]), flip(beta[:, :, 1]), s0_b)
    return o_f + flip(o_b), s_f, s_b

def gdn_out(o, z, norm_g):
    B, T = o.shape[:2]
    zh = z.reshape(B, T, B_HEADS, B_HEAD_DIM).astype(jnp.float32)
    y = o * lax.rsqrt(jnp.mean(o * o, axis=-1, keepdims=True) + NORM_EPS)
    y = y * norm_g.astype(jnp.float32) * jax.nn.silu(zh)
    return y.reshape(B, T, B_W)

def mix_out(p, o, n_chunks, gdn_norm_g, gm_norm_g, gm_ws, gm_bs, w_out):
    y_a = chunk_mlp(p[..., COL_Z_END:], n_chunks, gm_norm_g, gm_ws, gm_bs)
    y_b = gdn_out(o, p[..., N_STATE_COLS:COL_Z_END], gdn_norm_g).astype(p.dtype)
    return jnp.concatenate([y_a, y_b], axis=-1) @ w_out

def expert_choice_ffn(h, w_router, b_router, w_gate, w_up, w_down):
    B, N, D = h.shape
    cap = EC_CAPACITY * N // N_EXPERTS
    aff = jax.nn.softmax((h @ w_router + b_router).astype(jnp.float32), axis=-1)
    gate, idx = lax.top_k(jnp.swapaxes(aff, 1, 2), cap)
    xe = jax.vmap(lambda hb, ib: hb[ib])(h, idx)
    hid = jax.nn.silu(jnp.einsum("becd,edf->becf", xe, w_gate)) * jnp.einsum("becd,edf->becf", xe, w_up)
    ye = jnp.einsum("becf,efd->becd", hid, w_down) * gate[..., None].astype(h.dtype)
    return jax.vmap(lambda ib, yb: jnp.zeros((N, D), yb.dtype).at[ib.reshape(-1)].add(yb.reshape(-1, D)))(idx, ye)

def second_inputs(seed: int = 0) -> dict:
    key = jax.random.key(seed)
    ks = jax.random.split(key, 24)
    f32 = jnp.float32
    nrm = lambda k, shape, s: jax.random.normal(k, shape, f32) * s
    dt = jnp.exp(jax.random.uniform(ks[10], (DEPTH, 2, B_HEADS), f32, np.log(1e-3), np.log(1e-1)))
    return {
        "x": nrm(ks[0], (BATCH, SEQ, D_MODEL), 1.0),
        "c": nrm(ks[1], (BATCH, D_MODEL), 1.0),
        "ctx": nrm(ks[2], (BATCH, CTX_LEN, D_MODEL), 1.0),
        "c_ctx": nrm(ks[3], (D_MODEL,), 1.0),
        "w_mod": nrm(ks[4], (DEPTH, D_MODEL, N_MOD * D_MODEL), 0.5 * D_MODEL ** -0.5),
        "b_mod": nrm(ks[5], (DEPTH, N_MOD * D_MODEL), 0.02),
        "norm1_g": 1.0 + nrm(ks[6], (DEPTH, D_MODEL), 0.05),
        "norm2_g": 1.0 + nrm(ks[7], (DEPTH, D_MODEL), 0.05),
        "w_in": nrm(ks[8], (DEPTH, D_MODEL, IN_COLS), D_MODEL ** -0.5),
        "conv_w": nrm(ks[9], (DEPTH, CONV_K, COL_QKV), CONV_K ** -0.5),
        "a_log": jnp.log(jax.random.uniform(ks[11], (DEPTH, 2, B_HEADS), f32, 1.0, 16.0)),
        "dt_bias": dt + jnp.log(-jnp.expm1(-dt)),
        "gdn_norm_g": 1.0 + nrm(ks[12], (DEPTH, B_HEAD_DIM), 0.05),
        "gm_norm_g": 1.0 + nrm(ks[13], (DEPTH, A_W), 0.05),
        "gm_ws": nrm(ks[14], (DEPTH, A_GROUPS, A_CHUNK, A_CHUNK), A_CHUNK ** -0.5),
        "gm_bs": 1.0 + nrm(ks[15], (DEPTH, A_GROUPS, A_CHUNK), 0.1),
        "w_out": nrm(ks[16], (DEPTH, MIX_W, D_MODEL), MIX_W ** -0.5),
        "w_router": nrm(ks[17], (DEPTH, D_MODEL, N_EXPERTS), D_MODEL ** -0.5),
        "b_router": nrm(ks[18], (DEPTH, N_EXPERTS), 0.01),
        "w_gate": nrm(ks[19], (DEPTH, N_EXPERTS, D_MODEL, EXPERT_FF), D_MODEL ** -0.5),
        "w_up": nrm(ks[20], (DEPTH, N_EXPERTS, D_MODEL, EXPERT_FF), D_MODEL ** -0.5),
        "w_down": nrm(ks[21], (DEPTH, N_EXPERTS, EXPERT_FF, D_MODEL), EXPERT_FF ** -0.5),
        "final_norm_g": 1.0 + nrm(ks[22], (D_MODEL,), 0.05),
    }

def second_block(x, c, ctx, c_ctx, w_mod, b_mod, norm1_g, norm2_g, w_in, conv_w, a_log, dt_bias,
              gdn_norm_g, gm_norm_g, gm_ws, gm_bs, w_out, w_router, b_router, w_gate, w_up, w_down,
              final_norm_g):
    B, T, _ = x.shape
    rows = T // GRID_W
    n_lat_chunks = rows // ROWS_PER_CHUNK
    n_ctx_chunks = ctx.shape[1] // A_CHUNK
    h_lat, h_ctx = x, ctx
    for layer in range(DEPTH):
        last = layer == DEPTH - 1
        mod = jax.nn.silu(c) @ w_mod[layer] + b_mod[layer]
        mod_c = jax.nn.silu(c_ctx) @ w_mod[layer] + b_mod[layer]
        sh1, sc1, gt1, sh2, sc2, gt2 = jnp.split(mod[:, None, :], N_MOD, axis=-1)
        csh1, csc1, cgt1, csh2, csc2, cgt2 = jnp.split(mod_c, N_MOD, axis=-1)
        wl = w_in[layer]

        c_in = rms_norm(h_ctx, norm1_g[layer]) * (1.0 + csc1) + csh1
        p_ctx = c_in @ (wl[:, :N_STATE_COLS] if last else wl)
        qc, kc, vc, gc, bc = gdn_streams(p_ctx[..., :N_STATE_COLS], conv_w[layer], a_log[layer], dt_bias[layer])
        zero_state = jnp.zeros((B, B_HEADS, B_HEAD_DIM, B_HEAD_DIM), jnp.float32)
        o_ctx, s_f, s_b = gdn_two_dirs(qc, kc, vc, gc, bc, zero_state, zero_state)

        a_in = rms_norm(h_lat, norm1_g[layer]) * (1.0 + sc1) + sh1
        p_lat = a_in @ wl
        ql, kl, vl, gl, bl = gdn_streams(p_lat[..., :N_STATE_COLS], conv_w[layer], a_log[layer], dt_bias[layer])
        o_lat, _, _ = gdn_two_dirs(ql, kl, vl, gl, bl, s_f, s_b)
        h_lat = h_lat + gt1 * mix_out(p_lat, o_lat, n_lat_chunks, gdn_norm_g[layer], gm_norm_g[layer],
                                      gm_ws[layer], gm_bs[layer], w_out[layer])
        f_in = rms_norm(h_lat, norm2_g[layer]) * (1.0 + sc2) + sh2
        h_lat = h_lat + gt2 * expert_choice_ffn(f_in, w_router[layer], b_router[layer],
                                                w_gate[layer], w_up[layer], w_down[layer])

        if not last:
            h_ctx = h_ctx + cgt1 * mix_out(p_ctx, o_ctx, n_ctx_chunks, gdn_norm_g[layer], gm_norm_g[layer],
                                           gm_ws[layer], gm_bs[layer], w_out[layer])
            cf_in = rms_norm(h_ctx, norm2_g[layer]) * (1.0 + csc2) + csh2
            h_ctx = h_ctx + cgt2 * expert_choice_ffn(cf_in, w_router[layer], b_router[layer],
                                                     w_gate[layer], w_up[layer], w_down[layer])
    return rms_norm(h_lat, final_norm_g)


def setup_inputs(seed=0):
    out = dict(first_inputs(seed))
    for name, value in second_inputs(seed + 1).items():
        if name != "x":
            out[name + "_2"] = value
    return out


def reference(
    x, norm_ffn1, w_ffn1_gu, w_ffn1_down, norm_mix, w_in, conv_w, conv_b, lru_w_gates,
    lru_b_gates, lru_lambda, q_norm, k_norm, rel_pos_bias, w_out, norm_ffn2, w_ffn2_gu,
    w_ffn2_down, c_2, ctx_2, c_ctx_2, w_mod_2, b_mod_2, norm1_g_2, norm2_g_2, w_in_2, conv_w_2,
    a_log_2, dt_bias_2, gdn_norm_g_2, gm_norm_g_2, gm_ws_2, gm_bs_2, w_out_2, w_router_2,
    b_router_2, w_gate_2, w_up_2, w_down_2, final_norm_g_2,
):
    x = first_block(
        x, norm_ffn1, w_ffn1_gu, w_ffn1_down, norm_mix, w_in, conv_w, conv_b, lru_w_gates,
        lru_b_gates, lru_lambda, q_norm, k_norm, rel_pos_bias, w_out, norm_ffn2, w_ffn2_gu,
        w_ffn2_down,
    )
    return second_block(
        x, c_2, ctx_2, c_ctx_2, w_mod_2, b_mod_2, norm1_g_2, norm2_g_2, w_in_2, conv_w_2,
        a_log_2, dt_bias_2, gdn_norm_g_2, gm_norm_g_2, gm_ws_2, gm_bs_2, w_out_2, w_router_2,
        b_router_2, w_gate_2, w_up_2, w_down_2, final_norm_g_2,
    )


_drawn_inputs = setup_inputs


def setup_inputs(seed=0):
    import zlib

    import numpy as np

    out = dict(_drawn_inputs(seed))
    spreads = {}
    factors = {'norm_ffn1': 5.433,
     'norm_mix': 5.709,
     'lru_b_gates': 4.126,
     'q_norm': 8.0,
     'k_norm': 8.0,
     'rel_pos_bias': 19.445,
     'norm_ffn2': 18.735,
     'ctx_2': 200.0,
     'c_ctx_2': 200.0,
     'b_mod_2': 3.029,
     'norm1_g_2': 10.647,
     'norm2_g_2': 43.272,
     'gdn_norm_g_2': 45.74,
     'gm_norm_g_2': 41.231,
     'gm_bs_2': 23.306,
     'b_router_2': 200.0,
     'conv_b': 3.803,
     'a_log_2': 3.188}
    for name, (base, spread) in spreads.items():
        noise = np.random.default_rng([zlib.crc32(name.encode()), seed]).standard_normal(out[name].shape)
        drawn = base * np.exp(spread * noise) if base else spread * noise
        out[name] = jnp.asarray(drawn.astype(out[name].dtype))
    for name, factor in factors.items():
        out[name] = (out[name] * factor).astype(out[name].dtype)
    return out
```

```python
from contextlib import ExitStack, contextmanager

import numpy as np
import concourse.bass as bass
from concourse import mybir

P = 128
F32 = mybir.dt.float32
ALU = mybir.AluOpType
ACT = mybir.ActivationFunctionType
AX = mybir.AxisListType

HEAD = 4096


class Done:

    def __init__(self, counter, loop, at):
        self.counter, self.loop, self.at = counter, loop, at


class Loop:
    def __init__(self, name, passes, index):
        self.name, self.passes, self.index = name, passes, index


class Counter:

    def __init__(self, program, name, eng=None, by=1, head=HEAD):
        self.program, self.name, self.eng, self.by = program, name, eng, by
        self.sem = program.ctx.enter_context(program.nc.semaphore(name))
        self.base, self.here = head, 0
        self.head = head
        self.ended = {}
        if eng:
            self.waited = self.program.ctx.enter_context(program.nc.semaphore(name + "_waited"))
        program.counters.append(self)
        if head:
            program.nc.sync.sem_inc(self.sem, head)
        if program.loop:
            raise ValueError("a counter is made outside the loops")

    def did(self, instruction):
        instruction.then_inc(self.sem, self.by)
        self.here += self.by
        return self.last()

    def last(self):
        loop = self.program.loop
        return Done(self, loop, self.here if loop else self.base + self.here)

    def value(self, done, back):
        loop = self.program.loop
        if done.loop is None:
            return done.at
        if done.loop is loop:
            per = self.program.per_pass(loop.name, self.name)
            return loop.index * per + (self.base + done.at - back * per)
        base, per, passes = self.ended[done.loop.name]
        return base + per * (passes - 1) + done.at

    def wait(self, *dones, back=0):
        for done in dones:
            self.eng.wait_ge(done.counter.sem, done.counter.value(done, back))
            if done.loop and done.loop is self.program.loop:
                self.eng.sem_inc(self.waited, 1)


class Guard:

    def __init__(self, program, name):
        self.program, self.name = program, name
        self.marks = []

    def mark(self, *dones):
        self.marks = list(dones)
        if self.program.loop:
            self.program.carried[(self.program.loop.name, self.name)] = [
                (d.counter.name, d.at) for d in dones]

    def wait(self, engine):
        loop = self.program.loop
        engine.wait(*self.marks)
        if loop and not any(d.loop is loop for d in self.marks):
            for name, at in self.program.plan_carried.get((loop.name, self.name), []):
                counter = self.program.named(name)
                engine.wait(Done(counter, loop, at), back=1)


class Program:
    def __init__(self, nc, ctx, plan):
        self.nc, self.ctx = nc, ctx
        self.counters = []
        self.loop = None
        self.plan_counts, self.plan_carried = plan
        self.counts, self.carried = {}, {}
        self.pe = Counter(self, "pe_done", nc.tensor)
        self.act = Counter(self, "act_done", nc.scalar)
        self.dve = Counter(self, "dve_done", nc.vector)
        self.pool = Counter(self, "pool_done", nc.gpsimd)
        self.sp = Counter(self, "sp_done", nc.sync)
        self.compute = [self.pe, self.act, self.dve, self.pool]

    def named(self, name):
        return next(c for c in self.counters if c.name == name)

    def per_pass(self, loop, counter):
        return self.plan_counts.get((loop, counter), 1)

    @contextmanager
    def repeat(self, name, passes):
        for c in self.counters:
            c.base, c.here = c.base + c.here, 0
        with self.nc.Fori(0, passes) as index:
            self.loop = Loop(name, passes, index)
            yield index
            self.loop = None
        for c in self.counters:
            self.counts[(name, c.name)] = c.here
            c.ended[name] = (c.base, c.here, passes)
            c.base, c.here = c.base + c.here * passes, 0

    def barrier(self, *engines):
        for e in engines or self.compute:
            for c in self.counters:
                if c.base + c.here > c.head:
                    e.wait(c.last())


class Buffer:

    def __init__(self, program, name, mem, loads=False, head=HEAD):
        self.mem = mem
        self.guard = Guard(program, name)
        self.loads = Counter(program, name + "_in", by=16, head=head) if loads else None

    def load(self, engine, dst, src):
        self.guard.wait(engine)
        return self.loads.did(engine.eng.dma_start(dst, src))

    def more(self, engine, dst, src):
        return self.loads.did(engine.eng.dma_start(dst, src))


class Shared:
    pass


def build(nc, plan, t, out):
    with ExitStack() as ctx:
        p = Program(nc, ctx, plan)
        V, A, T, G = nc.vector, nc.scalar, nc.tensor, nc.gpsimd
        pe, act, dve, pool, sp = p.pe, p.act, p.dve, p.pool, p.sp

        def sb(name, shape, where=ctx, dt=F32):
            return where.enter_context(nc.sbuf_tensor(name, shape, dt))

        SEQ, D = t["x"].shape[1], t["x"].shape[2]
        KC = D // P
        TT = SEQ // P
        HALF = 512
        NH = SEQ // HALF
        CTX = t["ctx_2"].shape[1]
        ALL = CTX + SEQ
        FF = t["w_ffn1_down"].shape[1]
        EPS = 1e-6

        bank = [Buffer(p, f"bank{n}", ctx.enter_context(nc.psum_tensor(f"bank{n}", [P, 512], F32)))
                for n in range(8)]
        xT = sb("xT", [P, KC, SEQ])
        hT = sb("hT", [P, KC, SEQ])
        WCOL = 256
        ring = [Buffer(p, f"ring{n}", sb(f"ring{n}", [P, KC * WCOL]), loads=True) for n in range(4)]
        ident = sb("ident", [P, P])
        ones = sb("ones", [P, P])
        ones64 = sb("ones64", [P, P])
        eps = sb("eps", [P, 1])
        squares = [Buffer(p, f"squares{n}", sb(f"squares{n}", [P, HALF])) for n in range(2)]
        inv = Buffer(p, "inv", sb("inv", [P, HALF]))
        stdev = Buffer(p, "stdev", sb("stdev", [P, HALF]))
        temps = [Buffer(p, f"temp{n}", sb(f"temp{n}", [P, HALF])) for n in range(2)]
        PACK_A = ["norm_ffn1", "norm_mix", "norm_ffn2", "conv_b", "conv_w", "lru_b_gates", "lru_lambda"]
        PACK_B = ["norm1_g_2", "norm2_g_2", "conv_w_2", "gdn_norm_g_2", "c_2", "c_ctx_2", "b_mod_2"]
        packs = [Buffer(p, f"pack{n}", None, loads=True) for n in range(2)]
        cols = [sb(f"cols{n}", [P, P]) for n in range(2)]
        column = {}
        stream = {n: Counter(p, n, by=16) for n in ("bias_in", "gates_in", "shift_in", "scratch_out")}

        skew = nc.dram_tensor("skew", [240, 64, P], F32, kind="Internal").ap()

        zeroed = pool.did(G.memset(ident[:, :], 0.0))
        pool.wait(zeroed)
        have_ident = pool.did(G.affine_select(out=ident[:, :], in_=ident[:, :], compare_op=ALU.not_equal, fill=1.0,
                                              base=0, pattern=[[-1, P]], channel_multiplier=1))
        V.memset(ones[:, :], 1.0)
        V.memset(eps[:, :], EPS)
        have_zero64 = dve.did(V.memset(ones64[:, :], 0.0))
        dve.wait(have_zero64)
        V.memset(ones64[0:64, 0:64], 1.0)
        have_ones = dve.did(V.memset(ones64[64:P, 64:P], 1.0))

        with ExitStack() as own:
            for n, names in enumerate((PACK_A, PACK_B)):
                rows = sb(f"rows{n}", [P, P], own)
                cleared = pool.did(G.memset(rows[:, :], 0.0))
                sp.wait(cleared)
                at = 0
                for name in names:
                    src = t[name]
                    flat = src if len(src.shape) == 1 else src.rearrange(
                        {2: "a b -> (a b)", 3: "a b c -> (a b c)", 4: "a b c d -> (a b c d)"}[len(src.shape)])
                    k = flat.shape[0] // P
                    loaded = packs[n].more(sp, rows[at:at + k, :], flat.rearrange("(k q) -> k q", q=P))
                    column[name] = (n, at)
                    at += k
                if n == 1:
                    for name in ("q_norm", "k_norm"):
                        for h in range(2):
                            loaded = packs[n].more(sp, rows[at:at + 1, h * 64:h * 64 + 64], t[name])
                        column[name] = (n, at)
                        at += 1
                pe.wait(loaded, have_ident, have_ones)
                turned = pe.did(T.transpose(bank[n].mem[:, 0:P], rows[:, :], ident[:, :]))
                dve.wait(turned)
                have_cols = dve.did(V.tensor_copy(cols[n][:, :], bank[n].mem[:, 0:P]))
                bank[n].guard.mark(have_cols)

            def col(name, k=0, n=1):
                which, at = column[name]
                return cols[which][:, at + k:at + k + n]

        def evacuate(n, dst, src):
            if n % 2:
                return act.did(A.activation(dst, src, ACT.Copy))
            return dve.did(V.tensor_copy(dst, src))

        def turn_in(src, dst, n_tiles, name, tiles_a_pass):
            rows = src.rearrange("(n q) d -> q n d", q=P)
            with p.repeat(name, n_tiles // tiles_a_pass) as i:
                for s in range(tiles_a_pass // 2):
                    slot = ring[s]
                    tiles = slot.mem[:, :].rearrange("q (n d) -> q n d", n=2)
                    here = slot.load(sp, tiles, rows[:, bass.ds(i * tiles_a_pass + 2 * s, 2), :])
                    for n in range(2):
                        for g in range(2):
                            b = bank[4 * s + 2 * n + g]
                            pe.wait(here)
                            b.guard.wait(pe)
                            for k in range(4):
                                done = T.transpose(b.mem[:, k * P:(k + 1) * P],
                                                   tiles[:, n, (4 * g + k) * P:(4 * g + k + 1) * P], ident[:, :])
                            done = pe.did(done)
                            (act if g else dve).wait(done)
                            out_ap = dst(i * tiles_a_pass + 2 * s + n, 4 * g)
                            b.guard.mark(evacuate(g, out_ap, b.mem[:, :].rearrange("q (k c) -> q k c", k=4)))
                    slot.guard.mark(done)

        turn_in(t["x"][0], lambda n, k: xT[:, k:k + 4, bass.ds(n * P, P)], TT, "turn_x", 4)

        def settle(*engines):
            p.barrier(*engines)

        def rms(src, dst, gain, blocks, shift=None, ready=()):
            finals = []
            for n, (c0, w) in enumerate(blocks):
                b = bank[n % 2]
                b.guard.wait(pe)
                for k in range(KC):
                    sq = squares[k % 2]
                    sq.guard.wait(act)
                    act.wait(*ready)
                    squared = act.did(A.activation(sq.mem[:, 0:w], src(c0, w, k), ACT.Square))
                    pe.wait(squared)
                    summed = pe.did(T.matmul(b.mem[:, 0:w], ones[:, :], sq.mem[:, 0:w], start=k == 0, stop=k == KC - 1))
                    sq.guard.mark(summed)
                act.wait(summed)
                stdev.guard.wait(act)
                rooted = act.did(A.activation(stdev.mem[:, 0:w], b.mem[:, 0:w], ACT.Sqrt, bias=eps[:, :],
                                              scale=1.0 / D))
                b.guard.mark(rooted)
                dve.wait(rooted, *ready)
                inv.guard.wait(dve)
                inverted = dve.did(V.reciprocal(inv.mem[:, 0:w], stdev.mem[:, 0:w]))
                stdev.guard.mark(inverted)
                dve.wait(inverted)
                for k in range(KC):
                    done = dve.did(V.scalar_tensor_tensor(out=dst(c0, w, k), in0=src(c0, w, k), scalar=gain(k),
                                                          in1=inv.mem[:, 0:w], op0=ALU.mult, op1=ALU.mult))
                    if shift is not None:
                        act.wait(done)
                        moved = act.did(A.activation(dst(c0, w, k), dst(c0, w, k), ACT.Identity, bias=shift(k)))
                inv.guard.mark(done)
                finals = [done] if shift is None else [moved]
            return finals

        HALVES = [(h * HALF, HALF) for h in range(NH)]
        at_x = lambda c, w, k: xT[:, k, c:c + w]
        at_h = lambda c, w, k: hT[:, k, c:c + w]

        def swiglu(name, gain, w_gu, w_down):
            settle()
            NF = FF // P
            normed = rms(at_x, at_h, lambda k: col(gain, k), HALVES)
            wide = w_gu.rearrange("(k q) n -> q k n", q=P)
            tall = w_down.rearrange("(k q) n -> q k n", q=P)
            with ExitStack() as own:
                hidden = sb(name + "_hidden", [P, NF, SEQ], own)
                pe.wait(*normed)
                with p.repeat(name + "_up", FF // WCOL) as i:
                    tiles, here = [], []
                    for s in range(2):
                        tile = ring[s].mem[:, :].rearrange("q (k n) -> q k n", k=KC)
                        here.append(ring[s].load(sp, tile, wide[:, :, bass.ds(i * WCOL + s * FF, WCOL)]))
                        tiles.append(tile)
                    for c in range(WCOL // P):
                        for h in range(NH):
                            g, u = (bank[(c * NH + h) * 2 + s] for s in range(2))
                            both = []
                            for s, b in enumerate((g, u)):
                                b.guard.wait(pe)
                                pe.wait(here[s])
                                for k in range(KC):
                                    done = T.matmul(b.mem[:, :], tiles[s][:, k, c * P:(c + 1) * P],
                                                    hT[:, k, h * HALF:(h + 1) * HALF], start=k == 0, stop=k == KC - 1)
                                both.append(pe.did(done))
                                ring[s].guard.mark(both[-1])
                            tmp = temps[h]
                            tmp.guard.wait(act)
                            act.wait(both[0])
                            gated = act.did(A.activation(tmp.mem[:, :], g.mem[:, :], ACT.Silu))
                            g.guard.mark(gated)
                            dve.wait(gated, both[1])
                            made = dve.did(V.tensor_tensor(hidden[:, bass.ds(2 * i + c, 1), h * HALF:(h + 1) * HALF],
                                                           u.mem[:, None, :], tmp.mem[:, None, :], ALU.mult))
                            u.guard.mark(made)
                            tmp.guard.mark(made)
                pe.wait(made)
                parts = [(k, min(KC, NF - k)) for k in range(0, NF, KC)]
                with p.repeat(name + "_down", D // WCOL) as i:
                    for s, (k0, kn) in enumerate(parts):
                        tile = ring[s].mem[:, 0:kn * WCOL].rearrange("q (k n) -> q k n", k=kn)
                        here = ring[s].load(sp, tile, tall[:, k0:k0 + kn, bass.ds(i * WCOL, WCOL)])
                        pe.wait(here)
                        for c in range(WCOL // P):
                            for h in range(NH):
                                b = bank[c * NH + h]
                                if s == 0:
                                    b.guard.wait(pe)
                                for k in range(kn):
                                    done = T.matmul(b.mem[:, :], tile[:, k, c * P:(c + 1) * P],
                                                    hidden[:, k0 + k, h * HALF:(h + 1) * HALF],
                                                    start=k0 + k == 0, stop=k0 + k == NF - 1)
                                done = pe.did(done)
                                if s == len(parts) - 1:
                                    dve.wait(done)
                                    x_at = xT[:, bass.ds(2 * i + c, 1), h * HALF:(h + 1) * HALF]
                                    b.guard.mark(dve.did(V.scalar_tensor_tensor(
                                        out=x_at, in0=b.mem[:, None, :], scalar=0.5, in1=x_at,
                                        op0=ALU.mult, op1=ALU.add)))
                        ring[s].guard.mark(done)

        def turn_out(dst, name, src):
            rows = dst.rearrange("(n q) d -> q n d", q=P)
            with ExitStack() as own:
                lines = [Buffer(p, f"{name}_line{n}", sb(f"{name}_line{n}", [P, D], own), loads=True) for n in range(2)]
                with p.repeat(name, TT // 2) as i:
                    for n in range(2):
                        line = lines[n]
                        for g in range(2):
                            b = bank[2 * n + g]
                            col0 = temps[g]
                            b.guard.wait(pe)
                            col0.guard.wait(dve)
                            staged = dve.did(V.tensor_copy(
                                col0.mem[:, :].rearrange("q (k c) -> q k c", k=4),
                                src[:, 4 * g:4 * g + 4, bass.ds((2 * i + n) * P, P)]))
                            pe.wait(staged)
                            for k in range(4):
                                done = T.transpose(b.mem[:, k * P:(k + 1) * P], col0.mem[:, k * P:(k + 1) * P], ident[:, :])
                            done = pe.did(done)
                            col0.guard.mark(done)
                            act.wait(done)
                            if g == 0:
                                line.guard.wait(act)
                            moved = act.did(A.activation(line.mem[:, g * HALF:(g + 1) * HALF], b.mem[:, :], ACT.Copy))
                            b.guard.mark(moved)
                        sp.wait(moved)
                        line.guard.mark(line.loads.did(nc.sync.dma_start(rows[:, bass.ds(2 * i + n, 1), :], line.mem[:, None, :])))
                settle()

        e = Shared()
        e.p, e.nc, e.t, e.sb, e.bank = p, nc, t, sb, bank
        e.ring, e.xT, e.hT, e.ident, e.ones = ring, xT, hT, ident, ones
        e.ones64, e.eps, e.squares, e.inv, e.stdev = ones64, eps, squares, inv, stdev
        e.temps, e.column, e.cols, e.col, e.stream = temps, column, cols, col, stream
        e.skew, e.SEQ, e.D, e.KC, e.TT = skew, SEQ, D, KC, TT
        e.HALF, e.NH, e.CTX, e.ALL, e.WCOL = HALF, NH, CTX, ALL, WCOL
        e.HALVES, e.at_x, e.at_h, e.evacuate, e.turn_in = HALVES, at_x, at_h, evacuate, turn_in
        e.turn_out, e.settle, e.rms = turn_out, settle, rms

        swiglu("ffn1", "norm_ffn1", t["w_ffn1_gu"][0], t["w_ffn1_down"][0])
        mix_block(e)
        swiglu("ffn2", "norm_ffn2", t["w_ffn2_gu"][0], t["w_ffn2_down"][0])
        second_block(e, out)
        p.barrier(sp)
        return p.counts, p.carried


def softplus(e, x, out, w, parts, where, name):
    p, nc = e.p, e.nc
    V, dve, act = nc.vector, p.dve, p.act
    y, u, s, acc = (e.sb(f"{name}_{n}", [P, w], where) for n in ("y", "u", "u2", "sum"))
    y, u, s, acc = (b[0:parts, :] for b in (y, u, s, acc))

    def step(ins):
        done = dve.did(ins)
        dve.wait(done)
        return done

    act.wait(step(V.scalar_tensor_tensor(out=y, in0=x, scalar=-1.0, in1=x, op0=ALU.mult, op1=ALU.max)))
    dve.wait(act.did(nc.scalar.activation(y, y, ACT.Exp, scale=-1.0)))
    step(V.tensor_scalar(u, y, 2.0, None, ALU.add))
    step(V.reciprocal(u, u))
    step(V.tensor_tensor(u, u, y, ALU.mult))
    step(V.tensor_tensor(s, u, u, ALU.mult))
    terms = 9
    step(V.tensor_scalar(acc, s, 1.0 / (2 * terms - 1), None, ALU.mult))
    for n in range(terms - 2, 0, -1):
        step(V.scalar_tensor_tensor(out=acc, in0=acc, scalar=1.0 / (2 * n + 1), in1=s, op0=ALU.add, op1=ALU.mult))
    step(V.scalar_tensor_tensor(out=acc, in0=acc, scalar=1.0, in1=u, op0=ALU.add, op1=ALU.mult))
    step(V.tensor_scalar(acc, acc, 2.0, None, ALU.mult))
    return step(V.scalar_tensor_tensor(out=out, in0=x, scalar=0.0, in1=acc, op0=ALU.max, op1=ALU.add))


def mix_block(e):
    p, nc, t = e.p, e.nc, e.t
    V, A, T, G = nc.vector, nc.scalar, nc.tensor, nc.gpsimd
    pe, act, dve, pool, sp = p.pe, p.act, p.dve, p.pool, p.sp
    bank, ring, hT, xT, ident = e.bank, e.ring, e.hT, e.xT, e.ident
    SEQ, KC, HALF, NH, TT, D = e.SEQ, e.KC, e.HALF, e.NH, e.TT, e.D
    GRID, WROWS, WCOLS, HD = 64, 8, 16, t["q_norm"].shape[1]
    NROW = SEQ // GRID
    NDR, NDC = t["rel_pos_bias"].shape[2:]
    HEADS = t["rel_pos_bias"].shape[1]
    CONV, LEFT = t["conv_w"].shape[1], 2
    MASKED = -1e30

    e.settle()
    with ExitStack() as own:
        yT = e.sb("yT", [P, KC, SEQ], own)
        slope = e.sb("slope", [P, 16], own)
        minus = e.sb("minus_slope", [P, 16], own)
        qgain = e.sb("qgain", [P, 1], own)
        part = ExitStack()

        def buf(name, shape, loads=False):
            return Buffer(p, "mix_" + name, e.sb("mix_" + name, shape, part), loads)

        normed = e.rms(e.at_x, e.at_h, lambda k: e.col("norm_mix", k), e.HALVES)

        lanes = HEADS * NDR // 2
        with ExitStack() as first:
            wide = e.sb("bias_rows", [P, 2, P], first)
            wiped = pool.did(G.memset(wide[:, :, :], 0.0))
            sp.wait(wiped)
            rows = t["rel_pos_bias"][0].rearrange("h r c -> (h r) c").rearrange("(a b) c -> b a c", b=lanes)
            start = GRID - 1 - (NDC - 1) // 2
            got = e.stream["bias_in"].did(nc.sync.dma_start(wide[0:lanes, :, start:start + NDC], rows))
            sp.wait(got)
            for a in range(2):
                spread = e.stream["scratch_out"].did(nc.sync.dma_start(
                    e.skew[a * lanes:(a + 1) * lanes, :, :], wide[0:lanes, a, None, :].broadcast_to([lanes, GRID, P])))
            dve.wait(dve.did(V.tensor_scalar(slope[:, :], e.col("lru_lambda", 0, 16), -1.0, None, ALU.mult)))
            softplus(e, slope[:, :], slope[:, :], 16, P, first, "softplus")
            dve.did(V.tensor_scalar(minus[:, :], slope[:, :], -8.0, None, ALU.mult))
            V.tensor_scalar(qgain[:, :], e.col("q_norm"), HD ** -0.5, None, ALU.mult)
            dve.wait(dve.last())
            have_slopes = dve.did(V.tensor_scalar(slope[:, :], slope[:, :], 8.0, None, ALU.mult))
            sp.wait(spread)
            act.wait(have_slopes)
            e.settle()

        q, k, att, xc, r, ig, hs, outer, sgb = (
            buf(n, [P, SEQ]) for n in ("q", "k", "att", "xc", "r", "ig", "hs", "outer", "sgb"))
        v = buf("v", [P, TT, P])
        vodd = buf("vodd", [P, TT - 1, P], True)
        xr = buf("xr", [P, SEQ + CONV - 1])
        bias = buf("bias", [P, NDR, GRID], True)
        wgate = buf("wgate", [P, 4, P], True)
        prob = [buf(f"prob{n}", [P, HALF]) for n in range(2)]
        probT = [buf(f"probT{n}", [P, HALF]) for n in range(2)]
        diag = [buf(f"diag{n}", [P, P]) for n in range(2)]
        stat = [buf(f"stat{n}", [P, 4]) for n in range(2)]

        cleared = [pool.did(G.memset(xr.mem[:, :], 0.0)), pool.did(G.memset(wgate.mem[:, :, :], 0.0))]
        sp.wait(*cleared)
        act.wait(*cleared)
        w_in = t["w_in"][0].rearrange("(k q) (b n) -> q k b n", q=P, b=7)
        XR, GR, QB, KB, VB, GA, GB = range(7)
        skewed = bass.AP(e.skew.tensor, GRID - 1, [[NDR * GRID * P, HEADS], [P - 1, GRID], [GRID * P, NDR], [1, GRID]])
        gates = t["lru_w_gates"][0].rearrange("d g n i o -> n i (d g) o")
        pe.wait(*normed)

        with p.repeat("mix", KC) as i:
            where = {}
            for s, blocks in enumerate(((QB, KB), (VB, XR), (GR, GA), (GB,))):
                tile = ring[s].mem[:, :].rearrange("q (b k n) -> q b k n", b=2, k=KC)
                ring[s].guard.wait(sp)
                for n, b in enumerate(blocks):
                    here = ring[s].more(sp, tile[:, n, :, :], w_in[:, :, b, bass.ds(i * P, P)])
                for n, b in enumerate(blocks):
                    where[b] = (ring[s], tile[:, n, :, :], here)
            bias.guard.wait(sp)
            for h in range(2):
                have_bias = bias.more(sp, bias.mem[h * 64:h * 64 + 64, :, :], skewed[bass.ds(2 * i + h, 1), :, :, :].rearrange("a c r w -> (a c) r w"))
            wgate.guard.wait(sp)
            for h in range(2):
                have_gates = wgate.more(sp, wgate.mem[h * 64:h * 64 + 64, :, h * 64:h * 64 + 64],
                                        gates[bass.ds(2 * i + h, 1), :, :, :].rearrange("a i g o -> (a i) g o"))
            pool.wait(have_bias)
            for h in range(2):
                for lo, sign, base in ((0, 1, WCOLS // 2), (WCOLS, -1, WCOLS // 2 - 1 - WCOLS)):
                    part_ap = bias.mem[h * 64:h * 64 + 64, :, lo:lo + GRID - WCOLS]
                    masked = pool.did(G.affine_select(out=part_ap, in_=part_ap, compare_op=ALU.is_ge, fill=MASKED,
                                                      base=base, pattern=[[0, NDR], [sign, GRID - WCOLS]],
                                                      channel_multiplier=-sign))
                    pool.wait(masked)

            turn = [0]

            def project(block, h):
                slot, tile, here = where[block]
                b = bank[turn[0] % 2]
                turn[0] += 1
                b.guard.wait(pe)
                pe.wait(here)
                for kc in range(KC):
                    done = T.matmul(b.mem[:, :], tile[:, kc, :], hT[:, kc, h * HALF:(h + 1) * HALF],
                                    start=kc == 0, stop=kc == KC - 1)
                done = pe.did(done)
                slot.guard.mark(done)
                return b, done

            def norm_heads(block, dst, gain):
                finals = []
                for h in range(NH):
                    at = dst.mem[:, h * HALF:(h + 1) * HALF]
                    b, done = project(block, h)
                    act.wait(done)
                    if h == 0:
                        dst.guard.wait(act)
                    copied = act.did(A.activation(at, b.mem[:, :], ACT.Copy))
                    sq = e.squares[h % 2]
                    sq.guard.wait(act)
                    squared = act.did(A.activation(sq.mem[:, :], b.mem[:, :], ACT.Square))
                    b.guard.mark(squared)
                    s = bank[6 + h]
                    s.guard.wait(pe)
                    pe.wait(squared)
                    summed = pe.did(T.matmul(s.mem[:, :], e.ones64[:, :], sq.mem[:, :], start=True, stop=True))
                    sq.guard.mark(summed)
                    act.wait(summed)
                    e.stdev.guard.wait(act)
                    rooted = act.did(A.activation(e.stdev.mem[:, :], s.mem[:, :], ACT.Sqrt, bias=e.eps[:, :],
                                                  scale=1.0 / HD))
                    s.guard.mark(rooted)
                    dve.wait(rooted)
                    e.inv.guard.wait(dve)
                    inverted = dve.did(V.reciprocal(e.inv.mem[:, :], e.stdev.mem[:, :]))
                    e.stdev.guard.mark(inverted)
                    dve.wait(inverted, copied)
                    finals.append(dve.did(V.scalar_tensor_tensor(out=at, in0=at, scalar=gain, in1=e.inv.mem[:, :],
                                                                 op0=ALU.mult, op1=ALU.mult)))
                    e.inv.guard.mark(finals[-1])
                return finals[-1]

            q_ready = norm_heads(QB, q, qgain[:, :])
            k_ready = norm_heads(KB, k, e.col("k_norm"))

            slot, tile, here = where[VB]
            for g in range(2):
                b = bank[turn[0] % 2]
                turn[0] += 1
                b.guard.wait(pe)
                pe.wait(here)
                for n in range(4):
                    for kc in range(KC):
                        done = T.matmul(b.mem[:, n * P:(n + 1) * P], hT[:, kc, (4 * g + n) * P:(4 * g + n + 1) * P],
                                        tile[:, kc, :], start=kc == 0, stop=kc == KC - 1)
                done = pe.did(done)
                slot.guard.mark(done)
                dve.wait(done)
                if g == 0:
                    v.guard.wait(dve)
                v_ready = dve.did(V.tensor_copy(v.mem[:, 4 * g:4 * g + 4, :],
                                                b.mem[:, :].rearrange("q (n c) -> q n c", n=4)))
                b.guard.mark(v_ready)
            sp.wait(v_ready)
            vodd.guard.wait(sp)
            vodd.more(sp, vodd.mem[0:64, :, :], v.mem[64:P, 0:TT - 1, :])
            vodd_ready = vodd.more(sp, vodd.mem[64:P, :, :], v.mem[0:64, 1:TT, :])

            state = {}

            def through(block, h, func, dst, at0=0):
                def run():
                    b, done = project(block, h)
                    act.wait(done)
                    if h == 0:
                        dst.guard.wait(act)
                    lo = at0 + h * HALF
                    made = act.did(A.activation(dst.mem[:, lo:lo + HALF], b.mem[:, :], func))
                    b.guard.mark(made)
                    state[block] = made
                return run

            def gate_outer(h):
                def run():
                    b, done = project(GA, h)
                    tmp = e.temps[h]
                    act.wait(done)
                    tmp.guard.wait(act)
                    made = act.did(A.activation(tmp.mem[:, :], b.mem[:, :], ACT.Sigmoid))
                    b.guard.mark(made)
                    dve.wait(made, state[GR])
                    at = outer.mem[:, h * HALF:(h + 1) * HALF]
                    state["outer"] = dve.did(V.tensor_tensor(at, at, tmp.mem[:, :], ALU.mult))
                    tmp.guard.mark(state["outer"])
                return run

            def convolve():
                dve.wait(state[XR])
                xc.guard.wait(dve)
                done = dve.did(V.tensor_scalar(xc.mem[:, :], xr.mem[:, 0:SEQ], wcol(0), e.cols[bn][:, bass.ds(i + b0, 1)],
                                               ALU.mult, ALU.add))
                for tap in range(1, CONV):
                    dve.wait(done)
                    done = dve.did(V.scalar_tensor_tensor(out=xc.mem[:, :], in0=xr.mem[:, tap:tap + SEQ],
                                                          scalar=wcol(tap), in1=xc.mem[:, :],
                                                          op0=ALU.mult, op1=ALU.add))
                xr.guard.mark(done)
                state["xc"] = done

            bn, b0 = e.column["conv_b"]
            wn, w0 = e.column["conv_w"]
            gn, g0 = e.column["lru_b_gates"]
            wcol = lambda tap: e.cols[wn][:, bass.ds(i + (w0 + tap * KC), 1)]

            def gate(d, g, h):
                dst = (r, ig)[g]

                def run():
                    b = bank[turn[0] % 2]
                    turn[0] += 1
                    b.guard.wait(pe)
                    pe.wait(have_gates, state["xc"])
                    done = pe.did(T.matmul(b.mem[:, :], wgate.mem[:, 2 * d + g, :], xc.mem[:, h * HALF:(h + 1) * HALF],
                                           start=True, stop=True))
                    wgate.guard.mark(done)
                    act.wait(done)
                    if h == 0:
                        dst.guard.wait(act)
                    made = act.did(A.activation(dst.mem[:, h * HALF:(h + 1) * HALF], b.mem[:, :], ACT.Sigmoid,
                                                bias=e.cols[gn][:, bass.ds(i + (g0 + (2 * d + g) * KC), 1)]))
                    b.guard.mark(made)
                    state[("gate", g)] = made
                return run

            def recur(d):
                def run():
                    last = d == 1
                    for h in range(NH):
                        sl = slice(h * HALF, (h + 1) * HALF)
                        th, den = e.temps[0].mem, e.temps[1].mem
                        act.wait(state[("gate", 0)])
                        e.temps[0].guard.wait(act)
                        tanhs = act.did(A.activation(th[:, :], r.mem[:, sl], ACT.Tanh, scale=slope[:, bass.ds(i + d * KC, 1)]))
                        decays = act.did(A.activation(r.mem[:, sl], r.mem[:, sl], ACT.Exp, scale=minus[:, bass.ds(i + d * KC, 1)]))
                        dve.wait(tanhs, state[("gate", 1)])
                        e.temps[1].guard.wait(dve)
                        done = dve.did(V.tensor_scalar(den[:, :], th[:, :], 1.0, None, ALU.add))
                        dve.wait(done)
                        done = dve.did(V.reciprocal(den[:, :], den[:, :]))
                        dve.wait(done)
                        done = dve.did(V.scalar_tensor_tensor(out=th[:, :], in0=th[:, :], scalar=2.0, in1=den[:, :],
                                                              op0=ALU.mult, op1=ALU.mult))
                        e.temps[1].guard.mark(done)
                        act.wait(done)
                        rooted = act.did(A.activation(th[:, :], th[:, :], ACT.Sqrt))
                        done = dve.did(V.tensor_tensor(ig.mem[:, sl], ig.mem[:, sl], xc.mem[:, sl], ALU.mult))
                        dve.wait(done, rooted)
                        done = dve.did(V.tensor_tensor(ig.mem[:, sl], ig.mem[:, sl], th[:, :], ALU.mult))
                        e.temps[0].guard.mark(done)
                    dve.wait(done, decays)
                    if d == 0:
                        hs.guard.wait(dve)
                        done = dve.did(V.tensor_tensor_scan(hs.mem[:, :], r.mem[:, :], ig.mem[:, :], 0.0, ALU.mult, ALU.add))
                        r.guard.mark(done)
                        ig.guard.mark(done)
                        state["h"] = done
                    else:
                        done = dve.did(V.tensor_tensor_scan(xc.mem[:, ::-1], r.mem[:, ::-1], ig.mem[:, ::-1], 0.0,
                                                            ALU.mult, ALU.add))
                        r.guard.mark(done)
                        ig.guard.mark(done)
                        dve.wait(done, state["h"])
                        done = dve.did(V.tensor_tensor(hs.mem[:, :], hs.mem[:, :], xc.mem[:, :], ALU.add))
                        xc.guard.mark(done)
                        dve.wait(done, state["outer"])
                        state["lru"] = dve.did(V.tensor_tensor(hs.mem[:, :], hs.mem[:, :], outer.mem[:, :], ALU.mult))
                        outer.guard.mark(state["lru"])
                return run

            pieces = [through(XR, 0, ACT.Copy, xr, LEFT), through(XR, 1, ACT.Copy, xr, LEFT), convolve,
                      through(GR, 0, ACT.Gelu_apprx_tanh, outer), through(GR, 1, ACT.Gelu_apprx_tanh, outer),
                      gate_outer(0), gate_outer(1),
                      through(GB, 0, ACT.Sigmoid, sgb), through(GB, 1, ACT.Sigmoid, sgb)]
            for d in range(2):
                pieces += [gate(d, 0, 0), gate(d, 0, 1), gate(d, 1, 0), gate(d, 1, 1), recur(d)]

            rows = {}

            def scores(row):
                b, pr, st, dg = bank[2 + row % 2], prob[row % 2], stat[row % 2], diag[row % 2]
                first = min(max(row - WROWS // 2, 0), NROW - WROWS)
                b.guard.wait(pe)
                pe.wait(q_ready, k_ready)
                for h in range(2):
                    hp = slice(h * 64, h * 64 + 64)
                    done = T.matmul(b.mem[hp, :], q.mem[hp, row * GRID:(row + 1) * GRID],
                                    k.mem[hp, first * GRID:first * GRID + HALF], start=True, stop=True)
                done = pe.did(done)
                if row == NROW - 1:
                    q.guard.mark(done)
                    k.guard.mark(done)
                dr = first - row + WROWS - 1
                dve.wait(done, masked)
                pr.guard.wait(dve)
                biased = dve.did(V.tensor_tensor_reduce(
                    pr.mem[:, :], b.mem[:, :], bias.mem[:, dr:dr + WROWS, :].rearrange("q r c -> q (r c)"),
                    1.0, MASKED, ALU.add, ALU.max, st.mem[:, 0:1]))
                b.guard.mark(biased)
                if row == NROW - 1:
                    bias.guard.mark(biased)
                dve.wait(biased)
                negated = dve.did(V.tensor_scalar(st.mem[:, 1:2], st.mem[:, 0:1], -1.0, None, ALU.mult))
                act.wait(negated)
                raised = act.did(A.activation(pr.mem[:, :], pr.mem[:, :], ACT.Exp, bias=st.mem[:, 1:2],
                                              accum_out=st.mem[:, 2:3]))
                rows[row] = [first, raised, None, None]

            def weigh(row):
                st, dg = stat[row % 2], diag[row % 2]
                dve.wait(rows[row][1])
                inverted = dve.did(V.reciprocal(st.mem[:, 3:4], st.mem[:, 2:3]))
                dve.wait(inverted)
                dg.guard.wait(dve)
                rows[row][2] = dve.did(V.tensor_scalar(dg.mem[:, :], ident[:, :], st.mem[:, 3:4], None, ALU.mult))

            def turn_probs(row):
                b, pr, pt, dg = bank[4 + row % 2], prob[row % 2], probT[row % 2], diag[row % 2]
                b.guard.wait(pe)
                pe.wait(rows[row][2], rows[row][1])
                for n in range(4):
                    done = T.matmul(b.mem[:, n * P:(n + 1) * P], pr.mem[:, n * P:(n + 1) * P], dg.mem[:, :],
                                    start=True, stop=True)
                done = pe.did(done)
                pr.guard.mark(done)
                dg.guard.mark(done)
                act.wait(done)
                pt.guard.wait(act)
                rows[row][3] = act.did(A.activation(pt.mem[:, :], b.mem[:, :], ACT.Copy))
                b.guard.mark(rows[row][3])

            def values(row):
                b, pt = bank[6 + row % 2], probT[row % 2]
                first = rows[row][0]
                b.guard.wait(pe)
                pe.wait(rows[row][3], v_ready, vodd_ready)
                for n in range(4):
                    vt = vodd.mem[:, first // 2 + n, :] if first % 2 else v.mem[:, first // 2 + n, :]
                    done = T.matmul(b.mem[:, 0:P], vt, pt.mem[:, n * P:(n + 1) * P], start=n == 0, stop=n == 3)
                done = pe.did(done)
                pt.guard.mark(done)
                if row == NROW - 1:
                    v.guard.mark(done, vodd_ready)
                    vodd.guard.mark(done)
                dve.wait(done)
                if row == 0:
                    att.guard.wait(dve)
                for h in range(2):
                    hp = slice(h * 64, h * 64 + 64)
                    kept = dve.did(V.tensor_copy(att.mem[hp, row * GRID:(row + 1) * GRID], b.mem[hp, h * 64:h * 64 + 64]))
                b.guard.mark(kept)
                return kept

            for step in range(NROW + 3):
                if step >= 1 and step - 1 < NROW:
                    weigh(step - 1)
                if step < NROW:
                    scores(step)
                if pieces:
                    pieces.pop(0)()
                if 0 <= step - 1 < NROW:
                    turn_probs(step - 1)
                if 0 <= step - 2 < NROW:
                    kept = values(step - 2)
            while pieces:
                pieces.pop(0)()
            dve.wait(kept, state["lru"], state[GB])
            done = dve.did(V.tensor_tensor(att.mem[:, :], att.mem[:, :], sgb.mem[:, :], ALU.mult))
            sgb.guard.mark(done)
            dve.wait(done)
            done = dve.did(V.tensor_tensor(yT[:, bass.ds(i, 1), :], att.mem[:, None, :], hs.mem[:, None, :], ALU.add))
            att.guard.mark(done)
            hs.guard.mark(done)
        part.close()
        add_product(e, "mix_out", t["w_out"][0], lambda k, c: yT[:, k, c], done)


def add_product(e, name, w, rhs, ready, scale=None):
    p, nc = e.p, e.nc
    V, T = nc.vector, nc.tensor
    wide = w.rearrange("(k q) n -> q k n", q=P)
    KC, HALF = e.KC, e.HALF
    C = e.WCOL // P
    p.pe.wait(ready)
    with p.repeat(name, e.D // e.WCOL // 2) as i:
        for s in range(2):
            slot = e.ring[s]
            tile = slot.mem[:, :].rearrange("q (k n) -> q k n", k=KC)
            here = slot.load(p.sp, tile, wide[:, :, bass.ds((2 * i + s) * e.WCOL, e.WCOL)])
            p.pe.wait(here)
            for c in range(C):
                for h in range(e.NH):
                    b = e.bank[(s * C + c) * e.NH + h]
                    b.guard.wait(p.pe)
                    for k in range(KC):
                        done = T.matmul(b.mem[:, :], tile[:, k, c * P:(c + 1) * P], rhs(k, slice(h * HALF, (h + 1) * HALF)),
                                        start=k == 0, stop=k == KC - 1)
                    done = p.pe.did(done)
                    p.dve.wait(done)
                    x_at = e.xT[:, bass.ds((2 * i + s) * C + c, 1), h * HALF:(h + 1) * HALF]
                    by = 1.0 if scale is None else scale(i, s * C + c)
                    b.guard.mark(p.dve.did(V.scalar_tensor_tensor(out=x_at, in0=b.mem[:, None, :], scalar=by, in1=x_at,
                                                                 op0=ALU.mult, op1=ALU.add)))
            slot.guard.mark(done)


def second_block(e, out):
    p, nc, t = e.p, e.nc, e.t
    V, A, T, G = nc.vector, nc.scalar, nc.tensor, nc.gpsimd
    pe, act, dve, pool, sp = p.pe, p.act, p.dve, p.pool, p.sp
    bank, ring, hT, xT, ident, ones = e.bank, e.ring, e.hT, e.xT, e.ident, e.ones
    SEQ, KC, HALF, NH, TT, D, CTX, ALL = e.SEQ, e.KC, e.HALF, e.NH, e.TT, e.D, e.CTX, e.ALL
    WCOL = e.WCOL
    H2, HD2 = 4, 128
    WIDE = H2 * HD2
    NT, NCT = ALL // P, CTX // P
    DIRS = 2
    e.settle()

    def step(counter, ins):
        done = counter.did(ins)
        counter.wait(done)
        return done

    q_rows = nc.dram_tensor("q_cols", [NT, P, H2, P], F32, kind="Internal").ap()
    k_cols = nc.dram_tensor("k_cols", [NT, P, H2, P], F32, kind="Internal").ap()
    k_rows = nc.dram_tensor("k_rows", [NT, P, H2, P], F32, kind="Internal").ap()
    v_rows = nc.dram_tensor("v_rows", [NT, P, H2, P], F32, kind="Internal").ap()
    f_rows = nc.dram_tensor("f_rows", [SEQ, D], F32, kind="Internal").ap()
    sum_rows = nc.dram_tensor("sum_rows", [SEQ, D], F32, kind="Internal").ap()
    gate_row = nc.dram_tensor("gate_row", [D], F32, kind="Internal").ap()

    with ExitStack() as own:
        N_MOD = t["w_mod_2"].shape[2] // P
        mod = e.sb("mod", [P, N_MOD, 2], own)
        gains = e.sb("gains", [P, 3, KC], own)
        dec_in = e.sb("dec_in", [P, NT, 8], own)
        beta = e.sb("beta", [P, NT, 8], own)
        with ExitStack() as first:
            cond = e.sb("cond", [P, KC, 2], first)
            for n, name in enumerate(("c_2", "c_ctx_2")):
                have_cond = act.did(A.activation(cond[:, :, n], e.col(name, 0, KC), ACT.Silu))
            pe.wait(have_cond)
            wide = t["w_mod_2"][0].rearrange("(k q) n -> q k n", q=P)
            C = WCOL // P
            with p.repeat("modulate", N_MOD // C // 4) as i:
                for s in range(4):
                    tile = ring[s].mem[:, :].rearrange("q (k n) -> q k n", k=KC)
                    here = ring[s].load(sp, tile, wide[:, :, bass.ds((4 * i + s) * WCOL, WCOL)])
                    b = bank[s]
                    b.guard.wait(pe)
                    pe.wait(here)
                    for c in range(C):
                        for k in range(KC):
                            done = T.matmul(b.mem[:, 2 * c:2 * c + 2], tile[:, k, c * P:(c + 1) * P], cond[:, k, :],
                                            start=k == 0, stop=k == KC - 1)
                    done = pe.did(done)
                    ring[s].guard.mark(done)
                    dve.wait(done)
                    made = dve.did(V.tensor_copy(mod[:, bass.ds((4 * i + s) * C, C), :],
                                                 b.mem[:, 0:2 * C].rearrange("q (c v) -> q c v", c=C)))
                    b.guard.mark(made)
            dve.wait(made)
            for v in range(2):
                done = step(dve, V.tensor_tensor(mod[:, :, v], mod[:, :, v], e.col("b_mod_2", 0, N_MOD), ALU.add))
            e.settle()
        SH1, SC1, GT1, SH2, SC2, GT2 = (n * KC for n in range(6))
        for n, (name, at, v) in enumerate((("norm1_g_2", SC1, 0), ("norm1_g_2", SC1, 1), ("norm2_g_2", SC2, 0))):
            have_gains = step(dve, V.scalar_tensor_tensor(out=gains[:, n, :], in0=mod[:, at:at + KC, v], scalar=1.0,
                                                          in1=e.col(name, 0, KC), op0=ALU.add, op1=ALU.mult))
        act.wait(have_gains)

        late = ExitStack()
        zs = e.sb("zs", [P, H2, SEQ], late)
        ya = e.sb("ya", [P, H2, SEQ], late)
        with ExitStack() as mid:
            cT = e.sb("cT", [P, KC, CTX], mid)
            e.turn_in(t["ctx_2"][0], lambda n, k: cT[:, k:k + 4, bass.ds(n * P, P)], NCT, "turn_ctx", 2)
            e.settle()
            at_c = lambda c, w, k: cT[:, k, c:c + w]
            e.rms(at_c, at_c, lambda k: gains[:, 1, k:k + 1], [(0, CTX)], shift=lambda k: mod[:, SH1 + k, 1:2])
            normed = e.rms(e.at_x, e.at_h, lambda k: gains[:, 0, k:k + 1], e.HALVES,
                           shift=lambda k: mod[:, SH1 + k, 0:1])
            e.settle()
            w_in = t["w_in_2"][0]
            by_k = w_in.rearrange("(k q) n -> q k n", q=P)
            COL_AB = 3 * WIDE
            COL_Z = COL_AB + 16
            COL_U = COL_Z + WIDE
            COL_V = COL_U + WIDE

            with ExitStack() as gate_mem:
                wab = Buffer(p, "wab", e.sb("wab", [P, KC, 16], gate_mem), True)
                wide_vec = Buffer(p, "wide_vec", e.sb("wide_vec", [P, 2, 8], gate_mem), True)
                here = wab.load(sp, wab.mem[:, :, :], by_k[:, :, COL_AB:COL_AB + 16])
                for n, name in enumerate(("a_log_2", "dt_bias_2")):
                    vec = wide_vec.more(sp, wide_vec.mem[:, n, :],
                                        t[name][0].rearrange("a b -> (a b)").partition_broadcast(P))
                pe.wait(here)
                for n in range(NT):
                    for k in range(KC):
                        lhs = cT[:, k, n * P:(n + 1) * P] if n < NCT else hT[:, k, (n - NCT) * P:(n - NCT + 1) * P]
                        done = T.matmul(bank[0].mem[:, 16 * n:16 * n + 16], lhs, wab.mem[:, k, :],
                                        start=k == 0, stop=k == KC - 1)
                done = pe.did(done)
                ab = bank[0].mem[:, 0:16 * NT].rearrange("q (n c) -> q n c", n=NT)
                act.wait(done, vec)
                act.did(A.activation(beta[:, :, :], ab[:, :, 8:16], ACT.Sigmoid))
                act.did(A.activation(wide_vec.mem[:, 0, :], wide_vec.mem[:, 0, :], ACT.Exp))
                dve.wait(done, vec, act.last())
                shape = [P, NT, 8]
                step(dve, V.tensor_tensor(dec_in[:, :, :], ab[:, :, 0:8],
                                          wide_vec.mem[:, 1, None, :].broadcast_to(shape), ALU.add))
                flat = dec_in[:, :, :].rearrange("q n c -> q (n c)")
                softplus(e, flat, flat, NT * 8, P, gate_mem, "softplus2")
                done = step(dve, V.scalar_tensor_tensor(out=dec_in[:, :, :], in0=dec_in[:, :, :], scalar=-1.0,
                                                        in1=wide_vec.mem[:, 0, None, :].broadcast_to(shape),
                                                        op0=ALU.mult, op1=ALU.mult))
                bank[0].guard.mark(done)
                e.settle()

            GAP = 2
            LEN = ALL + GAP
            BLOCKS = [(0, 512), (512, 512), (1024, LEN - 1024)]
            with ExitStack() as conv_mem:
                pre = [Buffer(p, f"pre{n}", e.sb(f"pre{n}", [P, LEN + 2], conv_mem)) for n in range(2)]
                post = [Buffer(p, f"post{n}", e.sb(f"post{n}", [P, LEN], conv_mem)) for n in range(3)]
                turned = [Buffer(p, f"turned{n}", e.sb(f"turned{n}", [P, NT, P], conv_mem), True) for n in range(2)]
                colsto = [Buffer(p, f"colsto{n}", None, True) for n in range(2)]
                for b in pre:
                    clear = pool.did(G.memset(b.mem[:, :], 0.0))
                dve.wait(clear)
                act.wait(clear)
                split = w_in[:, 0:3 * WIDE].rearrange("(k q) (b n) -> q k b n", q=P, b=3)
                wn, w0 = e.column["conv_w_2"]
                places = lambda m: [(m[:, 0:CTX], 0), (m[:, CTX + GAP:LEN], 1)]
                with p.repeat("qkv", H2) as i:
                    posts = []
                    for j in range(3):
                        tile = ring[j].mem[:, 0:KC * P].rearrange("q (k n) -> q k n", k=KC)
                        here = ring[j].load(sp, tile, split[:, :, j, bass.ds(i * P, P)])
                        pe.wait(here)
                        pr, po = pre[j % 2], post[j]
                        pr.guard.wait(act)
                        pr.guard.wait(dve)
                        for n in range(NH + 1):
                            b = bank[(j * 3 + n) % 4]
                            b.guard.wait(pe)
                            w = HALF if n < NH else CTX
                            for k in range(KC):
                                rhs = hT[:, k, n * HALF:(n + 1) * HALF] if n < NH else cT[:, k, :]
                                done = T.matmul(b.mem[:, 0:w], tile[:, k, :], rhs, start=k == 0, stop=k == KC - 1)
                            done = pe.did(done)
                            at = 1 + CTX + GAP + n * HALF if n < NH else 1
                            (act if n % 2 else dve).wait(done)
                            moved = e.evacuate(n, pr.mem[:, at:at + w], b.mem[:, 0:w])
                            b.guard.mark(moved)
                            dve.wait(moved)
                        ring[j].guard.mark(done)
                        wcol = lambda tap: e.cols[wn][:, bass.ds(i + (w0 + tap * 3 * H2 + j * H2), 1)]
                        po.guard.wait(dve)
                        done = step(dve, V.tensor_scalar(po.mem[:, :], pr.mem[:, 0:LEN], wcol(0), None, ALU.mult))
                        for tap in range(1, 3):
                            done = step(dve, V.scalar_tensor_tensor(out=po.mem[:, :], in0=pr.mem[:, tap:tap + LEN],
                                                                    scalar=wcol(tap), in1=po.mem[:, :],
                                                                    op0=ALU.mult, op1=ALU.add))
                        pr.guard.mark(done)
                        act.wait(done)
                        ready = act.did(A.activation(po.mem[:, :], po.mem[:, :], ACT.Silu))
                        if j < 2:
                            for n, (c0, w) in enumerate(BLOCKS):
                                s, sq = bank[4 + n % 2], e.squares[n % 2]
                                act.wait(ready)
                                sq.guard.wait(act)
                                squared = act.did(A.activation(sq.mem[:, 0:w], po.mem[:, c0:c0 + w], ACT.Square))
                                s.guard.wait(pe)
                                pe.wait(squared)
                                summed = pe.did(T.matmul(s.mem[:, 0:w], ones[:, :], sq.mem[:, 0:w], start=True, stop=True))
                                sq.guard.mark(summed)
                                act.wait(summed)
                                e.stdev.guard.wait(act)
                                rooted = act.did(A.activation(e.stdev.mem[:, 0:w], s.mem[:, 0:w], ACT.Sqrt, bias=e.eps[:, :]))
                                s.guard.mark(rooted)
                                dve.wait(rooted)
                                e.inv.guard.wait(dve)
                                inverted = step(dve, V.reciprocal(e.inv.mem[:, 0:w], e.stdev.mem[:, 0:w]))
                                e.stdev.guard.mark(inverted)
                                normal = dve.did(V.scalar_tensor_tensor(
                                    out=po.mem[:, c0:c0 + w], in0=po.mem[:, c0:c0 + w],
                                    scalar=HD2 ** -0.5 if j == 0 else 1.0, in1=e.inv.mem[:, 0:w],
                                    op0=ALU.mult, op1=ALU.mult))
                                e.inv.guard.mark(normal)
                            ready = normal
                        users = []
                        if j < 2:
                            sp.wait(ready)
                            to = (q_rows, k_cols)[j].rearrange("n q h c -> q n h c")[:, :, bass.ds(i, 1), :]
                            for part_ap, n in places(po.mem):
                                lo, hi = (0, NCT) if n == 0 else (NCT, NT)
                                stored = colsto[j].more(sp, to[:, lo:hi, 0, :], part_ap.rearrange("q (n c) -> q n c", c=P))
                            users.append(stored)
                        if j > 0:
                            tr = turned[j - 1]
                            for g in range(0, NT, 4):
                                b = bank[6 + (g // 4) % 2]
                                m = min(4, NT - g)
                                b.guard.wait(pe)
                                pe.wait(ready)
                                for n in range(m):
                                    at = (g + n) * P + (GAP if g + n >= NCT else 0)
                                    done = T.transpose(b.mem[:, n * P:(n + 1) * P], po.mem[:, at:at + P], ident[:, :])
                                done = pe.did(done)
                                dve.wait(done)
                                if g == 0:
                                    tr.guard.wait(dve)
                                flipped = dve.did(V.tensor_copy(tr.mem[:, g:g + m, :],
                                                                b.mem[:, 0:m * P].rearrange("q (n c) -> q n c", c=P)))
                                b.guard.mark(flipped)
                            users.append(done)
                            sp.wait(flipped)
                            to = (k_rows, v_rows)[j - 1].rearrange("n q h c -> q n h c")[:, :, bass.ds(i, 1), :]
                            tr.guard.mark(tr.more(sp, to[:, :, 0, :], tr.mem[:, :, :]))
                        po.guard.mark(*users)
                e.settle()

            with p.repeat("z_u", H2) as i:
                for j, (c0, dst, func) in enumerate(((COL_Z, zs, ACT.Silu), (COL_U, ya, ACT.Gelu))):
                    tile = ring[j].mem[:, 0:KC * P].rearrange("q (k n) -> q k n", k=KC)
                    here = ring[j].load(sp, tile, by_k[:, :, bass.ds(i * P + c0, P)])
                    pe.wait(here)
                    for h in range(NH):
                        b = bank[j * NH + h]
                        b.guard.wait(pe)
                        for k in range(KC):
                            done = T.matmul(b.mem[:, :], tile[:, k, :], hT[:, k, h * HALF:(h + 1) * HALF],
                                            start=k == 0, stop=k == KC - 1)
                        done = pe.did(done)
                        act.wait(done)
                        b.guard.mark(act.did(A.activation(dst[:, bass.ds(i, 1), h * HALF:(h + 1) * HALF],
                                                          b.mem[:, None, :], func)))
                    ring[j].guard.mark(done)

            with ExitStack() as mlp_mem:
                e.settle()
                ws = Buffer(p, "ws", e.sb("ws", [P, H2, P], mlp_mem), True)
                wsT = e.sb("wsT", [P, H2, P], mlp_mem)
                row = Buffer(p, "mlp_row", e.sb("mlp_row", [1, WIDE], mlp_mem), True)
                vgain = e.sb("vgain", [P, WIDE], mlp_mem)
                tokens = [Buffer(p, f"tokens{n}", e.sb(f"tokens{n}", [P, KC, P], mlp_mem)) for n in range(2)]
                vt = [Buffer(p, f"vt{n}", e.sb(f"vt{n}", [P, WIDE], mlp_mem)) for n in range(2)]
                vstat = e.sb("vstat", [P, 2, 2, H2], mlp_mem)
                here = ws.more(sp, ws.mem[:, :, :], t["gm_ws_2"][0].rearrange("g t s -> t g s"))
                row.more(sp, row.mem[:, :], t["gm_bs_2"][0].rearrange("g (a t) -> a g t", a=1))
                have_row = row.more(sp, vgain[:, :], t["gm_norm_g_2"][0].partition_broadcast(P))
                pe.wait(here)
                for g in range(H2):
                    done = T.transpose(bank[0].mem[:, g * P:(g + 1) * P], ws.mem[:, g, :], ident[:, :])
                dve.wait(pe.did(done))
                have_wsT = dve.did(V.tensor_copy(wsT[:, :, :], bank[0].mem[:, :].rearrange("q (g c) -> q g c", g=H2)))
                bank[0].guard.mark(have_wsT)
                wv = []
                for s in range(2):
                    wv.append(ring[s].mem[:, :].rearrange("q (k n) -> q k n", k=KC))
                    here = ring[s].load(sp, wv[s], by_k[:, :, COL_V + s * WCOL:COL_V + (s + 1) * WCOL])
                    pe.wait(here)
                pe.wait(have_wsT, have_row)
                dve.wait(have_row)
                with p.repeat("mlp", TT // 2) as i:
                    for n in range(2):
                        tk, v, b, mixed = tokens[n], vt[n], bank[2 + n], bank[4 + n]
                        at = bass.ds((2 * i + n) * P, P)
                        tk.guard.wait(dve)
                        copied = dve.did(V.tensor_copy(tk.mem[:, :, :], hT[:, :, at]))
                        pe.wait(copied)
                        b.guard.wait(pe)
                        for s in range(2):
                            for k in range(KC):
                                done = T.matmul(b.mem[:, s * WCOL:(s + 1) * WCOL], tk.mem[:, k, :], wv[s][:, k, :],
                                                start=k == 0, stop=k == KC - 1)
                        done = pe.did(done)
                        tk.guard.mark(done)
                        act.wait(done)
                        v.guard.wait(act)
                        made = act.did(A.activation(v.mem[:, :], b.mem[:, :], ACT.Gelu))
                        b.guard.mark(made)
                        act.wait(made)
                        sq = e.squares[n]
                        sq.guard.wait(act)
                        for g in range(H2):
                            sl = slice(g * P, (g + 1) * P)
                            done = act.did(A.activation(sq.mem[:, sl], v.mem[:, sl], ACT.Square,
                                                        accum_out=vstat[:, n, 0, g:g + 1]))
                        sq.guard.mark(done)
                        act.wait(done)
                        rooted = act.did(A.activation(vstat[:, n, 0, :], vstat[:, n, 0, :], ACT.Sqrt, bias=e.eps[:, :],
                                                      scale=1.0 / P))
                        dve.wait(rooted)
                        step(dve, V.reciprocal(vstat[:, n, 1, :], vstat[:, n, 0, :]))
                        for g in range(H2):
                            sl = slice(g * P, (g + 1) * P)
                            done = dve.did(V.scalar_tensor_tensor(out=v.mem[:, sl], in0=v.mem[:, sl],
                                                                  scalar=vstat[:, n, 1, g:g + 1], in1=vgain[:, sl],
                                                                  op0=ALU.mult, op1=ALU.mult))
                        act.wait(done)
                        pe.wait(done)
                        mixed.guard.wait(pe)
                        for g in range(H2):
                            sl = slice(g * P, (g + 1) * P)
                            T.matmul(mixed.mem[:, sl], ones[0:1, :], row.mem[0:1, sl], start=True, stop=False)
                            done = T.matmul(mixed.mem[:, sl], v.mem[:, sl], wsT[:, g, :], start=False, stop=True)
                        done = pe.did(done)
                        v.guard.mark(done)
                        dve.wait(done)
                        done = dve.did(V.tensor_tensor(ya[:, :, at], ya[:, :, at],
                                                       mixed.mem[:, :].rearrange("q (g c) -> q g c", g=H2), ALU.mult))
                        mixed.guard.mark(done)
                ring[0].guard.mark(pe.last())
                ring[1].guard.mark(pe.last())
                e.settle()

        own_acc = hT[:, 0:4, :].rearrange("q k (a c) -> q (k a) c", a=2)
        o_sum = own_acc.rearrange("q (n) (h c) -> q n h c", h=H2)
        spare = hT[:, 4:8, :].rearrange("q k (a c) -> q (k a) c", a=2)
        delta_rule(e, late, step, dec_in, beta, (q_rows, k_cols, k_rows, v_rows), o_sum, spare, NT, NCT, H2)

        with ExitStack() as gdn_out:
            flat = [Buffer(p, f"flat{n}", e.sb(f"flat{n}", [P, H2, P], gdn_out)) for n in range(2)]
            ostat = e.sb("ostat", [P, 2, 2, H2], gdn_out)
            with p.repeat("gdn_out", TT // 2) as i:
                for n in range(2):
                    fl, b, sq = flat[n], bank[n], e.squares[n]
                    tile = o_sum[:, bass.ds(2 * i + n, 1), :, :].rearrange("q a h c -> q (a h) c")
                    sq.guard.wait(act)
                    for h in range(H2):
                        done = act.did(A.activation(sq.mem[:, h * P:(h + 1) * P], tile[:, h, :], ACT.Square,
                                                    accum_out=ostat[:, n, 0, h:h + 1]))
                    sq.guard.mark(done)
                    act.wait(done)
                    rooted = act.did(A.activation(ostat[:, n, 0, :], ostat[:, n, 0, :], ACT.Sqrt, bias=e.eps[:, :],
                                                  scale=1.0 / P))
                    dve.wait(rooted)
                    inverted = step(dve, V.reciprocal(ostat[:, n, 1, :], ostat[:, n, 0, :]))
                    fl.guard.wait(dve)
                    done = dve.did(V.tensor_tensor(fl.mem[:, :, :], tile, ostat[:, n, 1, :, None].broadcast_to([P, H2, P]),
                                                   ALU.mult))
                    act.wait(done)
                    pe.wait(done)
                    b.guard.wait(pe)
                    for h in range(H2):
                        done = T.transpose(b.mem[:, h * P:(h + 1) * P], fl.mem[:, h, :], ident[:, :])
                    done = pe.did(done)
                    fl.guard.mark(done)
                    dve.wait(done)
                    at = zs[:, :, bass.ds((2 * i + n) * P, P)]
                    done = dve.did(V.scalar_tensor_tensor(out=at, in0=b.mem[:, :].rearrange("q (h c) -> q h c", h=H2),
                                                          scalar=e.col("gdn_norm_g_2"), in1=at,
                                                          op0=ALU.mult, op1=ALU.mult))
                    b.guard.mark(done)
            e.settle()

        def y_cols(k, c):
            return ya[:, k, c] if k < H2 else zs[:, k - H2, c]

        add_product(e, "mix2_out", t["w_out_2"][0], y_cols, done, lambda i, c: mod[:, bass.ds(4 * i + (GT1 + c), 1), 0])
        e.settle()
        late.close()
        experts(e, own, step, out, mod, gains, (SH2, GT2), f_rows, sum_rows, gate_row)


def delta_rule(e, outer_mem, step, dec_in, beta, stores, o_sum, spare, NT, NCT, H2):
    p, nc, t = e.p, e.nc, e.t
    V, A, T, G = nc.vector, nc.scalar, nc.tensor, nc.gpsimd
    pe, act, dve, pool, sp = p.pe, p.act, p.dve, p.pool, p.sp
    bank, ring, ident, ones = e.bank, e.ring, e.ident, e.ones
    W = H2 * P
    LEVELS = [1, 2, 4, 8, 16, 32, 64]
    with ExitStack() as own:
        upto = e.sb("upto", [P, 2, P], own)
        after = e.sb("after", [P, 2, P], own)
        pair = e.sb("pair", [P, 2, len(LEVELS), P], own)

        def select(ap, base, pattern, cm):
            return step(pool, G.affine_select(out=ap, in_=ap, compare_op=ALU.is_ge, fill=0.0, base=base,
                                              pattern=pattern, channel_multiplier=cm))

        G.memset(upto[:, :, :], 1.0)
        G.memset(after[:, :, :], 1.0)
        step(pool, G.memset(pair[:, :, :, :], 0.0))
        select(upto[:, 0, :], 0, [[1, P]], -1)
        select(upto[:, 1, :], 0, [[-1, P]], 1)
        select(after[:, 0, :], -1, [[-1, P]], 1)
        select(after[:, 1, :], -1, [[1, P]], -1)
        for n, b in enumerate(LEVELS):
            blocks = P // (2 * b)
            for side in range(2):
                ap = pair[:, side, n, :].rearrange("q (m s c) -> q m s c", s=2, c=b)[:, :, side, :]
                step(pool, G.memset(ap, 1.0))
                first = b if side == 0 else 0
                select(ap, -first, [[-2 * b, blocks], [0, b]], 1)
                select(ap, first + b - 1, [[2 * b, blocks], [0, b]], -1)
        masks_ready = pool.last()

        spares = iter(range(spare.shape[1]))

        def tile(name, d):
            if d == 0:
                n = next(spares, None)
                if n is not None:
                    return Buffer(p, f"{name}_{d}", spare[:, n, :].rearrange("q (h c) -> q h c", h=H2))
            return Buffer(p, f"{name}_{d}", e.sb(f"{name}_{d}", [P, H2, P], own)[:, :, :])

        names = ("gmask", "decT", "A", "AT", "ATb", "X", "XT", "Y", "bv", "kg", "r", "attT", "S")
        work = [{n: tile(n, d) for n in names} for d in range(2)]
        small = [e.sb(f"small{d}", [P, 6, H2], own) for d in range(2)]
        b4 = lambda m: m.rearrange("q (h c) -> q h c", h=H2)
        SH = [P, H2, P]
        for w in work:
            cleared = dve.did(V.memset(w["S"].mem, 0.0))
        cleared = dve.did(V.memset(o_sum, 0.0))
        dve.wait(cleared, masks_ready)
        pe.wait(cleared, masks_ready)
        pool.wait(cleared)
        act.wait(cleared)

        def load(d, u, tile_at):
            slot = ring[2 * u + d]
            parts = slot.mem[:, :].rearrange("q (a h c) -> q a h c", a=4, h=H2)
            slot.guard.wait(sp)
            for n, s in enumerate(stores):
                here = slot.more(sp, parts[:, n, :, :], s[bass.ds(tile_at, 1), :, :, :].rearrange("a q h c -> (a q) h c"))
            return slot, [parts[:, n, :, :] for n in range(4)], here

        GS, BE, EGC, EGL, ETOT, BEGC = range(6)

        def chunk(d, slot, parts, here, tile_at, out_at):
            w, sm = work[d], small[d]
            B = [bank[4 * d + n] for n in range(4)]
            qT, kT, kr, vr = parts
            sml = lambda n: sm[:, n, :]
            wide = lambda n: sm[:, n, :, None].broadcast_to(SH)
            up = upto[:, d, :]
            aft = after[:, d, :]
            below = lambda n: pair[:, d, n, None, :].broadcast_to(SH)
            above = lambda n: pair[:, 1 - d, n, None, :].broadcast_to(SH)
            small_guard[d].wait(dve)
            dve.did(V.tensor_copy(sml(GS), dec_in[:, bass.ds(tile_at, 1), 4 * d:4 * d + 4].rearrange("q a h -> q (a h)")))
            got = step(dve, V.tensor_copy(sml(BE), beta[:, bass.ds(tile_at, 1), 4 * d:4 * d + 4].rearrange("q a h -> q (a h)")))
            w["gmask"].guard.wait(dve)
            masked = dve.did(V.tensor_tensor(w["gmask"].mem, aft[:, None, :].broadcast_to(SH), wide(GS), ALU.mult))
            pe.wait(got)
            B[0].guard.wait(pe)
            T.matmul(B[0].mem[:, 0:H2], up, sml(GS), start=True, stop=True)
            T.matmul(B[0].mem[:, H2:2 * H2], aft, sml(GS), start=True, stop=True)
            done = pe.did(T.matmul(B[0].mem[:, 2 * H2:3 * H2], ones[:, :], sml(GS), start=True, stop=True))
            act.wait(done)
            small_guard[d].wait(act)
            sums = act.did(A.activation(sm[:, EGC:EGC + 3, :], B[0].mem[:, 0:3 * H2].rearrange("q (a h) -> q a h", a=3), ACT.Exp))
            B[0].guard.mark(sums)
            dve.wait(sums)
            begc = step(dve, V.tensor_tensor(sml(BEGC), sml(BE), sml(EGC), ALU.mult))
            pe.wait(masked)
            B[1].guard.wait(pe)
            for h in range(H2):
                done = T.matmul(B[1].mem[:, h * P:(h + 1) * P], w["gmask"].mem[:, h, :], up, start=True, stop=True)
            done = pe.did(done)
            act.wait(done)
            w["decT"].guard.wait(act)
            decT = act.did(A.activation(w["decT"].mem, b4(B[1].mem[:, :]), ACT.Exp))
            B[1].guard.mark(decT)
            B[2].guard.wait(pe)
            for h in range(H2):
                done = T.matmul(B[2].mem[:, h * P:(h + 1) * P], up, w["gmask"].mem[:, h, :], start=True, stop=True)
            done = pe.did(done)
            w["gmask"].guard.mark(done)
            act.wait(done)
            w["A"].guard.wait(act)
            dec = act.did(A.activation(w["A"].mem, b4(B[2].mem[:, :]), ACT.Exp))
            B[2].guard.mark(dec)
            pool.wait(decT)
            decT = pool.did(G.tensor_tensor(w["decT"].mem, w["decT"].mem, up[:, None, :].broadcast_to(SH), ALU.mult))
            yield
            pe.wait(here)
            B[3].guard.wait(pe)
            for h in range(H2):
                done = T.matmul(B[3].mem[:, h * P:(h + 1) * P], kT[:, h, :], kT[:, h, :], start=True, stop=True)
            kk = pe.did(done)
            B[0].guard.wait(pe)
            for h in range(H2):
                done = T.matmul(B[0].mem[:, h * P:(h + 1) * P], kT[:, h, :], qT[:, h, :], start=True, stop=True)
            kq = pe.did(done)
            dve.wait(kk, dec)
            done = dve.did(V.tensor_tensor(w["A"].mem, b4(B[3].mem[:, :]), w["A"].mem, ALU.mult))
            B[3].guard.mark(done)
            dve.wait(done)
            a_ready = dve.did(V.tensor_tensor(w["A"].mem, w["A"].mem, wide(BE), ALU.mult))
            pe.wait(a_ready)
            B[1].guard.wait(pe)
            for h in range(H2):
                done = T.transpose(B[1].mem[:, h * P:(h + 1) * P], w["A"].mem[:, h, :], ident[:, :])
            done = pe.did(done)
            act.wait(done)
            w["AT"].guard.wait(act)
            at_ready = act.did(A.activation(w["AT"].mem, b4(B[1].mem[:, :]), ACT.Copy))
            B[1].guard.mark(at_ready)
            dve.wait(kq, decT)
            w["attT"].guard.wait(dve)
            att = dve.did(V.tensor_tensor(w["attT"].mem, b4(B[0].mem[:, :]), w["decT"].mem, ALU.mult))
            B[0].guard.mark(att)
            w["decT"].guard.mark(att)
            pool.wait(here, sums, got)
            w["bv"].guard.wait(pool)
            bv = pool.did(G.tensor_tensor(w["bv"].mem, vr, wide(BE), ALU.mult))
            w["kg"].guard.wait(pool)
            kg = pool.did(G.tensor_tensor(w["kg"].mem, kr, wide(EGL), ALU.mult))
            yield
            w["X"].guard.wait(dve)
            w["XT"].guard.wait(dve)
            eye = ident[:, None, :].broadcast_to(SH)
            step(dve, V.tensor_tensor(w["X"].mem, w["A"].mem, below(0), ALU.mult))
            x = dve.did(V.tensor_tensor(w["X"].mem, eye, w["X"].mem, ALU.subtract))
            dve.wait(at_ready)
            w["A"].guard.mark(x, at_ready)
            step(dve, V.tensor_tensor(w["XT"].mem, w["AT"].mem, above(0), ALU.mult))
            xt = dve.did(V.tensor_tensor(w["XT"].mem, eye, w["XT"].mem, ALU.subtract))
            for n in range(1, len(LEVELS)):
                last = n == len(LEVELS) - 1
                pool.wait(at_ready)
                w["ATb"].guard.wait(pool)
                atb = pool.did(G.tensor_tensor(w["ATb"].mem, w["AT"].mem, above(n), ALU.mult))
                pe.wait(atb, x)
                B[1].guard.wait(pe)
                for h in range(H2):
                    done = T.matmul(B[1].mem[:, h * P:(h + 1) * P], w["ATb"].mem[:, h, :], w["X"].mem[:, h, :],
                                    start=True, stop=True)
                done = pe.did(done)
                w["ATb"].guard.mark(done)
                act.wait(done)
                w["Y"].guard.wait(act)
                y = act.did(A.activation(w["Y"].mem, b4(B[1].mem[:, :]), ACT.Copy))
                B[1].guard.mark(y)
                pe.wait(y, xt)
                B[3].guard.wait(pe)
                for h in range(H2):
                    done = T.matmul(B[3].mem[:, h * P:(h + 1) * P], w["Y"].mem[:, h, :], w["XT"].mem[:, h, :],
                                    start=True, stop=True)
                zt = pe.did(done)
                if not last:
                    B[2].guard.wait(pe)
                    for h in range(H2):
                        done = T.matmul(B[2].mem[:, h * P:(h + 1) * P], w["XT"].mem[:, h, :], w["Y"].mem[:, h, :],
                                        start=True, stop=True)
                    z = pe.did(done)
                    dve.wait(z)
                    x = dve.did(V.tensor_tensor(w["X"].mem, w["X"].mem, b4(B[2].mem[:, :]), ALU.subtract))
                    B[2].guard.mark(x)
                else:
                    z = zt
                    w["X"].guard.mark(zt)
                w["Y"].guard.mark(z)
                dve.wait(zt, z)
                xt = dve.did(V.tensor_tensor(w["XT"].mem, w["XT"].mem, b4(B[3].mem[:, :]), ALU.subtract))
                B[3].guard.mark(xt)
                yield
            w["AT"].guard.mark(atb)
            pe.wait(here)
            w["S"].guard.wait(pe)
            B[2].guard.wait(pe)
            for h in range(H2):
                done = T.matmul(B[2].mem[:, h * P:(h + 1) * P], kT[:, h, :], w["S"].mem[:, h, :], start=True, stop=True)
            ks = pe.did(done)
            dve.wait(ks, begc, bv)
            w["r"].guard.wait(dve)
            done = step(dve, V.tensor_tensor(w["r"].mem, b4(B[2].mem[:, :]), wide(BEGC), ALU.mult))
            B[2].guard.mark(done)
            r = dve.did(V.tensor_tensor(w["r"].mem, w["bv"].mem, w["r"].mem, ALU.subtract))
            w["bv"].guard.mark(r)
            if out_at is not None:
                B[0].guard.wait(pe)
                for h in range(H2):
                    done = T.matmul(B[0].mem[:, h * P:(h + 1) * P], qT[:, h, :], w["S"].mem[:, h, :], start=True, stop=True)
                qs = pe.did(done)
            pe.wait(r, xt)
            B[1].guard.wait(pe)
            for h in range(H2):
                done = T.matmul(B[1].mem[:, h * P:(h + 1) * P], w["XT"].mem[:, h, :], w["r"].mem[:, h, :], start=True, stop=True)
            done = pe.did(done)
            w["XT"].guard.mark(done)
            act.wait(done)
            w["Y"].guard.wait(act)
            vn = act.did(A.activation(w["Y"].mem, b4(B[1].mem[:, :]), ACT.Copy))
            B[1].guard.mark(vn)
            yield
            pe.wait(vn, kg)
            B[3].guard.wait(pe)
            for h in range(H2):
                done = T.matmul(B[3].mem[:, h * P:(h + 1) * P], w["kg"].mem[:, h, :], w["Y"].mem[:, h, :], start=True, stop=True)
            ds = pe.did(done)
            w["kg"].guard.mark(ds)
            dve.wait(ds)
            step(dve, V.tensor_tensor(w["S"].mem, w["S"].mem, wide(ETOT), ALU.mult))
            s_new = dve.did(V.tensor_tensor(w["S"].mem, w["S"].mem, b4(B[3].mem[:, :]), ALU.add))
            w["S"].guard.mark(s_new)
            B[3].guard.mark(s_new)
            if out_at is None:
                slot.guard.mark(ds, kg)
                w["Y"].guard.mark(ds)
                w["r"].guard.mark(ds)
                w["attT"].guard.mark(ds)
                small_guard[d].mark(s_new, kg)
                return
            pe.wait(att)
            B[2].guard.wait(pe)
            for h in range(H2):
                done = T.matmul(B[2].mem[:, h * P:(h + 1) * P], w["attT"].mem[:, h, :], w["Y"].mem[:, h, :], start=True, stop=True)
            av = pe.did(done)
            w["Y"].guard.mark(av)
            w["attT"].guard.mark(av)
            slot.guard.mark(av, kg)
            dve.wait(qs)
            done = step(dve, V.tensor_tensor(w["r"].mem, b4(B[0].mem[:, :]), wide(EGC), ALU.mult))
            B[0].guard.mark(done)
            small_guard[d].mark(done, kg)
            dve.wait(av)
            done = dve.did(V.tensor_tensor(w["r"].mem, w["r"].mem, b4(B[2].mem[:, :]), ALU.add))
            B[2].guard.mark(done)
            dve.wait(done)
            o_guard.wait(dve)
            at = o_sum[:, bass.ds(out_at, 1), :, :].rearrange("q a h c -> q (a h) c")
            done = step(dve, V.tensor_tensor(at, at, w["r"].mem, ALU.add))
            o_guard.mark(done)
            w["r"].guard.mark(done)

        small_guard = [Guard(p, f"small{d}") for d in range(2)]
        o_guard = Guard(p, "o_sum")
        o_guard.mark(cleared)

        def both(u, forward, backward, outs):
            loads = [load(d, u, at) for d, at in enumerate((forward, backward))]
            runs = [chunk(d, *loads[d], at, outs[d]) for d, at in enumerate((forward, backward))]
            while runs:
                for g in list(runs):
                    if next(g, "over") == "over":
                        runs.remove(g)

        for s in range(NCT):
            both(s % 2, s, NCT - 1 - s, (None, None))
        with p.repeat("delta", (NT - NCT) // 2) as i:
            for u in range(2):
                both(u, 2 * i + (NCT + u), i * -2 + (NT - 1 - u), (2 * i + u, i * -2 + (NT - NCT - 1 - u)))
        e.settle()


def experts(e, own, step, out, mod, gains, rows_of_mod, f_rows, sum_rows, gate_row):
    p, nc, t = e.p, e.nc, e.t
    V, A, T, G = nc.vector, nc.scalar, nc.tensor, nc.gpsimd
    pe, act, dve, pool, sp = p.pe, p.act, p.dve, p.pool, p.sp
    bank, ring, hT, xT, ident, ones = e.bank, e.ring, e.hT, e.xT, e.ident, e.ones
    SEQ, KC, HALF, TT, D = e.SEQ, e.KC, e.HALF, e.TT, e.D
    SH2, GT2 = rows_of_mod
    NE = t["w_router_2"].shape[2]
    CAP = 2 * SEQ // NE
    FX = t["w_gate_2"].shape[3]
    assert CAP == P and FX == D

    e.rms(e.at_x, e.at_h, lambda k: gains[:, 2, k:k + 1], e.HALVES, shift=lambda k: mod[:, SH2 + k, 0:1])
    e.settle()
    e.turn_out(f_rows, "turn_f", hT)
    e.turn_out(sum_rows, "turn_sum", xT)

    picks = e.sb("picks", [P, 2, NE + 1], own)
    gate2 = e.sb("gate2", [P, D], own)
    with ExitStack() as route:
        gcols = e.sb("gcols", [KC, P], route)
        lines = Buffer(p, "gate_lines", None, True)
        pe.wait(dve.last())
        done = pe.did(T.transpose(bank[7].mem[0:KC, 0:P], mod[:, GT2:GT2 + KC, 0], ident[:, :]))
        dve.wait(done)
        flat = dve.did(V.tensor_copy(gcols[:, :], bank[7].mem[0:KC, 0:P]))
        bank[7].guard.mark(flat)
        act.wait(flat)
        stored = lines.more(act, gate_row.rearrange("(k q) -> k q", q=P), gcols[:, :])
        act.wait(stored)
        have_gate2 = lines.more(act, gate2[:, :], gate_row.partition_broadcast(P))
        wr = Buffer(p, "wr", e.sb("wr", [P, KC, NE], route), True)
        br = e.sb("br", [P, NE], route)
        aff = e.sb("aff", [P, TT, NE], route)
        peak = e.sb("peak", [P, 2, TT], route)
        wr.more(act, wr.mem[:, :, :], t["w_router_2"][0].rearrange("(k q) n -> q k n", q=P))
        here = wr.more(act, br[:, :], t["b_router_2"][0].partition_broadcast(P))
        pe.wait(here)
        bank[6].guard.wait(pe)
        for n in range(TT):
            for k in range(KC):
                done = T.matmul(bank[6].mem[:, NE * n:NE * n + NE], hT[:, k, n * P:(n + 1) * P], wr.mem[:, k, :],
                                start=k == 0, stop=k == KC - 1)
        done = pe.did(done)
        dve.wait(done, here)
        S3 = [P, TT, NE]
        done = step(dve, V.tensor_tensor(aff[:, :, :], bank[6].mem[:, 0:NE * TT].rearrange("q (n c) -> q n c", n=TT),
                                         br[:, None, :].broadcast_to(S3), ALU.add))
        bank[6].guard.mark(done)
        step(dve, V.tensor_reduce(peak[:, 0, :], aff[:, :, :], AX.X, ALU.max))
        done = step(dve, V.tensor_tensor(aff[:, :, :], aff[:, :, :], peak[:, 0, :, None].broadcast_to(S3), ALU.subtract))
        act.wait(done)
        raised = act.did(A.activation(aff[:, :, :], aff[:, :, :], ACT.Exp))
        dve.wait(raised)
        step(dve, V.tensor_reduce(peak[:, 1, :], aff[:, :, :], AX.X, ALU.add))
        step(dve, V.reciprocal(peak[:, 1, :], peak[:, 1, :]))
        done = step(dve, V.tensor_tensor(aff[:, :, :], aff[:, :, :], peak[:, 1, :, None].broadcast_to(S3), ALU.mult))
        affT = e.sb("affT", [NE, SEQ], route)
        top = e.sb("top", [NE, 8], route)
        top_at = e.sb("top_at", [NE, 8], route, mybir.dt.uint32)
        chosen = e.sb("chosen", [NE, 2, CAP], route)
        pe.wait(done)
        for h in range(2):
            b = bank[h]
            b.guard.wait(pe)
            for n in range(4):
                done = T.transpose(b.mem[0:NE, n * P:(n + 1) * P], aff[:, 4 * h + n, :], ident[:, :])
            done = pe.did(done)
            dve.wait(done)
            b.guard.mark(step(dve, V.tensor_copy(affT[:, h * HALF:(h + 1) * HALF], b.mem[0:NE, :])))
        with p.repeat("choose", CAP // 8) as i:
            step(dve, V.max(top[:, :], affT[:, :]))
            step(dve, V.max_index(top_at[:, :], top[:, :], affT[:, :]))
            V.tensor_copy(chosen[:, 0, bass.ds(i * 8, 8)], top[:, :])
            V.tensor_copy(chosen[:, 1, bass.ds(i * 8, 8)], top_at[:, :])
            done = step(dve, V.match_replace(affT[:, :], top[:, :], affT[:, :], -1.0))
        dve.wait(done)
        pe.wait(done)
        bank[7].guard.wait(pe)
        T.transpose(bank[7].mem[:, 0:NE], chosen[:, 0, :], ident[0:NE, 0:NE])
        done = pe.did(T.transpose(bank[7].mem[:, NE:2 * NE], chosen[:, 1, :], ident[0:NE, 0:NE]))
        dve.wait(done)
        step(dve, V.memset(picks[:, :, :], 0.0))
        picked = dve.did(V.tensor_copy(picks[:, :, 0:NE], bank[7].mem[:, 0:2 * NE].rearrange("q (a n) -> q a n", a=2)))
        bank[7].guard.mark(picked)
        dve.wait(picked)
        e.settle()

    with ExitStack() as mem:
        more = [Buffer(p, f"more{n}", e.sb(f"more{n}", [P, 2 * D], mem), loads=True) for n in range(8)]
        slots = ring + more
        p.barrier(sp)
        index = [e.sb(f"index{n}", [P, 1], mem, mybir.dt.int32) for n in range(2)]
        xe = Buffer(p, "xe", e.sb("xe", [P, D], mem), True, head=0)
        xeT = Buffer(p, "xeT", e.sb("xeT", [P, KC, P], mem))
        hid = Buffer(p, "hid", e.sb("hid", [P, FX], mem))
        hidT = Buffer(p, "hidT", e.sb("hidT", [P, KC, P], mem))
        ye = Buffer(p, "ye", e.sb("ye", [P, D], mem), True, head=0)
        ahead = Guard(p, "index_ahead")
        NU = KC // 2
        index_ap = lambda ap: bass.IndirectOffsetOnAxis(ap=ap, axis=0)

        def gather(which):
            pool.wait(which)
            xe.guard.wait(pool)
            return xe.loads.did(G.indirect_dma_start(out=xe.mem[:, :], out_offset=None, in_=f_rows,
                                                     in_offset=index_ap(index[1][:, :])))

        def turn8(src, dst, ready):
            for g in range(2):
                b = bank[6 + g]
                b.guard.wait(pe)
                pe.wait(*ready)
                for k in range(4):
                    done = T.transpose(b.mem[:, k * P:(k + 1) * P], src.mem[:, (4 * g + k) * P:(4 * g + k + 1) * P],
                                       ident[:, :])
                done = pe.did(done)
                act.wait(done)
                if g == 0:
                    dst.guard.wait(act)
                copied = act.did(A.activation(dst.mem[:, 4 * g:4 * g + 4, :],
                                              b.mem[:, :].rearrange("q (k c) -> q k c", k=4), ACT.Copy))
                b.guard.mark(copied)
            src.guard.mark(done)
            return copied

        first = dve.did(V.tensor_copy(index[1][:, :], picks[:, 1, 0:1]))
        gathered = gather(first)
        xeT_ready = turn8(xe, xeT, [gathered])
        xeT_made = Guard(p, "xeT_made")
        xeT_made.mark(xeT_ready)
        ahead.mark(gathered)
        dve.wait(have_gate2)
        pool.wait(have_gate2)
        ye.guard.mark(ye.loads.did(G.dma_start(ye.mem[0:1, :], gate_row.rearrange("(a n) -> a n", a=1))))
        weights = [t[n][0].rearrange("x (u a q) n -> u q x a n", q=P, a=2) for n in ("w_gate_2", "w_up_2", "w_down_2")]
        with p.repeat("experts", NE) as i:
            landed = []
            for m in range(3):
                for u in range(NU):
                    slot = slots[m * NU + u]
                    tile = slot.mem[:, :].rearrange("q (a n) -> q a n", a=2)
                    here = slot.load(sp, tile, weights[m][u][:, bass.ds(i, 1), :, :].rearrange("q x a n -> q (x a) n"))
                    landed.append((slot, tile, here))
            ye.guard.wait(dve)
            now = dve.did(V.tensor_copy(index[0][:, :], picks[:, 1, bass.ds(i, 1)]))
            ahead.wait(dve)
            following = dve.did(V.tensor_copy(index[1][:, :], picks[:, 1, bass.ds(i + 1, 1)]))
            gathered = gather(following)
            ahead.mark(gathered)

            def product(m, lhs, banks):
                for b in banks:
                    b.guard.wait(pe)
                for u in range(NU):
                    slot, tile, here = landed[m * NU + u]
                    pe.wait(here)
                    for a in range(2):
                        k = 2 * u + a
                        for h, b in enumerate(banks):
                            done = T.matmul(b.mem[:, :], lhs.mem[:, k, :], tile[:, a, h * HALF:(h + 1) * HALF],
                                            start=k == 0, stop=k == KC - 1)
                    done = pe.did(done)
                    slot.guard.mark(done)
                return done

            xeT_made.wait(pe)
            gate_done = product(0, xeT, bank[0:2])
            hid.guard.wait(act)
            act.wait(gate_done)
            for h in range(2):
                gated = act.did(A.activation(hid.mem[:, h * HALF:(h + 1) * HALF], bank[h].mem[:, :], ACT.Silu))
                bank[h].guard.mark(gated)
            up_done = product(1, xeT, bank[2:4])
            xeT.guard.mark(up_done)
            dve.wait(gated, up_done)
            for h in range(2):
                sl = slice(h * HALF, (h + 1) * HALF)
                made = dve.did(V.tensor_tensor(hid.mem[:, sl], hid.mem[:, sl], bank[2 + h].mem[:, :], ALU.mult))
                bank[2 + h].guard.mark(made)
            xeT_ready = turn8(xe, xeT, [gathered])
            xeT_made.mark(xeT_ready)
            hidT_ready = turn8(hid, hidT, [made])
            pe.wait(hidT_ready)
            down_done = product(2, hidT, bank[4:6])
            hidT.guard.mark(down_done)
            dve.wait(down_done)
            for h in range(2):
                sl = slice(h * HALF, (h + 1) * HALF)
                scaled = dve.did(V.scalar_tensor_tensor(out=ye.mem[:, sl], in0=bank[4 + h].mem[:, :],
                                                        scalar=picks[:, 0, bass.ds(i, 1)], in1=gate2[:, sl],
                                                        op0=ALU.mult, op1=ALU.mult))
                bank[4 + h].guard.mark(scaled)
            pool.wait(scaled, now)
            ye.guard.wait(pool)
            ye.guard.mark(ye.loads.did(G.indirect_dma_start(out=sum_rows, out_offset=index_ap(index[0][:, :]),
                                                            in_=ye.mem[:, :], in_offset=None, compute_op=ALU.add)))
        e.settle()
    with ExitStack() as mem:
        fgain = Buffer(p, "fgain", e.sb("fgain", [P, D], mem), True)
        lines = [Buffer(p, f"sum{n}", e.sb(f"sum{n}", [P, D], mem), True) for n in range(2)]
        squared = [Buffer(p, f"sqr{n}", e.sb(f"sqr{n}", [P, D], mem)) for n in range(2)]
        done_rows = [Buffer(p, f"fin{n}", e.sb(f"fin{n}", [P, D], mem), True) for n in range(2)]
        fstat = e.sb("fstat", [P, 2, 2], mem)
        p.barrier(sp)
        have_gain = fgain.more(sp, fgain.mem[:, :], t["final_norm_g_2"].partition_broadcast(P))
        dve.wait(have_gain)
        src = sum_rows.rearrange("(n q) d -> q n d", q=P)
        dst = out[0].rearrange("(n q) d -> q n d", q=P)
        with p.repeat("last_norm", TT // 2) as i:
            for n in range(2):
                line, sq, fin = lines[n], squared[n], done_rows[n]
                here = line.load(sp, line.mem[:, None, :], src[:, bass.ds(2 * i + n, 1), :])
                act.wait(here)
                sq.guard.wait(act)
                summed = act.did(A.activation(sq.mem[:, :], line.mem[:, :], ACT.Square, accum_out=fstat[:, n, 0:1]))
                act.wait(summed)
                rooted = act.did(A.activation(fstat[:, n, 0:1], fstat[:, n, 0:1], ACT.Sqrt, bias=e.eps[:, :], scale=1.0 / D))
                dve.wait(rooted)
                step(dve, V.reciprocal(fstat[:, n, 1:2], fstat[:, n, 0:1]))
                fin.guard.wait(dve)
                normed = dve.did(V.scalar_tensor_tensor(out=fin.mem[:, :], in0=line.mem[:, :], scalar=fstat[:, n, 1:2],
                                                        in1=fgain.mem[:, :], op0=ALU.mult, op1=ALU.mult))
                line.guard.mark(normed)
                sq.guard.mark(normed)
                act.wait(normed)
                fin.guard.mark(fin.more(act, dst[:, bass.ds(2 * i + n, 1), :], fin.mem[:, None, :]))


NAMES = ["x", "norm_ffn1", "w_ffn1_gu", "w_ffn1_down", "norm_mix", "w_in", "conv_w", "conv_b", "lru_w_gates",
         "lru_b_gates", "lru_lambda", "q_norm", "k_norm", "rel_pos_bias", "w_out", "norm_ffn2", "w_ffn2_gu",
         "w_ffn2_down", "c_2", "ctx_2", "c_ctx_2", "w_mod_2", "b_mod_2", "norm1_g_2", "norm2_g_2", "w_in_2",
         "conv_w_2", "a_log_2", "dt_bias_2", "gdn_norm_g_2", "gm_norm_g_2", "gm_ws_2", "gm_bs_2", "w_out_2",
         "w_router_2", "b_router_2", "w_gate_2", "w_up_2", "w_down_2", "final_norm_g_2"]


def kernel(**inputs):
    import concourse.bacc as bacc
    from concourse.bass_utils import run_bass_kernel_spmd

    arrays = {n: np.ascontiguousarray(inputs[n]) for n in NAMES}

    def program(plan):
        nc = bacc.Bacc("TRN2", target_bir_lowering=False, num_devices=1)
        t = {n: nc.dram_tensor("in_" + n, a.shape, F32, kind="ExternalInput").ap() for n, a in arrays.items()}
        out = nc.dram_tensor("out_0", t["x"].shape, F32, kind="ExternalOutput").ap()
        return nc, build(nc, plan, t, out)

    _, plan = program(({}, {}))
    nc, _ = program(plan)
    r = run_bass_kernel_spmd(nc, [{"in_" + n: a for n, a in arrays.items()}], core_ids=[0])
    return r.results[0]["out_0"]
```

```python
from contextlib import ExitStack, contextmanager

import numpy as np
import concourse.bass as bass
from concourse import mybir

P = 128
F32 = mybir.dt.float32
ALU = mybir.AluOpType
ACT = mybir.ActivationFunctionType
AX = mybir.AxisListType

HEAD = 4096


class Done:

    def __init__(self, counter, loop, at):
        self.counter, self.loop, self.at = counter, loop, at


class Loop:
    def __init__(self, name, passes, index):
        self.name, self.passes, self.index = name, passes, index


class Counter:

    def __init__(self, program, name, eng=None, by=1, head=HEAD):
        self.program, self.name, self.eng, self.by = program, name, eng, by
        self.sem = program.ctx.enter_context(program.nc.semaphore(name))
        self.base, self.here = head, 0
        self.head = head
        self.ended = {}
        if eng:
            self.waited = self.program.ctx.enter_context(program.nc.semaphore(name + "_waited"))
        program.counters.append(self)
        if head:
            program.nc.sync.sem_inc(self.sem, head)
        if program.loop:
            raise ValueError("a counter is made outside the loops")

    def did(self, instruction):
        instruction.then_inc(self.sem, self.by)
        self.here += self.by
        return self.last()

    def last(self):
        loop = self.program.loop
        return Done(self, loop, self.here if loop else self.base + self.here)

    def value(self, done, back):
        loop = self.program.loop
        if done.loop is None:
            return done.at
        if done.loop is loop:
            per = self.program.per_pass(loop.name, self.name)
            return loop.index * per + (self.base + done.at - back * per)
        base, per, passes = self.ended[done.loop.name]
        return base + per * (passes - 1) + done.at

    def wait(self, *dones, back=0):
        for done in dones:
            self.eng.wait_ge(done.counter.sem, done.counter.value(done, back))
            if done.loop and done.loop is self.program.loop:
                self.eng.sem_inc(self.waited, 1)


class Guard:

    def __init__(self, program, name):
        self.program, self.name = program, name
        self.marks = []

    def mark(self, *dones):
        self.marks = list(dones)
        if self.program.loop:
            self.program.carried[(self.program.loop.name, self.name)] = [
                (d.counter.name, d.at) for d in dones]

    def wait(self, engine):
        loop = self.program.loop
        engine.wait(*self.marks)
        if loop and not any(d.loop is loop for d in self.marks):
            for name, at in self.program.plan_carried.get((loop.name, self.name), []):
                counter = self.program.named(name)
                engine.wait(Done(counter, loop, at), back=1)


class Program:
    def __init__(self, nc, ctx, plan):
        self.nc, self.ctx = nc, ctx
        self.counters = []
        self.loop = None
        self.plan_counts, self.plan_carried = plan
        self.counts, self.carried = {}, {}
        self.pe = Counter(self, "pe_done", nc.tensor)
        self.act = Counter(self, "act_done", nc.scalar)
        self.dve = Counter(self, "dve_done", nc.vector)
        self.pool = Counter(self, "pool_done", nc.gpsimd)
        self.sp = Counter(self, "sp_done", nc.sync)
        self.compute = [self.pe, self.act, self.dve, self.pool]

    def named(self, name):
        return next(c for c in self.counters if c.name == name)

    def per_pass(self, loop, counter):
        return self.plan_counts.get((loop, counter), 1)

    @contextmanager
    def repeat(self, name, passes):
        for c in self.counters:
            c.base, c.here = c.base + c.here, 0
        with self.nc.Fori(0, passes) as index:
            self.loop = Loop(name, passes, index)
            yield index
            self.loop = None
        for c in self.counters:
            self.counts[(name, c.name)] = c.here
            c.ended[name] = (c.base, c.here, passes)
            c.base, c.here = c.base + c.here * passes, 0

    def barrier(self, *engines):
        for e in engines or self.compute:
            for c in self.counters:
                if c.base + c.here > c.head:
                    e.wait(c.last())


class Buffer:

    def __init__(self, program, name, mem, loads=False, head=HEAD):
        self.mem = mem
        self.guard = Guard(program, name)
        self.loads = Counter(program, name + "_in", by=16, head=head) if loads else None

    def load(self, engine, dst, src):
        self.guard.wait(engine)
        return self.loads.did(engine.eng.dma_start(dst, src))

    def more(self, engine, dst, src):
        return self.loads.did(engine.eng.dma_start(dst, src))


class Shared:
    pass


def build(nc, plan, t, out):
    with ExitStack() as ctx:
        p = Program(nc, ctx, plan)
        V, A, T, G = nc.vector, nc.scalar, nc.tensor, nc.gpsimd
        pe, act, dve, pool, sp = p.pe, p.act, p.dve, p.pool, p.sp

        def sb(name, shape, where=ctx, dt=F32):
            return where.enter_context(nc.sbuf_tensor(name, shape, dt))

        SEQ, D = t["x"].shape[1], t["x"].shape[2]
        KC = D // P
        TT = SEQ // P
        HALF = 512
        NH = SEQ // HALF
        CTX = t["ctx_2"].shape[1]
        ALL = CTX + SEQ
        FF = t["w_ffn1_down"].shape[1]
        EPS = 1e-6

        bank = [Buffer(p, f"bank{n}", ctx.enter_context(nc.psum_tensor(f"bank{n}", [P, 512], F32)))
                for n in range(8)]
        xT = sb("xT", [P, KC, SEQ])
        hT = sb("hT", [P, KC, SEQ])
        WCOL = 256
        ring = [Buffer(p, f"ring{n}", sb(f"ring{n}", [P, KC * WCOL]), loads=True) for n in range(4)]
        ident = sb("ident", [P, P])
        ones = sb("ones", [P, P])
        ones64 = sb("ones64", [P, P])
        eps = sb("eps", [P, 1])
        squares = [Buffer(p, f"squares{n}", sb(f"squares{n}", [P, HALF])) for n in range(2)]
        inv = Buffer(p, "inv", sb("inv", [P, HALF]))
        stdev = Buffer(p, "stdev", sb("stdev", [P, HALF]))
        temps = [Buffer(p, f"temp{n}", sb(f"temp{n}", [P, HALF])) for n in range(2)]
        PACK_A = ["norm_ffn1", "norm_mix", "norm_ffn2", "conv_b", "conv_w", "lru_b_gates", "lru_lambda"]
        PACK_B = ["norm1_g_2", "norm2_g_2", "conv_w_2", "gdn_norm_g_2", "c_2", "c_ctx_2", "b_mod_2"]
        packs = [Buffer(p, f"pack{n}", None, loads=True) for n in range(2)]
        cols = [sb(f"cols{n}", [P, P]) for n in range(2)]
        column = {}
        stream = {n: Counter(p, n, by=16) for n in ("bias_in", "gates_in", "shift_in", "scratch_out")}

        skew = nc.dram_tensor("skew", [240, 64, P], F32, kind="Internal").ap()

        zeroed = pool.did(G.memset(ident[:, :], 0.0))
        pool.wait(zeroed)
        have_ident = pool.did(G.affine_select(out=ident[:, :], in_=ident[:, :], compare_op=ALU.not_equal, fill=1.0,
                                              base=0, pattern=[[-1, P]], channel_multiplier=1))
        V.memset(ones[:, :], 1.0)
        V.memset(eps[:, :], EPS)
        have_zero64 = dve.did(V.memset(ones64[:, :], 0.0))
        dve.wait(have_zero64)
        V.memset(ones64[0:64, 0:64], 1.0)
        have_ones = dve.did(V.memset(ones64[64:P, 64:P], 1.0))

        with ExitStack() as own:
            for n, names in enumerate((PACK_A, PACK_B)):
                rows = sb(f"rows{n}", [P, P], own)
                cleared = pool.did(G.memset(rows[:, :], 0.0))
                sp.wait(cleared)
                at = 0
                for name in names:
                    src = t[name]
                    flat = src if len(src.shape) == 1 else src.rearrange(
                        {2: "a b -> (a b)", 3: "a b c -> (a b c)", 4: "a b c d -> (a b c d)"}[len(src.shape)])
                    k = flat.shape[0] // P
                    loaded = packs[n].more(sp, rows[at:at + k, :], flat.rearrange("(k q) -> k q", q=P))
                    column[name] = (n, at)
                    at += k
                if n == 1:
                    for name in ("q_norm", "k_norm"):
                        for h in range(2):
                            loaded = packs[n].more(sp, rows[at:at + 1, h * 64:h * 64 + 64], t[name])
                        column[name] = (n, at)
                        at += 1
                pe.wait(loaded, have_ident, have_ones)
                turned = pe.did(T.transpose(bank[n].mem[:, 0:P], rows[:, :], ident[:, :]))
                dve.wait(turned)
                have_cols = dve.did(V.tensor_copy(cols[n][:, :], bank[n].mem[:, 0:P]))
                bank[n].guard.mark(have_cols)

            def col(name, k=0, n=1):
                which, at = column[name]
                return cols[which][:, at + k:at + k + n]

        def evacuate(n, dst, src):
            if n % 2:
                return act.did(A.activation(dst, src, ACT.Copy))
            return dve.did(V.tensor_copy(dst, src))

        def turn_in(src, dst, n_tiles, name, tiles_a_pass):
            rows = src.rearrange("(n q) d -> q n d", q=P)
            with p.repeat(name, n_tiles // tiles_a_pass) as i:
                for s in range(tiles_a_pass // 2):
                    slot = ring[s]
                    tiles = slot.mem[:, :].rearrange("q (n d) -> q n d", n=2)
                    here = slot.load(sp, tiles, rows[:, bass.ds(i * tiles_a_pass + 2 * s, 2), :])
                    for n in range(2):
                        for g in range(2):
                            b = bank[4 * s + 2 * n + g]
                            pe.wait(here)
                            b.guard.wait(pe)
                            for k in range(4):
                                done = T.transpose(b.mem[:, k * P:(k + 1) * P],
                                                   tiles[:, n, (4 * g + k) * P:(4 * g + k + 1) * P], ident[:, :])
                            done = pe.did(done)
                            (act if g else dve).wait(done)
                            out_ap = dst(i * tiles_a_pass + 2 * s + n, 4 * g)
                            b.guard.mark(evacuate(g, out_ap, b.mem[:, :].rearrange("q (k c) -> q k c", k=4)))
                    slot.guard.mark(done)

        turn_in(t["x"][0], lambda n, k: xT[:, k:k + 4, bass.ds(n * P, P)], TT, "turn_x", 4)

        def settle(*engines):
            p.barrier(*engines)

        def rms(src, dst, gain, blocks, shift=None, ready=()):
            finals = []
            for n, (c0, w) in enumerate(blocks):
                b = bank[n % 2]
                b.guard.wait(pe)
                for k in range(KC):
                    sq = squares[k % 2]
                    sq.guard.wait(act)
                    act.wait(*ready)
                    squared = act.did(A.activation(sq.mem[:, 0:w], src(c0, w, k), ACT.Square))
                    pe.wait(squared)
                    summed = pe.did(T.matmul(b.mem[:, 0:w], ones[:, :], sq.mem[:, 0:w], start=k == 0, stop=k == KC - 1))
                    sq.guard.mark(summed)
                act.wait(summed)
                stdev.guard.wait(act)
                rooted = act.did(A.activation(stdev.mem[:, 0:w], b.mem[:, 0:w], ACT.Sqrt, bias=eps[:, :],
                                              scale=1.0 / D))
                b.guard.mark(rooted)
                dve.wait(rooted, *ready)
                inv.guard.wait(dve)
                inverted = dve.did(V.reciprocal(inv.mem[:, 0:w], stdev.mem[:, 0:w]))
                stdev.guard.mark(inverted)
                dve.wait(inverted)
                for k in range(KC):
                    done = dve.did(V.scalar_tensor_tensor(out=dst(c0, w, k), in0=src(c0, w, k), scalar=gain(k),
                                                          in1=inv.mem[:, 0:w], op0=ALU.mult, op1=ALU.mult))
                    if shift is not None:
                        act.wait(done)
                        moved = act.did(A.activation(dst(c0, w, k), dst(c0, w, k), ACT.Identity, bias=shift(k)))
                inv.guard.mark(done)
                finals = [done] if shift is None else [moved]
            return finals

        HALVES = [(h * HALF, HALF) for h in range(NH)]
        at_x = lambda c, w, k: xT[:, k, c:c + w]
        at_h = lambda c, w, k: hT[:, k, c:c + w]

        def swiglu(name, gain, w_gu, w_down, beside=None):
            settle()
            NF = FF // P
            normed = rms(at_x, at_h, lambda k: col(gain, k), HALVES)
            wide = w_gu.rearrange("(k q) n -> q k n", q=P)
            tall = w_down.rearrange("(k q) n -> q k n", q=P)
            with ExitStack() as own:
                hidden = sb(name + "_hidden", [P, NF, SEQ], own)
                pe.wait(*normed)
                with p.repeat(name + "_up", FF // WCOL) as i:
                    tiles, here = [], []
                    for s in range(2):
                        tile = ring[s].mem[:, :].rearrange("q (k n) -> q k n", k=KC)
                        here.append(ring[s].load(sp, tile, wide[:, :, bass.ds(i * WCOL + s * FF, WCOL)]))
                        tiles.append(tile)
                    groups = [(c, h) for c in range(WCOL // P) for h in range(NH)]

                    def product(s, b, c, h):
                        b.guard.wait(pe)
                        pe.wait(here[s])
                        for k in range(KC):
                            done = T.matmul(b.mem[:, :], tiles[s][:, k, c * P:(c + 1) * P],
                                            hT[:, k, h * HALF:(h + 1) * HALF], start=k == 0, stop=k == KC - 1)
                        done = pe.did(done)
                        ring[s].guard.mark(done)
                        return done

                    gates = [product(0, bank[n], c, h) for n, (c, h) in enumerate(groups)]
                    for n, (c, h) in enumerate(groups):
                        g, u, tmp = bank[n], bank[4 + n % 2], temps[n % 2]
                        have_up = product(1, u, c, h)
                        tmp.guard.wait(act)
                        act.wait(gates[n])
                        gated = act.did(A.activation(tmp.mem[:, :], g.mem[:, :], ACT.Silu))
                        g.guard.mark(gated)
                        dve.wait(gated, have_up)
                        made = dve.did(V.tensor_tensor(hidden[:, bass.ds(2 * i + c, 1), h * HALF:(h + 1) * HALF],
                                                       u.mem[:, None, :], tmp.mem[:, None, :], ALU.mult))
                        u.guard.mark(made)
                        tmp.guard.mark(made)
                    if beside:
                        beside(i)
                pe.wait(made)
                parts = [(k, min(KC, NF - k)) for k in range(0, NF, KC)]
                with p.repeat(name + "_down", D // WCOL) as i:
                    for s, (k0, kn) in enumerate(parts):
                        tile = ring[s].mem[:, 0:kn * WCOL].rearrange("q (k n) -> q k n", k=kn)
                        here = ring[s].load(sp, tile, tall[:, k0:k0 + kn, bass.ds(i * WCOL, WCOL)])
                        pe.wait(here)
                        for c in range(WCOL // P):
                            for h in range(NH):
                                b = bank[c * NH + h]
                                if s == 0:
                                    b.guard.wait(pe)
                                for k in range(kn):
                                    done = T.matmul(b.mem[:, :], tile[:, k, c * P:(c + 1) * P],
                                                    hidden[:, k0 + k, h * HALF:(h + 1) * HALF],
                                                    start=k0 + k == 0, stop=k0 + k == NF - 1)
                                done = pe.did(done)
                                if s == len(parts) - 1:
                                    dve.wait(done)
                                    x_at = xT[:, bass.ds(2 * i + c, 1), h * HALF:(h + 1) * HALF]
                                    b.guard.mark(dve.did(V.scalar_tensor_tensor(
                                        out=x_at, in0=b.mem[:, None, :], scalar=0.5, in1=x_at,
                                        op0=ALU.mult, op1=ALU.add)))
                        ring[s].guard.mark(done)

        def turn_out(dst, name, src):
            rows = dst.rearrange("(n q) d -> q n d", q=P)
            with ExitStack() as own:
                lines = [Buffer(p, f"{name}_line{n}", sb(f"{name}_line{n}", [P, D], own), loads=True) for n in range(2)]
                with p.repeat(name, TT // 2) as i:
                    for n in range(2):
                        line = lines[n]
                        for g in range(2):
                            b = bank[2 * n + g]
                            col0 = temps[g]
                            b.guard.wait(pe)
                            col0.guard.wait(dve)
                            staged = dve.did(V.tensor_copy(
                                col0.mem[:, :].rearrange("q (k c) -> q k c", k=4),
                                src[:, 4 * g:4 * g + 4, bass.ds((2 * i + n) * P, P)]))
                            pe.wait(staged)
                            for k in range(4):
                                done = T.transpose(b.mem[:, k * P:(k + 1) * P], col0.mem[:, k * P:(k + 1) * P], ident[:, :])
                            done = pe.did(done)
                            col0.guard.mark(done)
                            act.wait(done)
                            if g == 0:
                                line.guard.wait(act)
                            moved = act.did(A.activation(line.mem[:, g * HALF:(g + 1) * HALF], b.mem[:, :], ACT.Copy))
                            b.guard.mark(moved)
                        sp.wait(moved)
                        line.guard.mark(line.loads.did(nc.sync.dma_start(rows[:, bass.ds(2 * i + n, 1), :], line.mem[:, None, :])))
                settle()

        e = Shared()
        e.p, e.nc, e.t, e.sb, e.bank = p, nc, t, sb, bank
        e.ring, e.xT, e.hT, e.ident, e.ones = ring, xT, hT, ident, ones
        e.ones64, e.eps, e.squares, e.inv, e.stdev = ones64, eps, squares, inv, stdev
        e.temps, e.column, e.cols, e.col, e.stream = temps, column, cols, col, stream
        e.skew, e.SEQ, e.D, e.KC, e.TT = skew, SEQ, D, KC, TT
        e.HALF, e.NH, e.CTX, e.ALL, e.WCOL = HALF, NH, CTX, ALL, WCOL
        e.HALVES, e.at_x, e.at_h, e.evacuate, e.turn_in = HALVES, at_x, at_h, evacuate, turn_in
        e.turn_out, e.settle, e.rms = turn_out, settle, rms

        swiglu("ffn1", "norm_ffn1", t["w_ffn1_gu"][0], t["w_ffn1_down"][0])
        mix_block(e)
        e.mod, modulate = modulation(e)
        swiglu("ffn2", "norm_ffn2", t["w_ffn2_gu"][0], t["w_ffn2_down"][0], modulate)
        second_block(e, out)
        p.barrier(sp)
        return p.counts, p.carried


def softplus(e, x, out, w, parts, where, name):
    p, nc = e.p, e.nc
    V, dve, act = nc.vector, p.dve, p.act
    y, u, s, acc = (e.sb(f"{name}_{n}", [P, w], where) for n in ("y", "u", "u2", "sum"))
    y, u, s, acc = (b[0:parts, :] for b in (y, u, s, acc))

    def step(ins):
        done = dve.did(ins)
        dve.wait(done)
        return done

    act.wait(step(V.scalar_tensor_tensor(out=y, in0=x, scalar=-1.0, in1=x, op0=ALU.mult, op1=ALU.max)))
    dve.wait(act.did(nc.scalar.activation(y, y, ACT.Exp, scale=-1.0)))
    step(V.tensor_scalar(u, y, 2.0, None, ALU.add))
    step(V.reciprocal(u, u))
    step(V.tensor_tensor(u, u, y, ALU.mult))
    step(V.tensor_tensor(s, u, u, ALU.mult))
    terms = 9
    step(V.tensor_scalar(acc, s, 1.0 / (2 * terms - 1), None, ALU.mult))
    for n in range(terms - 2, 0, -1):
        step(V.scalar_tensor_tensor(out=acc, in0=acc, scalar=1.0 / (2 * n + 1), in1=s, op0=ALU.add, op1=ALU.mult))
    step(V.scalar_tensor_tensor(out=acc, in0=acc, scalar=1.0, in1=u, op0=ALU.add, op1=ALU.mult))
    step(V.tensor_scalar(acc, acc, 2.0, None, ALU.mult))
    return step(V.scalar_tensor_tensor(out=out, in0=x, scalar=0.0, in1=acc, op0=ALU.max, op1=ALU.add))


def mix_block(e):
    p, nc, t = e.p, e.nc, e.t
    V, A, T, G = nc.vector, nc.scalar, nc.tensor, nc.gpsimd
    pe, act, dve, pool, sp = p.pe, p.act, p.dve, p.pool, p.sp
    bank, ring, hT, xT, ident = e.bank, e.ring, e.hT, e.xT, e.ident
    SEQ, KC, HALF, NH, TT, D = e.SEQ, e.KC, e.HALF, e.NH, e.TT, e.D
    GRID, WROWS, WCOLS, HD = 64, 8, 16, t["q_norm"].shape[1]
    NROW = SEQ // GRID
    NDR, NDC = t["rel_pos_bias"].shape[2:]
    HEADS = t["rel_pos_bias"].shape[1]
    CONV, LEFT = t["conv_w"].shape[1], 2
    MASKED = -1e30

    e.settle()
    with ExitStack() as own:
        yT = e.sb("yT", [P, KC, SEQ], own)
        slope = e.sb("slope", [P, 16], own)
        minus = e.sb("minus_slope", [P, 16], own)
        qgain = e.sb("qgain", [P, 1], own)
        part = ExitStack()

        def buf(name, shape, loads=False):
            return Buffer(p, "mix_" + name, e.sb("mix_" + name, shape, part), loads)

        normed = e.rms(e.at_x, e.at_h, lambda k: e.col("norm_mix", k), e.HALVES)

        lanes = HEADS * NDR // 2
        with ExitStack() as first:
            wide = e.sb("bias_rows", [P, 2, P], first)
            wiped = pool.did(G.memset(wide[:, :, :], 0.0))
            sp.wait(wiped)
            rows = t["rel_pos_bias"][0].rearrange("h r c -> (h r) c").rearrange("(a b) c -> b a c", b=lanes)
            start = GRID - 1 - (NDC - 1) // 2
            got = e.stream["bias_in"].did(nc.sync.dma_start(wide[0:lanes, :, start:start + NDC], rows))
            sp.wait(got)
            for a in range(2):
                spread = e.stream["scratch_out"].did(nc.sync.dma_start(
                    e.skew[a * lanes:(a + 1) * lanes, :, :], wide[0:lanes, a, None, :].broadcast_to([lanes, GRID, P])))
            dve.wait(dve.did(V.tensor_scalar(slope[:, :], e.col("lru_lambda", 0, 16), -1.0, None, ALU.mult)))
            softplus(e, slope[:, :], slope[:, :], 16, P, first, "softplus")
            dve.did(V.tensor_scalar(minus[:, :], slope[:, :], -8.0, None, ALU.mult))
            V.tensor_scalar(qgain[:, :], e.col("q_norm"), HD ** -0.5, None, ALU.mult)
            dve.wait(dve.last())
            have_slopes = dve.did(V.tensor_scalar(slope[:, :], slope[:, :], 8.0, None, ALU.mult))
            sp.wait(spread)
            act.wait(have_slopes)
            e.settle()

        q, k, att, xc, r, ig, hs, outer, sgb = (
            buf(n, [P, SEQ]) for n in ("q", "k", "att", "xc", "r", "ig", "hs", "outer", "sgb"))
        v = buf("v", [P, TT, P])
        vodd = buf("vodd", [P, TT - 1, P], True)
        xr = buf("xr", [P, SEQ + CONV - 1])
        bias = buf("bias", [P, NDR, GRID], True)
        wgate = buf("wgate", [P, 4, P], True)
        prob = [buf(f"prob{n}", [P, HALF]) for n in range(2)]
        probT = [buf(f"probT{n}", [P, HALF]) for n in range(2)]
        diag = [buf(f"diag{n}", [P, P]) for n in range(2)]
        stat = [buf(f"stat{n}", [P, 4]) for n in range(2)]

        cleared = [pool.did(G.memset(xr.mem[:, :], 0.0)), pool.did(G.memset(wgate.mem[:, :, :], 0.0))]
        sp.wait(*cleared)
        act.wait(*cleared)
        w_in = t["w_in"][0].rearrange("(k q) (b n) -> q k b n", q=P, b=7)
        XR, GR, QB, KB, VB, GA, GB = range(7)
        skewed = bass.AP(e.skew.tensor, GRID - 1, [[NDR * GRID * P, HEADS], [P - 1, GRID], [GRID * P, NDR], [1, GRID]])
        gates = t["lru_w_gates"][0].rearrange("d g n i o -> n i (d g) o")
        pe.wait(*normed)

        with p.repeat("mix", KC) as i:
            where = {}
            for s, blocks in enumerate(((QB, KB), (VB, XR), (GR, GA), (GB,))):
                tile = ring[s].mem[:, :].rearrange("q (b k n) -> q b k n", b=2, k=KC)
                ring[s].guard.wait(sp)
                for n, b in enumerate(blocks):
                    here = ring[s].more(sp, tile[:, n, :, :], w_in[:, :, b, bass.ds(i * P, P)])
                for n, b in enumerate(blocks):
                    where[b] = (ring[s], tile[:, n, :, :], here)
            bias.guard.wait(sp)
            for h in range(2):
                have_bias = bias.more(sp, bias.mem[h * 64:h * 64 + 64, :, :], skewed[bass.ds(2 * i + h, 1), :, :, :].rearrange("a c r w -> (a c) r w"))
            wgate.guard.wait(sp)
            for h in range(2):
                have_gates = wgate.more(sp, wgate.mem[h * 64:h * 64 + 64, :, h * 64:h * 64 + 64],
                                        gates[bass.ds(2 * i + h, 1), :, :, :].rearrange("a i g o -> (a i) g o"))
            pool.wait(have_bias)
            for h in range(2):
                for lo, sign, base in ((0, 1, WCOLS // 2), (WCOLS, -1, WCOLS // 2 - 1 - WCOLS)):
                    part_ap = bias.mem[h * 64:h * 64 + 64, :, lo:lo + GRID - WCOLS]
                    masked = pool.did(G.affine_select(out=part_ap, in_=part_ap, compare_op=ALU.is_ge, fill=MASKED,
                                                      base=base, pattern=[[0, NDR], [sign, GRID - WCOLS]],
                                                      channel_multiplier=-sign))
                    pool.wait(masked)

            turn = [0]

            def project(block, h):
                slot, tile, here = where[block]
                b = bank[turn[0] % 2]
                turn[0] += 1
                b.guard.wait(pe)
                pe.wait(here)
                for kc in range(KC):
                    done = T.matmul(b.mem[:, :], tile[:, kc, :], hT[:, kc, h * HALF:(h + 1) * HALF],
                                    start=kc == 0, stop=kc == KC - 1)
                done = pe.did(done)
                slot.guard.mark(done)
                return b, done

            def head_cols(block, dst, h):
                at = dst.mem[:, h * HALF:(h + 1) * HALF]
                b, done = project(block, h)
                act.wait(done)
                if h == 0:
                    dst.guard.wait(act)
                copied = act.did(A.activation(at, b.mem[:, :], ACT.Copy))
                sq = e.squares[h]
                sq.guard.wait(act)
                squared = act.did(A.activation(sq.mem[:, :], b.mem[:, :], ACT.Square))
                b.guard.mark(squared)
                return copied, squared

            def norm_head_cols(dst, h, gain, made):
                at = dst.mem[:, h * HALF:(h + 1) * HALF]
                copied, squared = made
                s, sq = bank[6 + h], e.squares[h]
                s.guard.wait(pe)
                pe.wait(squared)
                summed = pe.did(T.matmul(s.mem[:, :], e.ones64[:, :], sq.mem[:, :], start=True, stop=True))
                sq.guard.mark(summed)
                act.wait(summed)
                e.stdev.guard.wait(act)
                rooted = act.did(A.activation(e.stdev.mem[:, :], s.mem[:, :], ACT.Sqrt, bias=e.eps[:, :], scale=1.0 / HD))
                s.guard.mark(rooted)
                dve.wait(rooted)
                e.inv.guard.wait(dve)
                inverted = dve.did(V.reciprocal(e.inv.mem[:, :], e.stdev.mem[:, :]))
                e.stdev.guard.mark(inverted)
                dve.wait(inverted, copied)
                done = dve.did(V.scalar_tensor_tensor(out=at, in0=at, scalar=gain, in1=e.inv.mem[:, :],
                                                      op0=ALU.mult, op1=ALU.mult))
                e.inv.guard.mark(done)
                return done

            q0 = head_cols(QB, q, 0)
            q1 = head_cols(QB, q, 1)
            norm_head_cols(q, 0, qgain[:, :], q0)
            k0 = head_cols(KB, k, 0)
            q_ready = norm_head_cols(q, 1, qgain[:, :], q1)
            k1 = head_cols(KB, k, 1)
            norm_head_cols(k, 0, e.col("k_norm"), k0)

            slot, tile, here = where[VB]
            for g in range(2):
                b = bank[turn[0] % 2]
                turn[0] += 1
                b.guard.wait(pe)
                pe.wait(here)
                for n in range(4):
                    for kc in range(KC):
                        done = T.matmul(b.mem[:, n * P:(n + 1) * P], hT[:, kc, (4 * g + n) * P:(4 * g + n + 1) * P],
                                        tile[:, kc, :], start=kc == 0, stop=kc == KC - 1)
                done = pe.did(done)
                slot.guard.mark(done)
                dve.wait(done)
                if g == 0:
                    v.guard.wait(dve)
                v_ready = dve.did(V.tensor_copy(v.mem[:, 4 * g:4 * g + 4, :],
                                                b.mem[:, :].rearrange("q (n c) -> q n c", n=4)))
                b.guard.mark(v_ready)
                if g == 0:
                    k_ready = norm_head_cols(k, 1, e.col("k_norm"), k1)
            sp.wait(v_ready)
            vodd.guard.wait(sp)
            vodd.more(sp, vodd.mem[0:64, :, :], v.mem[64:P, 0:TT - 1, :])
            vodd_ready = vodd.more(sp, vodd.mem[64:P, :, :], v.mem[0:64, 1:TT, :])

            state = {}

            def through(block, h, func, dst, at0=0):
                def run():
                    b, done = project(block, h)
                    act.wait(done)
                    if h == 0:
                        dst.guard.wait(act)
                    lo = at0 + h * HALF
                    made = act.did(A.activation(dst.mem[:, lo:lo + HALF], b.mem[:, :], func))
                    b.guard.mark(made)
                    state[block] = made
                return run

            def gate_outer(h):
                def run():
                    b, done = project(GA, h)
                    tmp = e.temps[h]
                    act.wait(done)
                    tmp.guard.wait(act)
                    made = act.did(A.activation(tmp.mem[:, :], b.mem[:, :], ACT.Sigmoid))
                    b.guard.mark(made)
                    dve.wait(made, state[GR])
                    at = outer.mem[:, h * HALF:(h + 1) * HALF]
                    state["outer"] = dve.did(V.tensor_tensor(at, at, tmp.mem[:, :], ALU.mult))
                    tmp.guard.mark(state["outer"])
                return run

            def convolve(taps):
                def run():
                    if 0 in taps:
                        dve.wait(state[XR])
                        xc.guard.wait(dve)
                        done = dve.did(V.tensor_scalar(xc.mem[:, :], xr.mem[:, 0:SEQ], wcol(0),
                                                       e.cols[bn][:, bass.ds(i + b0, 1)], ALU.mult, ALU.add))
                    else:
                        done = state["xc"]
                    for tap in taps:
                        if tap:
                            dve.wait(done)
                            done = dve.did(V.scalar_tensor_tensor(out=xc.mem[:, :], in0=xr.mem[:, tap:tap + SEQ],
                                                                  scalar=wcol(tap), in1=xc.mem[:, :],
                                                                  op0=ALU.mult, op1=ALU.add))
                    xr.guard.mark(done)
                    state["xc"] = done
                return run

            bn, b0 = e.column["conv_b"]
            wn, w0 = e.column["conv_w"]
            gn, g0 = e.column["lru_b_gates"]
            wcol = lambda tap: e.cols[wn][:, bass.ds(i + (w0 + tap * KC), 1)]

            def gate(d, g, h):
                dst = (r, ig)[g]

                def run():
                    b = bank[turn[0] % 2]
                    turn[0] += 1
                    b.guard.wait(pe)
                    pe.wait(have_gates, state["xc"])
                    done = pe.did(T.matmul(b.mem[:, :], wgate.mem[:, 2 * d + g, :], xc.mem[:, h * HALF:(h + 1) * HALF],
                                           start=True, stop=True))
                    wgate.guard.mark(done)
                    act.wait(done)
                    if h == 0:
                        dst.guard.wait(act)
                    made = act.did(A.activation(dst.mem[:, h * HALF:(h + 1) * HALF], b.mem[:, :], ACT.Sigmoid,
                                                bias=e.cols[gn][:, bass.ds(i + (g0 + (2 * d + g) * KC), 1)]))
                    b.guard.mark(made)
                    state[("gate", g)] = made
                return run

            def decay(d):
                def run():
                    act.wait(state[("gate", 0)])
                    for h in range(NH):
                        e.temps[h].guard.wait(act)
                        tanhs = act.did(A.activation(e.temps[h].mem[:, :], r.mem[:, h * HALF:(h + 1) * HALF], ACT.Tanh,
                                                     scale=slope[:, bass.ds(i + d * KC, 1)]))
                    act.wait(tanhs)
                    decays = act.did(A.activation(r.mem[:, :], r.mem[:, :], ACT.Exp,
                                                  scale=minus[:, bass.ds(i + d * KC, 1)]))
                    pool.wait(decays)
                    for h in range(NH):
                        sl = slice(h * HALF, (h + 1) * HALF)
                        e.squares[h].guard.wait(pool)
                        squared = pool.did(G.tensor_tensor(e.squares[h].mem[:, :], r.mem[:, sl], r.mem[:, sl], ALU.mult))
                    pool.wait(state[("gate", 1)])
                    gated = pool.did(G.tensor_tensor(ig.mem[:, :], ig.mem[:, :], xc.mem[:, :], ALU.mult))
                    state["decay"] = (tanhs, decays, squared, gated)
                return run

            def weight(d):
                def run():
                    tanhs, decays, squared, gated = state["decay"]
                    dve.wait(tanhs, squared)
                    for h in range(NH):
                        th = e.temps[h].mem
                        done = dve.did(V.scalar_tensor_tensor(out=th[:, :], in0=e.squares[h].mem[:, :], scalar=1.0,
                                                              in1=th[:, :], op0=ALU.add, op1=ALU.mult))
                        e.squares[h].guard.mark(done)
                    act.wait(done)
                    for h in range(NH):
                        state["root"] = act.did(A.activation(e.temps[h].mem[:, :], e.temps[h].mem[:, :], ACT.Sqrt))
                return run

            def drive(d):
                def run():
                    dve.wait(state["root"], state["decay"][3])
                    for h in range(NH):
                        sl = slice(h * HALF, (h + 1) * HALF)
                        done = dve.did(V.tensor_tensor(ig.mem[:, sl], ig.mem[:, sl], e.temps[h].mem[:, :], ALU.mult))
                        e.temps[h].guard.mark(done)
                    state["drive"] = done
                return run

            def scan(d):
                def run():
                    dve.wait(state["drive"], state["decay"][1])
                    if d == 0:
                        hs.guard.wait(dve)
                        done = dve.did(V.tensor_tensor_scan(hs.mem[:, :], r.mem[:, :], ig.mem[:, :], 0.0,
                                                            ALU.mult, ALU.add))
                        state["h"] = done
                    else:
                        done = dve.did(V.tensor_tensor_scan(xc.mem[:, ::-1], r.mem[:, ::-1], ig.mem[:, ::-1], 0.0,
                                                            ALU.mult, ALU.add))
                        pool.wait(done, state["h"], state["outer"])
                        both = pool.did(G.tensor_tensor(hs.mem[:, :], hs.mem[:, :], xc.mem[:, :], ALU.add))
                        xc.guard.mark(both)
                        pool.wait(both)
                        state["lru"] = pool.did(G.tensor_tensor(hs.mem[:, :], hs.mem[:, :], outer.mem[:, :], ALU.mult))
                        outer.guard.mark(state["lru"])
                    r.guard.mark(done)
                    ig.guard.mark(done)
                return run

            xr_half = [through(XR, h, ACT.Copy, xr, LEFT) for h in range(2)]
            gr_half = [through(GR, h, ACT.Gelu_apprx_tanh, outer) for h in range(2)]
            ga_half = [gate_outer(h) for h in range(2)]
            gb_half = [through(GB, h, ACT.Sigmoid, sgb) for h in range(2)]
            pieces = {0: [xr_half[0]], 1: [xr_half[1]], 2: [convolve((0, 1))], 3: [convolve((2, 3))],
                      4: [gate(0, 0, 0), gate(0, 0, 1), gate(0, 1, 0), gate(0, 1, 1)], 5: [gr_half[0], decay(0)],
                      6: [gr_half[1]], 7: [weight(0)], 8: [drive(0)], 9: [scan(0)],
                      10: [gate(1, 0, 0), gate(1, 0, 1), gate(1, 1, 0), gate(1, 1, 1), ga_half[0], ga_half[1]],
                      11: [decay(1)], 12: [], 13: [weight(1)], 14: [drive(1)], 15: [scan(1), gb_half[0]],
                      16: [gb_half[1]]}

            rows = {}

            def scores(row):
                b, pr, st, dg = bank[2 + row % 2], prob[row % 2], stat[row % 2], diag[row % 2]
                first = min(max(row - WROWS // 2, 0), NROW - WROWS)
                b.guard.wait(pe)
                pe.wait(q_ready, k_ready)
                for h in range(2):
                    hp = slice(h * 64, h * 64 + 64)
                    done = T.matmul(b.mem[hp, :], q.mem[hp, row * GRID:(row + 1) * GRID],
                                    k.mem[hp, first * GRID:first * GRID + HALF], start=True, stop=True)
                done = pe.did(done)
                if row == NROW - 1:
                    q.guard.mark(done)
                    k.guard.mark(done)
                dr = first - row + WROWS - 1
                dve.wait(done, masked)
                pr.guard.wait(dve)
                biased = dve.did(V.tensor_tensor_reduce(
                    pr.mem[:, :], b.mem[:, :], bias.mem[:, dr:dr + WROWS, :].rearrange("q r c -> q (r c)"),
                    1.0, MASKED, ALU.add, ALU.max, st.mem[:, 0:1]))
                b.guard.mark(biased)
                if row == NROW - 1:
                    bias.guard.mark(biased)
                dve.wait(biased)
                negated = dve.did(V.tensor_scalar(st.mem[:, 1:2], st.mem[:, 0:1], -1.0, None, ALU.mult))
                act.wait(negated)
                raised = act.did(A.activation(pr.mem[:, :], pr.mem[:, :], ACT.Exp, bias=st.mem[:, 1:2],
                                              accum_out=st.mem[:, 2:3]))
                rows[row] = [first, raised, None, None]

            def weigh(row):
                st, dg = stat[row % 2], diag[row % 2]
                dve.wait(rows[row][1])
                inverted = dve.did(V.reciprocal(st.mem[:, 3:4], st.mem[:, 2:3]))
                dve.wait(inverted)
                dg.guard.wait(dve)
                rows[row][2] = dve.did(V.tensor_scalar(dg.mem[:, :], ident[:, :], st.mem[:, 3:4], None, ALU.mult))

            def turn_probs(row):
                b, pr, pt, dg = bank[4 + row % 2], prob[row % 2], probT[row % 2], diag[row % 2]
                b.guard.wait(pe)
                pe.wait(rows[row][2], rows[row][1])
                for n in range(4):
                    done = T.matmul(b.mem[:, n * P:(n + 1) * P], pr.mem[:, n * P:(n + 1) * P], dg.mem[:, :],
                                    start=True, stop=True)
                done = pe.did(done)
                pr.guard.mark(done)
                dg.guard.mark(done)
                dve.wait(done)
                pt.guard.wait(dve)
                rows[row][3] = dve.did(V.tensor_copy(pt.mem[:, :], b.mem[:, :]))
                b.guard.mark(rows[row][3])

            def values(row):
                b, pt = bank[6 + row % 2], probT[row % 2]
                first = rows[row][0]
                b.guard.wait(pe)
                pe.wait(rows[row][3], v_ready, vodd_ready)
                for n in range(4):
                    vt = vodd.mem[:, first // 2 + n, :] if first % 2 else v.mem[:, first // 2 + n, :]
                    done = T.matmul(b.mem[:, 0:P], vt, pt.mem[:, n * P:(n + 1) * P], start=n == 0, stop=n == 3)
                done = pe.did(done)
                pt.guard.mark(done)
                if row == NROW - 1:
                    v.guard.mark(done, vodd_ready)
                    vodd.guard.mark(done)
                dve.wait(done)
                if row == 0:
                    att.guard.wait(dve)
                for h in range(2):
                    hp = slice(h * 64, h * 64 + 64)
                    kept = dve.did(V.tensor_copy(att.mem[hp, row * GRID:(row + 1) * GRID], b.mem[hp, h * 64:h * 64 + 64]))
                b.guard.mark(kept)
                return kept

            for step in range(NROW + 2):
                if step < NROW:
                    scores(step)
                if 0 <= step - 1 < NROW:
                    weigh(step - 1)
                for piece in pieces.get(step, []):
                    piece()
                if 0 <= step - 1 < NROW:
                    turn_probs(step - 1)
                if 0 <= step - 2 < NROW:
                    kept = values(step - 2)
            dve.wait(kept, state["lru"], state[GB])
            done = dve.did(V.tensor_tensor(att.mem[:, :], att.mem[:, :], sgb.mem[:, :], ALU.mult))
            sgb.guard.mark(done)
            dve.wait(done)
            done = dve.did(V.tensor_tensor(yT[:, bass.ds(i, 1), :], att.mem[:, None, :], hs.mem[:, None, :], ALU.add))
            att.guard.mark(done)
            hs.guard.mark(done)
        part.close()
        add_product(e, "mix_out", t["w_out"][0], lambda k, c: yT[:, k, c], done)


def add_product(e, name, w, rhs, ready, scale=None):
    p, nc = e.p, e.nc
    V, T = nc.vector, nc.tensor
    wide = w.rearrange("(k q) n -> q k n", q=P)
    KC, HALF = e.KC, e.HALF
    C = e.WCOL // P
    p.pe.wait(ready)
    with p.repeat(name, e.D // e.WCOL // 2) as i:
        for s in range(2):
            slot = e.ring[s]
            tile = slot.mem[:, :].rearrange("q (k n) -> q k n", k=KC)
            here = slot.load(p.sp, tile, wide[:, :, bass.ds((2 * i + s) * e.WCOL, e.WCOL)])
            p.pe.wait(here)
            for c in range(C):
                for h in range(e.NH):
                    b = e.bank[(s * C + c) * e.NH + h]
                    b.guard.wait(p.pe)
                    for k in range(KC):
                        done = T.matmul(b.mem[:, :], tile[:, k, c * P:(c + 1) * P], rhs(k, slice(h * HALF, (h + 1) * HALF)),
                                        start=k == 0, stop=k == KC - 1)
                    done = p.pe.did(done)
                    p.dve.wait(done)
                    x_at = e.xT[:, bass.ds((2 * i + s) * C + c, 1), h * HALF:(h + 1) * HALF]
                    by = 1.0 if scale is None else scale(i, s * C + c)
                    b.guard.mark(p.dve.did(V.scalar_tensor_tensor(out=x_at, in0=b.mem[:, None, :], scalar=by, in1=x_at,
                                                                 op0=ALU.mult, op1=ALU.add)))
            slot.guard.mark(done)


def modulation(e):
    p, nc, t = e.p, e.nc, e.t
    KC, WCOL = e.KC, e.WCOL
    N_MOD = t["w_mod_2"].shape[2] // P
    C = WCOL // P
    mod = e.sb("mod", [P, N_MOD, 2])
    cond = e.sb("cond", [P, KC, 2])
    e.settle()
    for n, name in enumerate(("c_2", "c_ctx_2")):
        have_cond = p.act.did(nc.scalar.activation(cond[:, :, n], e.col(name, 0, KC), ACT.Silu))
    p.pe.wait(have_cond)
    wide = t["w_mod_2"][0].rearrange("(k q) n -> q k n", q=P)

    def modulate(i):
        for s in range(2):
            slot, b = e.ring[2 + s], e.bank[6 + s]
            tile = slot.mem[:, :].rearrange("q (k n) -> q k n", k=KC)
            here = slot.load(p.sp, tile, wide[:, :, bass.ds((2 * i + s) * WCOL, WCOL)])
            b.guard.wait(p.pe)
            p.pe.wait(here)
            for c in range(C):
                for k in range(KC):
                    done = nc.tensor.matmul(b.mem[:, 2 * c:2 * c + 2], tile[:, k, c * P:(c + 1) * P], cond[:, k, :],
                                            start=k == 0, stop=k == KC - 1)
            done = p.pe.did(done)
            slot.guard.mark(done)
            p.dve.wait(done)
            b.guard.mark(p.dve.did(nc.vector.tensor_copy(mod[:, bass.ds((2 * i + s) * C, C), :],
                                                         b.mem[:, 0:2 * C].rearrange("q (c v) -> q c v", c=C))))

    e.cond, e.modulate = cond, modulate
    return mod, modulate


def second_block(e, out):
    p, nc, t = e.p, e.nc, e.t
    V, A, T, G = nc.vector, nc.scalar, nc.tensor, nc.gpsimd
    pe, act, dve, pool, sp = p.pe, p.act, p.dve, p.pool, p.sp
    bank, ring, hT, xT, ident, ones = e.bank, e.ring, e.hT, e.xT, e.ident, e.ones
    SEQ, KC, HALF, NH, TT, D, CTX, ALL = e.SEQ, e.KC, e.HALF, e.NH, e.TT, e.D, e.CTX, e.ALL
    WCOL = e.WCOL
    H2, HD2 = 4, 128
    WIDE = H2 * HD2
    NT, NCT = ALL // P, CTX // P
    DIRS = 2
    e.settle()

    def step(counter, ins):
        done = counter.did(ins)
        counter.wait(done)
        return done

    q_rows = nc.dram_tensor("q_cols", [NT, P, H2, P], F32, kind="Internal").ap()
    k_cols = nc.dram_tensor("k_cols", [NT, P, H2, P], F32, kind="Internal").ap()
    k_rows = nc.dram_tensor("k_rows", [NT, P, H2, P], F32, kind="Internal").ap()
    v_rows = nc.dram_tensor("v_rows", [NT, P, H2, P], F32, kind="Internal").ap()
    f_rows = nc.dram_tensor("f_rows", [SEQ, D], F32, kind="Internal").ap()
    sum_rows = nc.dram_tensor("sum_rows", [SEQ, D], F32, kind="Internal").ap()
    gate_row = nc.dram_tensor("gate_row", [D], F32, kind="Internal").ap()

    with ExitStack() as own:
        N_MOD = t["w_mod_2"].shape[2] // P
        mod = e.mod
        gains = e.sb("gains", [P, 3, KC], own)
        dec_in = e.sb("dec_in", [P, NT, 8], own)
        beta = e.sb("beta", [P, NT, 8], own)
        for n in range(2 * (t["w_ffn2_down"].shape[1] // WCOL), N_MOD * P // WCOL, 2):
            e.modulate(n // 2)
        dve.wait(dve.last())
        for v in range(2):
            step(dve, V.tensor_tensor(mod[:, :, v], mod[:, :, v], e.col("b_mod_2", 0, N_MOD), ALU.add))
        SH1, SC1, GT1, SH2, SC2, GT2 = (n * KC for n in range(6))
        for n, (name, at, v) in enumerate((("norm1_g_2", SC1, 0), ("norm1_g_2", SC1, 1), ("norm2_g_2", SC2, 0))):
            have_gains = step(dve, V.scalar_tensor_tensor(out=gains[:, n, :], in0=mod[:, at:at + KC, v], scalar=1.0,
                                                          in1=e.col(name, 0, KC), op0=ALU.add, op1=ALU.mult))
        act.wait(have_gains)

        late = ExitStack()
        zs = e.sb("zs", [P, H2, SEQ], late)
        ya = e.sb("ya", [P, H2, SEQ], late)
        with ExitStack() as mid:
            cT = e.sb("cT", [P, KC, CTX], mid)
            e.turn_in(t["ctx_2"][0], lambda n, k: cT[:, k:k + 4, bass.ds(n * P, P)], NCT, "turn_ctx", 2)
            e.settle()
            at_c = lambda c, w, k: cT[:, k, c:c + w]
            e.rms(at_c, at_c, lambda k: gains[:, 1, k:k + 1], [(0, CTX)], shift=lambda k: mod[:, SH1 + k, 1:2])
            normed = e.rms(e.at_x, e.at_h, lambda k: gains[:, 0, k:k + 1], e.HALVES,
                           shift=lambda k: mod[:, SH1 + k, 0:1])
            e.settle()
            w_in = t["w_in_2"][0]
            by_k = w_in.rearrange("(k q) n -> q k n", q=P)
            COL_AB = 3 * WIDE
            COL_Z = COL_AB + 16
            COL_U = COL_Z + WIDE
            COL_V = COL_U + WIDE

            with ExitStack() as gate_mem:
                wab = Buffer(p, "wab", e.sb("wab", [P, KC, 16], gate_mem), True)
                wide_vec = Buffer(p, "wide_vec", e.sb("wide_vec", [P, 2, 8], gate_mem), True)
                here = wab.load(sp, wab.mem[:, :, :], by_k[:, :, COL_AB:COL_AB + 16])
                for n, name in enumerate(("a_log_2", "dt_bias_2")):
                    vec = wide_vec.more(sp, wide_vec.mem[:, n, :],
                                        t[name][0].rearrange("a b -> (a b)").partition_broadcast(P))
                pe.wait(here)
                for n in range(NT):
                    for k in range(KC):
                        lhs = cT[:, k, n * P:(n + 1) * P] if n < NCT else hT[:, k, (n - NCT) * P:(n - NCT + 1) * P]
                        done = T.matmul(bank[0].mem[:, 16 * n:16 * n + 16], lhs, wab.mem[:, k, :],
                                        start=k == 0, stop=k == KC - 1)
                done = pe.did(done)
                ab = bank[0].mem[:, 0:16 * NT].rearrange("q (n c) -> q n c", n=NT)
                act.wait(done, vec)
                act.did(A.activation(beta[:, :, :], ab[:, :, 8:16], ACT.Sigmoid))
                act.did(A.activation(wide_vec.mem[:, 0, :], wide_vec.mem[:, 0, :], ACT.Exp))
                dve.wait(done, vec, act.last())
                shape = [P, NT, 8]
                step(dve, V.tensor_tensor(dec_in[:, :, :], ab[:, :, 0:8],
                                          wide_vec.mem[:, 1, None, :].broadcast_to(shape), ALU.add))
                flat = dec_in[:, :, :].rearrange("q n c -> q (n c)")
                softplus(e, flat, flat, NT * 8, P, gate_mem, "softplus2")
                done = step(dve, V.scalar_tensor_tensor(out=dec_in[:, :, :], in0=dec_in[:, :, :], scalar=-1.0,
                                                        in1=wide_vec.mem[:, 0, None, :].broadcast_to(shape),
                                                        op0=ALU.mult, op1=ALU.mult))
                bank[0].guard.mark(done)
                e.settle()

            GAP = 2
            LEN = ALL + GAP
            BLOCKS = [(0, 512), (512, 512), (1024, LEN - 1024)]
            with ExitStack() as conv_mem:
                pre = [Buffer(p, f"pre{n}", e.sb(f"pre{n}", [P, LEN + 2], conv_mem)) for n in range(2)]
                post = [Buffer(p, f"post{n}", e.sb(f"post{n}", [P, LEN], conv_mem)) for n in range(3)]
                turned = [Buffer(p, f"turned{n}", e.sb(f"turned{n}", [P, NT, P], conv_mem), True) for n in range(2)]
                norms = [Buffer(p, f"norms{n}", e.sb(f"norms{n}", [P, LEN], conv_mem)) for n in range(2)]
                colsto = [Buffer(p, f"colsto{n}", None, True) for n in range(2)]
                for b in pre:
                    clear = pool.did(G.memset(b.mem[:, :], 0.0))
                dve.wait(clear)
                act.wait(clear)
                split = w_in[:, 0:3 * WIDE].rearrange("(k q) (b n) -> q k b n", q=P, b=3)
                wn, w0 = e.column["conv_w_2"]
                places = lambda m: [(m[:, 0:CTX], 0), (m[:, CTX + GAP:LEN], 1)]
                with p.repeat("qkv", H2) as i:
                    ready, users = {}, {0: [], 1: [], 2: []}

                    def project(j):
                        tile = ring[j].mem[:, 0:KC * P].rearrange("q (k n) -> q k n", k=KC)
                        here = ring[j].load(sp, tile, split[:, :, j, bass.ds(i * P, P)])
                        pe.wait(here)
                        pr = pre[j % 2]
                        pr.guard.wait(act)
                        pr.guard.wait(dve)
                        moves = []
                        for n in range(NH + 1):
                            b = bank[(j * 3 + n) % 4]
                            b.guard.wait(pe)
                            w = HALF if n < NH else CTX
                            for k in range(KC):
                                rhs = hT[:, k, n * HALF:(n + 1) * HALF] if n < NH else cT[:, k, :]
                                done = T.matmul(b.mem[:, 0:w], tile[:, k, :], rhs, start=k == 0, stop=k == KC - 1)
                            done = pe.did(done)
                            at = 1 + CTX + GAP + n * HALF if n < NH else 1
                            act.wait(done)
                            moves.append(act.did(A.activation(pr.mem[:, at:at + w], b.mem[:, 0:w], ACT.Copy)))
                            b.guard.mark(moves[-1])
                        ring[j].guard.mark(done)
                        return moves

                    def convolve(j, moves):
                        pr, po = pre[j % 2], post[j]
                        wcol = lambda tap: e.cols[wn][:, bass.ds(i + (w0 + tap * 3 * H2 + j * H2), 1)]
                        dve.wait(*moves)
                        po.guard.wait(dve)
                        done = step(dve, V.tensor_scalar(po.mem[:, :], pr.mem[:, 0:LEN], wcol(0), None, ALU.mult))
                        for tap in range(1, 3):
                            done = step(dve, V.scalar_tensor_tensor(out=po.mem[:, :], in0=pr.mem[:, tap:tap + LEN],
                                                                    scalar=wcol(tap), in1=po.mem[:, :],
                                                                    op0=ALU.mult, op1=ALU.add))
                        pr.guard.mark(done)
                        act.wait(done)
                        ready[j] = act.did(A.activation(po.mem[:, :], po.mem[:, :], ACT.Silu))

                    def measure(j):
                        for n, (c0, w) in enumerate(BLOCKS):
                            s, sq = bank[4 + n % 2], e.squares[n % 2]
                            act.wait(ready[j])
                            sq.guard.wait(act)
                            squared = act.did(A.activation(sq.mem[:, 0:w], post[j].mem[:, c0:c0 + w], ACT.Square))
                            s.guard.wait(pe)
                            pe.wait(squared)
                            summed = pe.did(T.matmul(s.mem[:, 0:w], ones[:, :], sq.mem[:, 0:w], start=True, stop=True))
                            sq.guard.mark(summed)
                            act.wait(summed)
                            if n == 0:
                                norms[j].guard.wait(act)
                            rooted = act.did(A.activation(norms[j].mem[:, c0:c0 + w], s.mem[:, 0:w], ACT.Sqrt,
                                                          bias=e.eps[:, :]))
                            s.guard.mark(rooted)
                        return rooted

                    def normalise(j, rooted):
                        po = post[j]
                        dve.wait(rooted, ready[j])
                        step(dve, V.reciprocal(norms[j].mem[:, :], norms[j].mem[:, :]))
                        normal = dve.did(V.scalar_tensor_tensor(out=po.mem[:, :], in0=po.mem[:, :],
                                                                scalar=HD2 ** -0.5 if j == 0 else 1.0,
                                                                in1=norms[j].mem[:, :], op0=ALU.mult, op1=ALU.mult))
                        norms[j].guard.mark(normal)
                        ready[j] = normal
                        sp.wait(normal)
                        to = (q_rows, k_cols)[j].rearrange("n q h c -> q n h c")[:, :, bass.ds(i, 1), :]
                        for part_ap, n in places(po.mem):
                            lo, hi = (0, NCT) if n == 0 else (NCT, NT)
                            stored = colsto[j].more(sp, to[:, lo:hi, 0, :], part_ap.rearrange("q (n c) -> q n c", c=P))
                        users[j].append(stored)

                    def by_rows(j):
                        po, tr = post[j], turned[j - 1]
                        for g in range(0, NT, 4):
                            b = bank[6 + (g // 4) % 2]
                            m = min(4, NT - g)
                            b.guard.wait(pe)
                            pe.wait(ready[j])
                            for n in range(m):
                                at = (g + n) * P + (GAP if g + n >= NCT else 0)
                                done = T.transpose(b.mem[:, n * P:(n + 1) * P], po.mem[:, at:at + P], ident[:, :])
                            done = pe.did(done)
                            dve.wait(done)
                            if g == 0:
                                tr.guard.wait(dve)
                            flipped = dve.did(V.tensor_copy(tr.mem[:, g:g + m, :],
                                                            b.mem[:, 0:m * P].rearrange("q (n c) -> q n c", c=P)))
                            b.guard.mark(flipped)
                        users[j].append(done)
                        sp.wait(flipped)
                        to = (k_rows, v_rows)[j - 1].rearrange("n q h c -> q n h c")[:, :, bass.ds(i, 1), :]
                        tr.guard.mark(tr.more(sp, to[:, :, 0, :], tr.mem[:, :, :]))

                    convolve(0, project(0))
                    convolve(1, project(1))
                    normalise(0, measure(0))
                    moves = project(2)
                    normalise(1, measure(1))
                    convolve(2, moves)
                    by_rows(2)
                    by_rows(1)
                    for j in range(3):
                        post[j].guard.mark(*users[j])
                e.settle()

            with p.repeat("z_u", H2) as i:
                for j, (c0, dst, func) in enumerate(((COL_Z, zs, ACT.Silu), (COL_U, ya, ACT.Gelu))):
                    tile = ring[j].mem[:, 0:KC * P].rearrange("q (k n) -> q k n", k=KC)
                    here = ring[j].load(sp, tile, by_k[:, :, bass.ds(i * P + c0, P)])
                    pe.wait(here)
                    for h in range(NH):
                        b = bank[j * NH + h]
                        b.guard.wait(pe)
                        for k in range(KC):
                            done = T.matmul(b.mem[:, :], tile[:, k, :], hT[:, k, h * HALF:(h + 1) * HALF],
                                            start=k == 0, stop=k == KC - 1)
                        done = pe.did(done)
                        act.wait(done)
                        b.guard.mark(act.did(A.activation(dst[:, bass.ds(i, 1), h * HALF:(h + 1) * HALF],
                                                          b.mem[:, None, :], func)))
                    ring[j].guard.mark(done)

            with ExitStack() as mlp_mem:
                e.settle()
                ws = Buffer(p, "ws", e.sb("ws", [P, H2, P], mlp_mem), True)
                wsT = e.sb("wsT", [P, H2, P], mlp_mem)
                row = Buffer(p, "mlp_row", e.sb("mlp_row", [1, WIDE], mlp_mem), True)
                vgain = e.sb("vgain", [P, WIDE], mlp_mem)
                tokens = [Buffer(p, f"tokens{n}", e.sb(f"tokens{n}", [P, KC, P], mlp_mem)) for n in range(2)]
                vt = [Buffer(p, f"vt{n}", e.sb(f"vt{n}", [P, WIDE], mlp_mem)) for n in range(2)]
                vstat = e.sb("vstat", [P, 2, 2, H2], mlp_mem)
                here = ws.more(sp, ws.mem[:, :, :], t["gm_ws_2"][0].rearrange("g t s -> t g s"))
                row.more(sp, row.mem[:, :], t["gm_bs_2"][0].rearrange("g (a t) -> a g t", a=1))
                have_row = row.more(sp, vgain[:, :], t["gm_norm_g_2"][0].partition_broadcast(P))
                pe.wait(here)
                for g in range(H2):
                    done = T.transpose(bank[0].mem[:, g * P:(g + 1) * P], ws.mem[:, g, :], ident[:, :])
                dve.wait(pe.did(done))
                have_wsT = dve.did(V.tensor_copy(wsT[:, :, :], bank[0].mem[:, :].rearrange("q (g c) -> q g c", g=H2)))
                bank[0].guard.mark(have_wsT)
                wv = []
                for s in range(2):
                    wv.append(ring[s].mem[:, :].rearrange("q (k n) -> q k n", k=KC))
                    here = ring[s].load(sp, wv[s], by_k[:, :, COL_V + s * WCOL:COL_V + (s + 1) * WCOL])
                    pe.wait(here)
                pe.wait(have_wsT, have_row)
                dve.wait(have_row)
                with p.repeat("mlp", TT // 2) as i:
                    for n in range(2):
                        tk, v, b, mixed = tokens[n], vt[n], bank[2 + n], bank[4 + n]
                        at = bass.ds((2 * i + n) * P, P)
                        tk.guard.wait(dve)
                        copied = dve.did(V.tensor_copy(tk.mem[:, :, :], hT[:, :, at]))
                        pe.wait(copied)
                        b.guard.wait(pe)
                        for s in range(2):
                            for k in range(KC):
                                done = T.matmul(b.mem[:, s * WCOL:(s + 1) * WCOL], tk.mem[:, k, :], wv[s][:, k, :],
                                                start=k == 0, stop=k == KC - 1)
                        done = pe.did(done)
                        tk.guard.mark(done)
                        act.wait(done)
                        v.guard.wait(act)
                        made = act.did(A.activation(v.mem[:, :], b.mem[:, :], ACT.Gelu))
                        b.guard.mark(made)
                        act.wait(made)
                        sq = e.squares[n]
                        sq.guard.wait(act)
                        for g in range(H2):
                            sl = slice(g * P, (g + 1) * P)
                            done = act.did(A.activation(sq.mem[:, sl], v.mem[:, sl], ACT.Square,
                                                        accum_out=vstat[:, n, 0, g:g + 1]))
                        sq.guard.mark(done)
                        act.wait(done)
                        rooted = act.did(A.activation(vstat[:, n, 0, :], vstat[:, n, 0, :], ACT.Sqrt, bias=e.eps[:, :],
                                                      scale=1.0 / P))
                        dve.wait(rooted)
                        step(dve, V.reciprocal(vstat[:, n, 1, :], vstat[:, n, 0, :]))
                        for g in range(H2):
                            sl = slice(g * P, (g + 1) * P)
                            done = dve.did(V.scalar_tensor_tensor(out=v.mem[:, sl], in0=v.mem[:, sl],
                                                                  scalar=vstat[:, n, 1, g:g + 1], in1=vgain[:, sl],
                                                                  op0=ALU.mult, op1=ALU.mult))
                        act.wait(done)
                        pe.wait(done)
                        mixed.guard.wait(pe)
                        for g in range(H2):
                            sl = slice(g * P, (g + 1) * P)
                            T.matmul(mixed.mem[:, sl], ones[0:1, :], row.mem[0:1, sl], start=True, stop=False)
                            done = T.matmul(mixed.mem[:, sl], v.mem[:, sl], wsT[:, g, :], start=False, stop=True)
                        done = pe.did(done)
                        v.guard.mark(done)
                        dve.wait(done)
                        done = dve.did(V.tensor_tensor(ya[:, :, at], ya[:, :, at],
                                                       mixed.mem[:, :].rearrange("q (g c) -> q g c", g=H2), ALU.mult))
                        mixed.guard.mark(done)
                ring[0].guard.mark(pe.last())
                ring[1].guard.mark(pe.last())
                e.settle()

        own_acc = hT[:, 0:4, :].rearrange("q k (a c) -> q (k a) c", a=2)
        o_sum = own_acc.rearrange("q (n) (h c) -> q n h c", h=H2)
        spare = hT[:, 4:8, :].rearrange("q k (a c) -> q (k a) c", a=2)
        delta_rule(e, late, step, dec_in, beta, (q_rows, k_cols, k_rows, v_rows), o_sum, spare, NT, NCT, H2)

        with ExitStack() as gdn_out:
            flat = [Buffer(p, f"flat{n}", e.sb(f"flat{n}", [P, H2, P], gdn_out)) for n in range(2)]
            ostat = e.sb("ostat", [P, 2, 2, H2], gdn_out)
            with p.repeat("gdn_out", TT // 2) as i:
                for n in range(2):
                    fl, b, sq = flat[n], bank[n], e.squares[n]
                    tile = o_sum[:, bass.ds(2 * i + n, 1), :, :].rearrange("q a h c -> q (a h) c")
                    sq.guard.wait(act)
                    for h in range(H2):
                        done = act.did(A.activation(sq.mem[:, h * P:(h + 1) * P], tile[:, h, :], ACT.Square,
                                                    accum_out=ostat[:, n, 0, h:h + 1]))
                    sq.guard.mark(done)
                    act.wait(done)
                    rooted = act.did(A.activation(ostat[:, n, 0, :], ostat[:, n, 0, :], ACT.Sqrt, bias=e.eps[:, :],
                                                  scale=1.0 / P))
                    dve.wait(rooted)
                    inverted = step(dve, V.reciprocal(ostat[:, n, 1, :], ostat[:, n, 0, :]))
                    fl.guard.wait(dve)
                    done = dve.did(V.tensor_tensor(fl.mem[:, :, :], tile, ostat[:, n, 1, :, None].broadcast_to([P, H2, P]),
                                                   ALU.mult))
                    act.wait(done)
                    pe.wait(done)
                    b.guard.wait(pe)
                    for h in range(H2):
                        done = T.transpose(b.mem[:, h * P:(h + 1) * P], fl.mem[:, h, :], ident[:, :])
                    done = pe.did(done)
                    fl.guard.mark(done)
                    dve.wait(done)
                    at = zs[:, :, bass.ds((2 * i + n) * P, P)]
                    done = dve.did(V.scalar_tensor_tensor(out=at, in0=b.mem[:, :].rearrange("q (h c) -> q h c", h=H2),
                                                          scalar=e.col("gdn_norm_g_2"), in1=at,
                                                          op0=ALU.mult, op1=ALU.mult))
                    b.guard.mark(done)
            e.settle()

        def y_cols(k, c):
            return ya[:, k, c] if k < H2 else zs[:, k - H2, c]

        add_product(e, "mix2_out", t["w_out_2"][0], y_cols, done, lambda i, c: mod[:, bass.ds(4 * i + (GT1 + c), 1), 0])
        e.settle()
        late.close()
        experts(e, own, step, out, mod, gains, (SH2, GT2), f_rows, sum_rows, gate_row)


def delta_rule(e, outer_mem, step, dec_in, beta, stores, o_sum, spare, NT, NCT, H2):
    p, nc, t = e.p, e.nc, e.t
    V, A, T, G = nc.vector, nc.scalar, nc.tensor, nc.gpsimd
    pe, act, dve, pool, sp = p.pe, p.act, p.dve, p.pool, p.sp
    bank, ring, ident, ones = e.bank, e.ring, e.ident, e.ones
    W = H2 * P
    LEVELS = [1, 2, 4, 8, 16, 32, 64]
    with ExitStack() as own:
        upto = e.sb("upto", [P, 2, P], own)
        after = e.sb("after", [P, 2, P], own)
        pair = e.sb("pair", [P, 2, len(LEVELS), P], own)

        def select(ap, base, pattern, cm):
            return step(pool, G.affine_select(out=ap, in_=ap, compare_op=ALU.is_ge, fill=0.0, base=base,
                                              pattern=pattern, channel_multiplier=cm))

        G.memset(upto[:, :, :], 1.0)
        G.memset(after[:, :, :], 1.0)
        step(pool, G.memset(pair[:, :, :, :], 0.0))
        select(upto[:, 0, :], 0, [[1, P]], -1)
        select(upto[:, 1, :], 0, [[-1, P]], 1)
        select(after[:, 0, :], -1, [[-1, P]], 1)
        select(after[:, 1, :], -1, [[1, P]], -1)
        for n, b in enumerate(LEVELS):
            blocks = P // (2 * b)
            for side in range(2):
                ap = pair[:, side, n, :].rearrange("q (m s c) -> q m s c", s=2, c=b)[:, :, side, :]
                step(pool, G.memset(ap, 1.0))
                first = b if side == 0 else 0
                select(ap, -first, [[-2 * b, blocks], [0, b]], 1)
                select(ap, first + b - 1, [[2 * b, blocks], [0, b]], -1)
        masks_ready = pool.last()

        spares = iter(range(spare.shape[1]))

        def tile(name, d):
            if d == 0:
                n = next(spares, None)
                if n is not None:
                    return Buffer(p, f"{name}_{d}", spare[:, n, :].rearrange("q (h c) -> q h c", h=H2))
            return Buffer(p, f"{name}_{d}", e.sb(f"{name}_{d}", [P, H2, P], own)[:, :, :])

        names = ("gmask", "decT", "A", "AT", "ATb", "X", "XT", "Y", "bv", "kg", "r", "attT", "S")
        work = [{n: tile(n, d) for n in names} for d in range(2)]
        small = [e.sb(f"small{d}", [P, 6, H2], own) for d in range(2)]
        b4 = lambda m: m.rearrange("q (h c) -> q h c", h=H2)
        SH = [P, H2, P]
        for w in work:
            cleared = dve.did(V.memset(w["S"].mem, 0.0))
        cleared = dve.did(V.memset(o_sum, 0.0))
        dve.wait(cleared, masks_ready)
        pe.wait(cleared, masks_ready)
        pool.wait(cleared)
        act.wait(cleared)

        def load(d, u, tile_at):
            slot = ring[2 * u + d]
            parts = slot.mem[:, :].rearrange("q (a h c) -> q a h c", a=4, h=H2)
            slot.guard.wait(sp)
            for n, s in enumerate(stores):
                here = slot.more(sp, parts[:, n, :, :], s[bass.ds(tile_at, 1), :, :, :].rearrange("a q h c -> (a q) h c"))
            return slot, [parts[:, n, :, :] for n in range(4)], here

        GS, BE, EGC, EGL, ETOT, BEGC = range(6)

        def chunk(d, slot, parts, here, tile_at, out_at):
            w, sm = work[d], small[d]
            B = [bank[4 * d + n] for n in range(4)]
            qT, kT, kr, vr = parts
            sml = lambda n: sm[:, n, :]
            wide = lambda n: sm[:, n, :, None].broadcast_to(SH)
            up = upto[:, d, :]
            aft = after[:, d, :]
            below = lambda n: pair[:, d, n, None, :].broadcast_to(SH)
            above = lambda n: pair[:, 1 - d, n, None, :].broadcast_to(SH)
            small_guard[d].wait(dve)
            dve.did(V.tensor_copy(sml(GS), dec_in[:, bass.ds(tile_at, 1), 4 * d:4 * d + 4].rearrange("q a h -> q (a h)")))
            got = step(dve, V.tensor_copy(sml(BE), beta[:, bass.ds(tile_at, 1), 4 * d:4 * d + 4].rearrange("q a h -> q (a h)")))
            w["gmask"].guard.wait(dve)
            masked = dve.did(V.tensor_tensor(w["gmask"].mem, aft[:, None, :].broadcast_to(SH), wide(GS), ALU.mult))
            pe.wait(got)
            B[0].guard.wait(pe)
            T.matmul(B[0].mem[:, 0:H2], up, sml(GS), start=True, stop=True)
            T.matmul(B[0].mem[:, H2:2 * H2], aft, sml(GS), start=True, stop=True)
            done = pe.did(T.matmul(B[0].mem[:, 2 * H2:3 * H2], ones[:, :], sml(GS), start=True, stop=True))
            act.wait(done)
            small_guard[d].wait(act)
            sums = act.did(A.activation(sm[:, EGC:EGC + 3, :], B[0].mem[:, 0:3 * H2].rearrange("q (a h) -> q a h", a=3), ACT.Exp))
            B[0].guard.mark(sums)
            dve.wait(sums)
            begc = step(dve, V.tensor_tensor(sml(BEGC), sml(BE), sml(EGC), ALU.mult))
            yield
            pe.wait(masked)
            B[1].guard.wait(pe)
            for h in range(H2):
                done = T.matmul(B[1].mem[:, h * P:(h + 1) * P], w["gmask"].mem[:, h, :], up, start=True, stop=True)
            done = pe.did(done)
            act.wait(done)
            w["decT"].guard.wait(act)
            decT = act.did(A.activation(w["decT"].mem, b4(B[1].mem[:, :]), ACT.Exp))
            B[1].guard.mark(decT)
            B[2].guard.wait(pe)
            for h in range(H2):
                done = T.matmul(B[2].mem[:, h * P:(h + 1) * P], up, w["gmask"].mem[:, h, :], start=True, stop=True)
            done = pe.did(done)
            w["gmask"].guard.mark(done)
            act.wait(done)
            w["A"].guard.wait(act)
            dec = act.did(A.activation(w["A"].mem, b4(B[2].mem[:, :]), ACT.Exp))
            B[2].guard.mark(dec)
            pool.wait(decT)
            decT = pool.did(G.tensor_tensor(w["decT"].mem, w["decT"].mem, up[:, None, :].broadcast_to(SH), ALU.mult))
            yield
            pe.wait(here)
            B[3].guard.wait(pe)
            for h in range(H2):
                done = T.matmul(B[3].mem[:, h * P:(h + 1) * P], kT[:, h, :], kT[:, h, :], start=True, stop=True)
            kk = pe.did(done)
            B[0].guard.wait(pe)
            for h in range(H2):
                done = T.matmul(B[0].mem[:, h * P:(h + 1) * P], kT[:, h, :], qT[:, h, :], start=True, stop=True)
            kq = pe.did(done)
            dve.wait(kk, dec)
            done = dve.did(V.tensor_tensor(w["A"].mem, b4(B[3].mem[:, :]), w["A"].mem, ALU.mult))
            B[3].guard.mark(done)
            dve.wait(done)
            a_ready = dve.did(V.tensor_tensor(w["A"].mem, w["A"].mem, wide(BE), ALU.mult))
            yield
            pe.wait(a_ready)
            B[1].guard.wait(pe)
            for h in range(H2):
                done = T.transpose(B[1].mem[:, h * P:(h + 1) * P], w["A"].mem[:, h, :], ident[:, :])
            done = pe.did(done)
            act.wait(done)
            w["AT"].guard.wait(act)
            at_ready = act.did(A.activation(w["AT"].mem, b4(B[1].mem[:, :]), ACT.Copy))
            B[1].guard.mark(at_ready)
            dve.wait(kq, decT)
            w["attT"].guard.wait(dve)
            att = dve.did(V.tensor_tensor(w["attT"].mem, b4(B[0].mem[:, :]), w["decT"].mem, ALU.mult))
            B[0].guard.mark(att)
            w["decT"].guard.mark(att)
            pool.wait(here, sums, got)
            w["bv"].guard.wait(pool)
            bv = pool.did(G.tensor_tensor(w["bv"].mem, vr, wide(BE), ALU.mult))
            w["kg"].guard.wait(pool)
            kg = pool.did(G.tensor_tensor(w["kg"].mem, kr, wide(EGL), ALU.mult))
            yield
            w["X"].guard.wait(dve)
            w["XT"].guard.wait(dve)
            eye = ident[:, None, :].broadcast_to(SH)
            step(dve, V.tensor_tensor(w["X"].mem, w["A"].mem, below(0), ALU.mult))
            x = dve.did(V.tensor_tensor(w["X"].mem, eye, w["X"].mem, ALU.subtract))
            dve.wait(at_ready)
            w["A"].guard.mark(x, at_ready)
            step(dve, V.tensor_tensor(w["XT"].mem, w["AT"].mem, above(0), ALU.mult))
            xt = dve.did(V.tensor_tensor(w["XT"].mem, eye, w["XT"].mem, ALU.subtract))
            for n in range(1, len(LEVELS)):
                last = n == len(LEVELS) - 1
                pool.wait(at_ready)
                w["ATb"].guard.wait(pool)
                atb = pool.did(G.tensor_tensor(w["ATb"].mem, w["AT"].mem, above(n), ALU.mult))
                pe.wait(atb, x)
                B[1].guard.wait(pe)
                for h in range(H2):
                    done = T.matmul(B[1].mem[:, h * P:(h + 1) * P], w["ATb"].mem[:, h, :], w["X"].mem[:, h, :],
                                    start=True, stop=True)
                done = pe.did(done)
                w["ATb"].guard.mark(done)
                act.wait(done)
                w["Y"].guard.wait(act)
                y = act.did(A.activation(w["Y"].mem, b4(B[1].mem[:, :]), ACT.Copy))
                B[1].guard.mark(y)
                yield
                pe.wait(y, xt)
                B[3].guard.wait(pe)
                for h in range(H2):
                    done = T.matmul(B[3].mem[:, h * P:(h + 1) * P], w["Y"].mem[:, h, :], w["XT"].mem[:, h, :],
                                    start=True, stop=True)
                zt = pe.did(done)
                if not last:
                    B[2].guard.wait(pe)
                    for h in range(H2):
                        done = T.matmul(B[2].mem[:, h * P:(h + 1) * P], w["XT"].mem[:, h, :], w["Y"].mem[:, h, :],
                                        start=True, stop=True)
                    z = pe.did(done)
                    dve.wait(z)
                    x = dve.did(V.tensor_tensor(w["X"].mem, w["X"].mem, b4(B[2].mem[:, :]), ALU.subtract))
                    B[2].guard.mark(x)
                else:
                    z = zt
                    w["X"].guard.mark(zt)
                w["Y"].guard.mark(z)
                dve.wait(zt, z)
                xt = dve.did(V.tensor_tensor(w["XT"].mem, w["XT"].mem, b4(B[3].mem[:, :]), ALU.subtract))
                B[3].guard.mark(xt)
                yield
            w["AT"].guard.mark(atb)
            pe.wait(here)
            w["S"].guard.wait(pe)
            B[2].guard.wait(pe)
            for h in range(H2):
                done = T.matmul(B[2].mem[:, h * P:(h + 1) * P], kT[:, h, :], w["S"].mem[:, h, :], start=True, stop=True)
            ks = pe.did(done)
            dve.wait(ks, begc, bv)
            w["r"].guard.wait(dve)
            done = step(dve, V.tensor_tensor(w["r"].mem, b4(B[2].mem[:, :]), wide(BEGC), ALU.mult))
            B[2].guard.mark(done)
            r = dve.did(V.tensor_tensor(w["r"].mem, w["bv"].mem, w["r"].mem, ALU.subtract))
            w["bv"].guard.mark(r)
            if out_at is not None:
                B[0].guard.wait(pe)
                for h in range(H2):
                    done = T.matmul(B[0].mem[:, h * P:(h + 1) * P], qT[:, h, :], w["S"].mem[:, h, :], start=True, stop=True)
                qs = pe.did(done)
            yield
            pe.wait(r, xt)
            B[1].guard.wait(pe)
            for h in range(H2):
                done = T.matmul(B[1].mem[:, h * P:(h + 1) * P], w["XT"].mem[:, h, :], w["r"].mem[:, h, :], start=True, stop=True)
            done = pe.did(done)
            w["XT"].guard.mark(done)
            act.wait(done)
            w["Y"].guard.wait(act)
            vn = act.did(A.activation(w["Y"].mem, b4(B[1].mem[:, :]), ACT.Copy))
            B[1].guard.mark(vn)
            yield
            pe.wait(vn, kg)
            B[3].guard.wait(pe)
            for h in range(H2):
                done = T.matmul(B[3].mem[:, h * P:(h + 1) * P], w["kg"].mem[:, h, :], w["Y"].mem[:, h, :], start=True, stop=True)
            ds = pe.did(done)
            w["kg"].guard.mark(ds)
            dve.wait(ds)
            step(dve, V.tensor_tensor(w["S"].mem, w["S"].mem, wide(ETOT), ALU.mult))
            s_new = dve.did(V.tensor_tensor(w["S"].mem, w["S"].mem, b4(B[3].mem[:, :]), ALU.add))
            w["S"].guard.mark(s_new)
            B[3].guard.mark(s_new)
            if out_at is None:
                slot.guard.mark(ds, kg)
                w["Y"].guard.mark(ds)
                w["r"].guard.mark(ds)
                w["attT"].guard.mark(ds)
                small_guard[d].mark(s_new, kg)
                return
            pe.wait(att)
            B[2].guard.wait(pe)
            for h in range(H2):
                done = T.matmul(B[2].mem[:, h * P:(h + 1) * P], w["attT"].mem[:, h, :], w["Y"].mem[:, h, :], start=True, stop=True)
            av = pe.did(done)
            w["Y"].guard.mark(av)
            w["attT"].guard.mark(av)
            slot.guard.mark(av, kg)
            dve.wait(qs)
            done = step(dve, V.tensor_tensor(w["r"].mem, b4(B[0].mem[:, :]), wide(EGC), ALU.mult))
            B[0].guard.mark(done)
            small_guard[d].mark(done, kg)
            dve.wait(av)
            done = dve.did(V.tensor_tensor(w["r"].mem, w["r"].mem, b4(B[2].mem[:, :]), ALU.add))
            B[2].guard.mark(done)
            dve.wait(done)
            o_guard.wait(dve)
            at = o_sum[:, bass.ds(out_at, 1), :, :].rearrange("q a h c -> q (a h) c")
            done = step(dve, V.tensor_tensor(at, at, w["r"].mem, ALU.add))
            o_guard.mark(done)
            w["r"].guard.mark(done)

        small_guard = [Guard(p, f"small{d}") for d in range(2)]
        o_guard = Guard(p, "o_sum")
        o_guard.mark(cleared)

        def both(u, forward, backward, outs):
            loads = [load(d, u, at) for d, at in enumerate((forward, backward))]
            runs = [chunk(d, *loads[d], at, outs[d]) for d, at in enumerate((forward, backward))]
            while runs:
                for g in list(runs):
                    if next(g, "over") == "over":
                        runs.remove(g)

        for s in range(NCT):
            both(s % 2, s, NCT - 1 - s, (None, None))
        with p.repeat("delta", (NT - NCT) // 2) as i:
            for u in range(2):
                both(u, 2 * i + (NCT + u), i * -2 + (NT - 1 - u), (2 * i + u, i * -2 + (NT - NCT - 1 - u)))
        e.settle()


def experts(e, own, step, out, mod, gains, rows_of_mod, f_rows, sum_rows, gate_row):
    p, nc, t = e.p, e.nc, e.t
    V, A, T, G = nc.vector, nc.scalar, nc.tensor, nc.gpsimd
    pe, act, dve, pool, sp = p.pe, p.act, p.dve, p.pool, p.sp
    bank, ring, hT, xT, ident, ones = e.bank, e.ring, e.hT, e.xT, e.ident, e.ones
    SEQ, KC, HALF, TT, D = e.SEQ, e.KC, e.HALF, e.TT, e.D
    SH2, GT2 = rows_of_mod
    NE = t["w_router_2"].shape[2]
    CAP = 2 * SEQ // NE
    FX = t["w_gate_2"].shape[3]
    assert CAP == P and FX == D

    e.rms(e.at_x, e.at_h, lambda k: gains[:, 2, k:k + 1], e.HALVES, shift=lambda k: mod[:, SH2 + k, 0:1])
    e.settle()

    picks = e.sb("picks", [P, 2, NE + 1], own)
    gate2 = e.sb("gate2", [P, D], own)
    more = [Buffer(p, f"more{n}", e.sb(f"more{n}", [P, 2 * D], own), loads=True) for n in range(8)]
    p.barrier(sp)
    with ExitStack() as route:
        gcols = e.sb("gcols", [KC, P], route)
        lines = Buffer(p, "gate_lines", None, True)
        pe.wait(dve.last())
        done = pe.did(T.transpose(bank[7].mem[0:KC, 0:P], mod[:, GT2:GT2 + KC, 0], ident[:, :]))
        dve.wait(done)
        flat = dve.did(V.tensor_copy(gcols[:, :], bank[7].mem[0:KC, 0:P]))
        bank[7].guard.mark(flat)
        act.wait(flat)
        stored = lines.more(act, gate_row.rearrange("(k q) -> k q", q=P), gcols[:, :])
        act.wait(stored)
        have_gate2 = lines.more(act, gate2[:, :], gate_row.partition_broadcast(P))
        wr = Buffer(p, "wr", e.sb("wr", [P, KC, NE], route), True)
        br = e.sb("br", [P, NE], route)
        aff = e.sb("aff", [P, TT, NE], route)
        peak = e.sb("peak", [P, 2, TT], route)
        wr.more(act, wr.mem[:, :, :], t["w_router_2"][0].rearrange("(k q) n -> q k n", q=P))
        here = wr.more(act, br[:, :], t["b_router_2"][0].partition_broadcast(P))
        pe.wait(here)
        bank[6].guard.wait(pe)
        for n in range(TT):
            for k in range(KC):
                done = T.matmul(bank[6].mem[:, NE * n:NE * n + NE], hT[:, k, n * P:(n + 1) * P], wr.mem[:, k, :],
                                start=k == 0, stop=k == KC - 1)
        done = pe.did(done)
        dve.wait(done, here)
        S3 = [P, TT, NE]
        done = step(dve, V.tensor_tensor(aff[:, :, :], bank[6].mem[:, 0:NE * TT].rearrange("q (n c) -> q n c", n=TT),
                                         br[:, None, :].broadcast_to(S3), ALU.add))
        bank[6].guard.mark(done)
        step(dve, V.tensor_reduce(peak[:, 0, :], aff[:, :, :], AX.X, ALU.max))
        done = step(dve, V.tensor_tensor(aff[:, :, :], aff[:, :, :], peak[:, 0, :, None].broadcast_to(S3), ALU.subtract))
        act.wait(done)
        raised = act.did(A.activation(aff[:, :, :], aff[:, :, :], ACT.Exp))
        dve.wait(raised)
        step(dve, V.tensor_reduce(peak[:, 1, :], aff[:, :, :], AX.X, ALU.add))
        step(dve, V.reciprocal(peak[:, 1, :], peak[:, 1, :]))
        done = step(dve, V.tensor_tensor(aff[:, :, :], aff[:, :, :], peak[:, 1, :, None].broadcast_to(S3), ALU.mult))
        affT = e.sb("affT", [NE, SEQ], route)
        top = e.sb("top", [NE, 8], route)
        top_at = e.sb("top_at", [NE, 8], route, mybir.dt.uint32)
        chosen = e.sb("chosen", [NE, 2, CAP], route)
        pe.wait(done)
        for h in range(2):
            b = bank[h]
            b.guard.wait(pe)
            for n in range(4):
                done = T.transpose(b.mem[0:NE, n * P:(n + 1) * P], aff[:, 4 * h + n, :], ident[:, :])
            done = pe.did(done)
            dve.wait(done)
            b.guard.mark(step(dve, V.tensor_copy(affT[:, h * HALF:(h + 1) * HALF], b.mem[0:NE, :])))
        assert CAP // 8 == 2 * TT
        rows_out = [Buffer(p, f"rows_out{n}", e.sb(f"rows_out{n}", [P, D], route), True) for n in range(2)]
        for part, (name, src, dst) in enumerate((("f", hT, f_rows), ("x", xT, sum_rows))):
            dst = dst.rearrange("(n q) d -> q n d", q=P)
            with p.repeat("choose_" + name, TT // 2) as i:
                for u in range(2):
                    line, turned = rows_out[u], []
                    for g in range(2):
                        staging = e.temps[g]
                        staging.guard.wait(act)
                        staged = act.did(A.activation(
                            staging.mem[:, :].rearrange("q (k c) -> q k c", k=4),
                            src[:, 4 * g:4 * g + 4, bass.ds((2 * i + u) * P, P)], ACT.Copy))
                        bank[2 * u + g].guard.wait(pe)
                        pe.wait(staged)
                        for k in range(4):
                            done = T.transpose(bank[2 * u + g].mem[:, k * P:(k + 1) * P],
                                               staging.mem[:, k * P:(k + 1) * P], ident[:, :])
                        turned.append(pe.did(done))
                        staging.guard.mark(turned[g])
                    line.guard.wait(act)
                    for g in range(2):
                        act.wait(turned[g])
                        moved = act.did(A.activation(line.mem[:, g * HALF:(g + 1) * HALF], bank[2 * u + g].mem[:, :],
                                                     ACT.Copy))
                        bank[2 * u + g].guard.mark(moved)
                    sp.wait(moved)
                    line.guard.mark(line.loads.did(nc.sync.dma_start(dst[:, bass.ds(2 * i + u, 1), :],
                                                                     line.mem[:, None, :])))
                    step(dve, V.max(top[:, :], affT[:, :]))
                    step(dve, V.max_index(top_at[:, :], top[:, :], affT[:, :]))
                    at = (2 * i + (part * TT + u)) * 8
                    V.tensor_copy(chosen[:, 0, bass.ds(at, 8)], top[:, :])
                    V.tensor_copy(chosen[:, 1, bass.ds(at, 8)], top_at[:, :])
                    done = step(dve, V.match_replace(affT[:, :], top[:, :], affT[:, :], -1.0))
        dve.wait(done)
        pe.wait(done)
        bank[7].guard.wait(pe)
        T.transpose(bank[7].mem[:, 0:NE], chosen[:, 0, :], ident[0:NE, 0:NE])
        done = pe.did(T.transpose(bank[7].mem[:, NE:2 * NE], chosen[:, 1, :], ident[0:NE, 0:NE]))
        dve.wait(done)
        step(dve, V.memset(picks[:, :, :], 0.0))
        picked = dve.did(V.tensor_copy(picks[:, :, 0:NE], bank[7].mem[:, 0:2 * NE].rearrange("q (a n) -> q a n", a=2)))
        bank[7].guard.mark(picked)
        dve.wait(picked)
        e.settle()

    with ExitStack() as mem:
        slots = ring + more
        index = [e.sb(f"index{n}", [P, 1], mem, mybir.dt.int32) for n in range(2)]
        xe = Buffer(p, "xe", e.sb("xe", [P, D], mem), True, head=0)
        xeT = Buffer(p, "xeT", e.sb("xeT", [P, KC, P], mem))
        hid = Buffer(p, "hid", e.sb("hid", [P, FX], mem))
        hidT = Buffer(p, "hidT", e.sb("hidT", [P, KC, P], mem))
        ye = Buffer(p, "ye", e.sb("ye", [P, D], mem), True, head=0)
        ahead = Guard(p, "index_ahead")
        NU = KC // 2
        index_ap = lambda ap: bass.IndirectOffsetOnAxis(ap=ap, axis=0)

        def gather(which):
            pool.wait(which)
            xe.guard.wait(pool)
            return xe.loads.did(G.indirect_dma_start(out=xe.mem[:, :], out_offset=None, in_=f_rows,
                                                     in_offset=index_ap(index[1][:, :])))

        def turn8(src, dst, ready):
            for g in range(2):
                b = bank[6 + g]
                b.guard.wait(pe)
                pe.wait(*ready)
                for k in range(4):
                    done = T.transpose(b.mem[:, k * P:(k + 1) * P], src.mem[:, (4 * g + k) * P:(4 * g + k + 1) * P],
                                       ident[:, :])
                done = pe.did(done)
                act.wait(done)
                if g == 0:
                    dst.guard.wait(act)
                copied = act.did(A.activation(dst.mem[:, 4 * g:4 * g + 4, :],
                                              b.mem[:, :].rearrange("q (k c) -> q k c", k=4), ACT.Copy))
                b.guard.mark(copied)
            src.guard.mark(done)
            return copied

        first = dve.did(V.tensor_copy(index[1][:, :], picks[:, 1, 0:1]))
        gathered = gather(first)
        xeT_ready = turn8(xe, xeT, [gathered])
        xeT_made = Guard(p, "xeT_made")
        xeT_made.mark(xeT_ready)
        ahead.mark(gathered)
        dve.wait(have_gate2)
        pool.wait(have_gate2)
        ye.guard.mark(ye.loads.did(G.dma_start(ye.mem[0:1, :], gate_row.rearrange("(a n) -> a n", a=1))))
        weights = [t[n][0].rearrange("x (u a q) n -> u q x a n", q=P, a=2) for n in ("w_gate_2", "w_up_2", "w_down_2")]
        with p.repeat("experts", NE) as i:
            landed = []
            for m in range(3):
                for u in range(NU):
                    slot = slots[m * NU + u]
                    tile = slot.mem[:, :].rearrange("q (a n) -> q a n", a=2)
                    here = slot.load(sp, tile, weights[m][u][:, bass.ds(i, 1), :, :].rearrange("q x a n -> q (x a) n"))
                    landed.append((slot, tile, here))
            ye.guard.wait(dve)
            now = dve.did(V.tensor_copy(index[0][:, :], picks[:, 1, bass.ds(i, 1)]))
            ahead.wait(dve)
            following = dve.did(V.tensor_copy(index[1][:, :], picks[:, 1, bass.ds(i + 1, 1)]))
            gathered = gather(following)
            ahead.mark(gathered)

            def product(m, lhs, banks):
                for b in banks:
                    b.guard.wait(pe)
                for u in range(NU):
                    slot, tile, here = landed[m * NU + u]
                    pe.wait(here)
                    for a in range(2):
                        k = 2 * u + a
                        for h, b in enumerate(banks):
                            done = T.matmul(b.mem[:, :], lhs.mem[:, k, :], tile[:, a, h * HALF:(h + 1) * HALF],
                                            start=k == 0, stop=k == KC - 1)
                    done = pe.did(done)
                    slot.guard.mark(done)
                return done

            xeT_made.wait(pe)
            gate_done = product(0, xeT, bank[0:2])
            hid.guard.wait(act)
            act.wait(gate_done)
            for h in range(2):
                gated = act.did(A.activation(hid.mem[:, h * HALF:(h + 1) * HALF], bank[h].mem[:, :], ACT.Silu))
                bank[h].guard.mark(gated)
            up_done = product(1, xeT, bank[2:4])
            xeT.guard.mark(up_done)
            dve.wait(gated, up_done)
            for h in range(2):
                sl = slice(h * HALF, (h + 1) * HALF)
                made = dve.did(V.tensor_tensor(hid.mem[:, sl], hid.mem[:, sl], bank[2 + h].mem[:, :], ALU.mult))
                bank[2 + h].guard.mark(made)
            xeT_ready = turn8(xe, xeT, [gathered])
            xeT_made.mark(xeT_ready)
            hidT_ready = turn8(hid, hidT, [made])
            pe.wait(hidT_ready)
            down_done = product(2, hidT, bank[4:6])
            hidT.guard.mark(down_done)
            dve.wait(down_done)
            for h in range(2):
                sl = slice(h * HALF, (h + 1) * HALF)
                scaled = dve.did(V.scalar_tensor_tensor(out=ye.mem[:, sl], in0=bank[4 + h].mem[:, :],
                                                        scalar=picks[:, 0, bass.ds(i, 1)], in1=gate2[:, sl],
                                                        op0=ALU.mult, op1=ALU.mult))
                bank[4 + h].guard.mark(scaled)
            pool.wait(scaled, now)
            ye.guard.wait(pool)
            ye.guard.mark(ye.loads.did(G.indirect_dma_start(out=sum_rows, out_offset=index_ap(index[0][:, :]),
                                                            in_=ye.mem[:, :], in_offset=None, compute_op=ALU.add)))
        e.settle()
    with ExitStack() as mem:
        fgain = Buffer(p, "fgain", e.sb("fgain", [P, D], mem), True)
        lines = [Buffer(p, f"sum{n}", e.sb(f"sum{n}", [P, D], mem), True) for n in range(2)]
        squared = [Buffer(p, f"sqr{n}", e.sb(f"sqr{n}", [P, D], mem)) for n in range(2)]
        done_rows = [Buffer(p, f"fin{n}", e.sb(f"fin{n}", [P, D], mem), True) for n in range(2)]
        fstat = e.cond[:, 0:2, :]
        p.barrier(sp)
        have_gain = fgain.more(sp, fgain.mem[:, :], t["final_norm_g_2"].partition_broadcast(P))
        dve.wait(have_gain)
        src = sum_rows.rearrange("(n q) d -> q n d", q=P)
        dst = out[0].rearrange("(n q) d -> q n d", q=P)
        with p.repeat("last_norm", TT // 2) as i:
            for n in range(2):
                line, sq, fin = lines[n], squared[n], done_rows[n]
                here = line.load(sp, line.mem[:, None, :], src[:, bass.ds(2 * i + n, 1), :])
                act.wait(here)
                sq.guard.wait(act)
                summed = act.did(A.activation(sq.mem[:, :], line.mem[:, :], ACT.Square, accum_out=fstat[:, n, 0:1]))
                act.wait(summed)
                rooted = act.did(A.activation(fstat[:, n, 0:1], fstat[:, n, 0:1], ACT.Sqrt, bias=e.eps[:, :], scale=1.0 / D))
                dve.wait(rooted)
                step(dve, V.reciprocal(fstat[:, n, 1:2], fstat[:, n, 0:1]))
                fin.guard.wait(dve)
                normed = dve.did(V.scalar_tensor_tensor(out=fin.mem[:, :], in0=line.mem[:, :], scalar=fstat[:, n, 1:2],
                                                        in1=fgain.mem[:, :], op0=ALU.mult, op1=ALU.mult))
                line.guard.mark(normed)
                sq.guard.mark(normed)
                act.wait(normed)
                fin.guard.mark(fin.more(act, dst[:, bass.ds(2 * i + n, 1), :], fin.mem[:, None, :]))


NAMES = ["x", "norm_ffn1", "w_ffn1_gu", "w_ffn1_down", "norm_mix", "w_in", "conv_w", "conv_b", "lru_w_gates",
         "lru_b_gates", "lru_lambda", "q_norm", "k_norm", "rel_pos_bias", "w_out", "norm_ffn2", "w_ffn2_gu",
         "w_ffn2_down", "c_2", "ctx_2", "c_ctx_2", "w_mod_2", "b_mod_2", "norm1_g_2", "norm2_g_2", "w_in_2",
         "conv_w_2", "a_log_2", "dt_bias_2", "gdn_norm_g_2", "gm_norm_g_2", "gm_ws_2", "gm_bs_2", "w_out_2",
         "w_router_2", "b_router_2", "w_gate_2", "w_up_2", "w_down_2", "final_norm_g_2"]


def kernel(**inputs):
    import concourse.bacc as bacc
    from concourse.bass_utils import run_bass_kernel_spmd

    arrays = {n: np.ascontiguousarray(inputs[n]) for n in NAMES}

    def program(plan):
        nc = bacc.Bacc("TRN2", target_bir_lowering=False, num_devices=1)
        t = {n: nc.dram_tensor("in_" + n, a.shape, F32, kind="ExternalInput").ap() for n, a in arrays.items()}
        out = nc.dram_tensor("out_0", t["x"].shape, F32, kind="ExternalOutput").ap()
        return nc, build(nc, plan, t, out)

    _, plan = program(({}, {}))
    nc, _ = program(plan)
    r = run_bass_kernel_spmd(nc, [{"in_" + n: a for n, a in arrays.items()}], core_ids=[0])
    return r.results[0]["out_0"]
```
